# Optimizing a Trainium2 kernel written in Bass

```python
import math
import jax
import jax.numpy as jnp
from jax import lax
import numpy as np

D_MODEL = 1024
BATCH = 1
SEQ = 512
DEPTH = 1

NORM_EPS = 1e-6
D_FF = 2816
MACARON_WEIGHT = 0.5

DN_HEADS = 4
DN_HEAD_DIM = 128
DN_WIDTH = DN_HEADS * DN_HEAD_DIM
DN_CONV = 4
DN_CHUNK = 64

MB_HEADS = 8
MB_HEAD_DIM = 64
MB_WIDTH = MB_HEADS * MB_HEAD_DIM
MB_BLOCK = 256
MB_TOPK = 3
MB_QBLOCK = 64
ALIBI_MAX_BIAS = 8.0

PROJ_WIDTH = 4 * DN_WIDTH + 2 * DN_HEADS + 3 * MB_WIDTH + 2 * D_MODEL

kernel_name = "hybrid_deltanet_moba_macaron"

def rms_norm(x, w):
    xf = x.astype(jnp.float32)
    y = xf * lax.rsqrt(jnp.mean(xf * xf, axis=-1, keepdims=True) + NORM_EPS)
    return (y * w.astype(jnp.float32)).astype(x.dtype)

def l2_normalize(x):
    return x * lax.rsqrt(jnp.sum(x * x, axis=-1, keepdims=True) + NORM_EPS)

def swiglu(h, w_gate, w_up, w_down):
    return (jax.nn.silu(h @ w_gate) * (h @ w_up)) @ w_down

def causal_depthwise_conv(x, w):
    k_len, t_len = w.shape[0], x.shape[1]
    xp = jnp.pad(x, ((0, 0), (k_len - 1, 0), (0, 0)))
    y = xp[:, 0:t_len] * w[0]
    for i in range(1, k_len):
        y = y + xp[:, i:i + t_len] * w[i]
    return y

def split_projection(p):
    sizes = (3 * DN_WIDTH, DN_WIDTH, DN_HEADS, DN_HEADS, MB_WIDTH, MB_WIDTH, MB_WIDTH, D_MODEL, D_MODEL)
    parts, start = [], 0
    for s in sizes:
        parts.append(p[..., start:start + s])
        start += s
    return parts

def chunk_gated_delta_rule(q, k, v, g, beta):
    bsz, nh, t_len, dk = q.shape
    dv = v.shape[-1]
    c = DN_CHUNK
    n = t_len // c
    q = q.reshape(bsz, nh, n, c, dk)
    k = k.reshape(bsz, nh, n, c, dk)
    v = v.reshape(bsz, nh, n, c, dv)
    g = jnp.cumsum(g.reshape(bsz, nh, n, c), axis=-1)
    beta = beta.reshape(bsz, nh, n, c)
    incl = jnp.tril(jnp.ones((c, c), dtype=bool))
    strict = jnp.tril(jnp.ones((c, c), dtype=bool), -1)
    decay = jnp.exp(jnp.where(incl, g[..., :, None] - g[..., None, :], -jnp.inf))
    k_beta = k * beta[..., None]
    v_beta = v * beta[..., None]
    eye = jnp.eye(c, dtype=q.dtype)
    a_mat = jnp.where(strict, jnp.einsum('bhnid,bhnjd->bhnij', k_beta, k) * decay, 0.0) + eye
    t_mat = lax.linalg.triangular_solve(a_mat, jnp.broadcast_to(eye, a_mat.shape),
                                        left_side=True, lower=True, unit_diagonal=True)
    u = t_mat @ v_beta
    w = t_mat @ (k_beta * jnp.exp(g)[..., None])
    attn = jnp.where(incl, jnp.einsum('bhnid,bhnjd->bhnij', q, k) * decay, 0.0)
    q_dec = q * jnp.exp(g)[..., None]
    k_dec = k * jnp.exp(g[..., -1:] - g)[..., None]
    chunk_decay = jnp.exp(g[..., -1])

    def step(state, inp):
        q_i, k_i, u_i, w_i, a_i, d_i = inp
        v_new = u_i - w_i @ state
        o_i = q_i @ state + a_i @ v_new
        state = state * d_i[..., None, None] + jnp.einsum('bhcd,bhce->bhde', k_i, v_new)
        return state, o_i

    xs = (jnp.moveaxis(q_dec, 2, 0), jnp.moveaxis(k_dec, 2, 0), jnp.moveaxis(u, 2, 0),
          jnp.moveaxis(w, 2, 0), jnp.moveaxis(attn, 2, 0), jnp.moveaxis(chunk_decay, 2, 0))
    state0 = jnp.zeros((bsz, nh, dk, dv), q.dtype)
    _, o = lax.scan(step, state0, xs)
    return jnp.moveaxis(o, 0, 2).reshape(bsz, nh, t_len, dv)

def gated_deltanet(qkv, z, b, a, conv_w, a_log, dt_bias, norm_w):
    bsz, t_len, _ = qkv.shape
    qkv = jax.nn.silu(causal_depthwise_conv(qkv, conv_w)).astype(jnp.float32)
    q, k, v = jnp.split(qkv, 3, axis=-1)

    def heads(t):
        return t.reshape(bsz, t_len, DN_HEADS, DN_HEAD_DIM).transpose(0, 2, 1, 3)

    q = l2_normalize(heads(q)) * (DN_HEAD_DIM ** -0.5)
    k = l2_normalize(heads(k))
    v = heads(v)
    beta = jax.nn.sigmoid(b.astype(jnp.float32)).transpose(0, 2, 1)
    g = (-jnp.exp(a_log.astype(jnp.float32))
         * jax.nn.softplus(a.astype(jnp.float32) + dt_bias.astype(jnp.float32))).transpose(0, 2, 1)
    o = chunk_gated_delta_rule(q, k, v, g, beta).transpose(0, 2, 1, 3)
    zg = jax.nn.silu(z.astype(jnp.float32).reshape(bsz, t_len, DN_HEADS, DN_HEAD_DIM))
    o = rms_norm(o, norm_w) * zg
    return o.reshape(bsz, t_len, DN_WIDTH).astype(z.dtype)

def moba_attention(q, k, v):
    bsz, t_len, _ = q.shape
    n_blk = -(-t_len // MB_BLOCK)
    t_pad = n_blk * MB_BLOCK
    topk = min(MB_TOPK, n_blk)

    def heads(t):
        t = jnp.pad(t, ((0, 0), (0, t_pad - t_len), (0, 0)))
        return t.reshape(bsz, t_pad, MB_HEADS, MB_HEAD_DIM).transpose(0, 2, 1, 3)

    q, k, v = heads(q), heads(k), heads(v)
    kb = k.reshape(bsz, MB_HEADS, n_blk, MB_BLOCK, MB_HEAD_DIM)
    vb = v.reshape(bsz, MB_HEADS, n_blk, MB_BLOCK, MB_HEAD_DIM)
    kmean = jnp.mean(kb.astype(jnp.float32), axis=3)
    slopes = jnp.exp2(-ALIBI_MAX_BIAS * jnp.arange(1, MB_HEADS + 1, dtype=jnp.float32) / MB_HEADS)
    scale = MB_HEAD_DIM ** -0.5
    bi = jnp.arange(bsz)[:, None, None, None]
    hi = jnp.arange(MB_HEADS)[None, :, None, None]
    blk_off = jnp.arange(MB_BLOCK)

    def one_qblock(ci):
        start = ci * MB_QBLOCK
        own = start // MB_BLOCK
        q_c = lax.dynamic_slice_in_dim(q, start, MB_QBLOCK, axis=2)
        q_pos = start + jnp.arange(MB_QBLOCK)
        gate = jnp.einsum('bhqd,bhnd->bhqn', q_c.astype(jnp.float32), kmean)
        gate = jnp.where(jnp.arange(n_blk) < own, gate, -jnp.inf)
        _, idx = lax.top_k(gate, topk)
        sel_ok = idx < own
        k_sel = kb[bi, hi, idx]
        v_sel = vb[bi, hi, idx]
        k_pos_sel = idx[..., None] * MB_BLOCK + blk_off
        s_sel = (jnp.einsum('bhqd,bhqnkd->bhqnk', q_c, k_sel).astype(jnp.float32) * scale
                 - slopes[:, None, None, None] * (q_pos[:, None, None] - k_pos_sel))
        s_sel = jnp.where(sel_ok[..., None], s_sel, -jnp.inf)
        k_own = lax.dynamic_slice_in_dim(kb, own, 1, axis=2)[:, :, 0]
        v_own = lax.dynamic_slice_in_dim(vb, own, 1, axis=2)[:, :, 0]
        dist = q_pos[:, None] - (own * MB_BLOCK + blk_off)[None, :]
        s_own = (jnp.einsum('bhqd,bhkd->bhqk', q_c, k_own).astype(jnp.float32) * scale
                 - slopes[:, None, None] * dist)
        s_own = jnp.where(dist >= 0, s_own, -jnp.inf)
        logits = jnp.concatenate(
            [s_sel.reshape(bsz, MB_HEADS, MB_QBLOCK, topk * MB_BLOCK), s_own], axis=-1)
        p = jax.nn.softmax(logits, axis=-1).astype(v.dtype)
        p_sel = p[..., :topk * MB_BLOCK].reshape(bsz, MB_HEADS, MB_QBLOCK, topk, MB_BLOCK)
        p_own = p[..., topk * MB_BLOCK:]
        return (jnp.einsum('bhqnk,bhqnkd->bhqd', p_sel, v_sel)
                + jnp.einsum('bhqk,bhkd->bhqd', p_own, v_own))

    out = lax.map(one_qblock, jnp.arange(t_pad // MB_QBLOCK))
    out = out.transpose(1, 2, 0, 3, 4).reshape(bsz, MB_HEADS, t_pad, MB_HEAD_DIM)[:, :, :t_len]
    return out.transpose(0, 2, 1, 3).reshape(bsz, t_len, MB_WIDTH)

def setup_inputs(seed: int = 0) -> dict:
    key = jax.random.key(seed)
    ks = jax.random.split(key, 24)
    f32 = jnp.float32

    def dense(k, fan_in, fan_out):
        return jax.random.normal(k, (DEPTH, fan_in, fan_out), f32) * fan_in ** -0.5

    def gain(k, n):
        return 1.0 + 0.02 * jax.random.normal(k, (DEPTH, n), f32)

    x = jax.random.normal(ks[0], (BATCH, SEQ, D_MODEL), f32)
    dt = jnp.exp(jax.random.uniform(ks[9], (DEPTH, DN_HEADS), f32, math.log(1e-3), math.log(1e-1)))
    dn_dt_bias = dt + jnp.log(-jnp.expm1(-dt))
    dn_a_log = jnp.log(jax.random.uniform(ks[10], (DEPTH, DN_HEADS), f32, 1.0, 16.0))
    return {
        'x': x,
        'ffn1_pre_w': gain(ks[1], D_MODEL),
        'ffn1_w_gate': dense(ks[2], D_MODEL, D_FF),
        'ffn1_w_up': dense(ks[3], D_MODEL, D_FF),
        'ffn1_w_down': dense(ks[4], D_FF, D_MODEL),
        'ffn1_post_w': gain(ks[5], D_MODEL),
        'mix_pre_w': gain(ks[6], D_MODEL),
        'w_in': dense(ks[7], D_MODEL, PROJ_WIDTH),
        'dn_conv_w': jax.random.normal(ks[8], (DEPTH, DN_CONV, 3 * DN_WIDTH), f32) * DN_CONV ** -0.5,
        'dn_a_log': dn_a_log,
        'dn_dt_bias': dn_dt_bias,
        'dn_norm_w': gain(ks[11], DN_HEAD_DIM),
        'w_branch_dn': dense(ks[12], DN_WIDTH, D_MODEL),
        'w_branch_mb': dense(ks[13], MB_WIDTH, D_MODEL),
        'w_out': dense(ks[14], D_MODEL, D_MODEL),
        'mix_post_w': gain(ks[15], D_MODEL),
        'ffn2_pre_w': gain(ks[16], D_MODEL),
        'ffn2_w_gate': dense(ks[17], D_MODEL, D_FF),
        'ffn2_w_up': dense(ks[18], D_MODEL, D_FF),
        'ffn2_w_down': dense(ks[19], D_FF, D_MODEL),
        'ffn2_post_w': gain(ks[20], D_MODEL),
    }

def reference(x, ffn1_pre_w, ffn1_w_gate, ffn1_w_up, ffn1_w_down, ffn1_post_w,
              mix_pre_w, w_in, dn_conv_w, dn_a_log, dn_dt_bias, dn_norm_w,
              w_branch_dn, w_branch_mb, w_out, mix_post_w,
              ffn2_pre_w, ffn2_w_gate, ffn2_w_up, ffn2_w_down, ffn2_post_w):
    for l in range(DEPTH):
        h = swiglu(rms_norm(x, ffn1_pre_w[l]), ffn1_w_gate[l], ffn1_w_up[l], ffn1_w_down[l])
        x = x + MACARON_WEIGHT * rms_norm(h, ffn1_post_w[l])
        h = rms_norm(x, mix_pre_w[l])
        dn_qkv, dn_z, dn_b, dn_a, mb_q, mb_k, mb_v, gate_dn, gate_mb = split_projection(h @ w_in[l])
        y_dn = gated_deltanet(dn_qkv, dn_z, dn_b, dn_a, dn_conv_w[l], dn_a_log[l],
                              dn_dt_bias[l], dn_norm_w[l]) @ w_branch_dn[l]
        y_mb = moba_attention(mb_q, mb_k, mb_v) @ w_branch_mb[l]
        merged = jax.nn.sigmoid(gate_dn) * y_dn + jax.nn.sigmoid(gate_mb) * y_mb
        x = x + rms_norm(merged @ w_out[l], mix_post_w[l])
        h = swiglu(rms_norm(x, ffn2_pre_w[l]), ffn2_w_gate[l], ffn2_w_up[l], ffn2_w_down[l])
        x = x + MACARON_WEIGHT * rms_norm(h, ffn2_post_w[l])
    return x


_drawn_inputs = setup_inputs


def setup_inputs(seed=0):
    import zlib

    import numpy as np

    out = dict(_drawn_inputs(seed))
    spreads = {}
    factors = {'ffn1_pre_w': 2.938,
     'ffn1_post_w': 4.31,
     'dn_norm_w': 4.343,
     'mix_post_w': 11.205,
     'ffn2_pre_w': 19.487,
     'ffn2_post_w': 36.607}
    for name, (base, spread) in spreads.items():
        noise = np.random.default_rng([zlib.crc32(name.encode()), seed]).standard_normal(out[name].shape)
        drawn = base * np.exp(spread * noise) if base else spread * noise
        out[name] = jnp.asarray(drawn.astype(out[name].dtype))
    for name, factor in factors.items():
        out[name] = (out[name] * factor).astype(out[name].dtype)
    return out
```

```python
from contextlib import ExitStack

import concourse.bass as bass
from concourse import mybir

F32 = mybir.dt.float32
F32R = mybir.dt.float32r
ALU = mybir.AluOpType
ACT = mybir.ActivationFunctionType
AX = mybir.AxisListType

P = 128
T, D, FF = 512, 1024, 2816
NT, NK, NF = T // P, D // P, FF // P
H, HD = 4, 128
C = 64
MH, MD = 8, 64
EPS = 1e-6
DNW, MBW = H * HD, MH * MD
COL_Z = 3 * DNW
COL_BA = COL_Z + DNW
COL_MBQ = COL_BA + 2 * H
COL_MBV = COL_MBQ + 2 * MBW
COL_GDN = COL_MBV + MBW
COL_GMB = COL_GDN + D

RING = 4
AHEAD = 2
N_FFN = 3 * NF
S_QKV = N_FFN
S_MBQK = S_QKV + 12
S_Z = S_MBQK + 8
S_MBV = S_Z + 4
S_MERGE = S_MBV + 4
S_OUT = S_MERGE + 3 * NK
S_FFN2 = S_OUT + NK
N_SLABS = S_FFN2 + N_FFN
LEVELS = 6
FINS = (0, NF, NF + NK)
KB = 1024

SEMAPHORES = """slab_hi slab_lo slab_used const_in const_made ffn_silu ffn_act
split_hi split_lo y_ready y_square y_root y_inverse y_scaled x_done x_square x_root x_inverse h_done
h_turned hT_hi hT_lo wpost_in wpre_in x_kept x_back ba_hi ba_lo ba_ready convw_ready convw_done
exp_b exp_a beta_sum beta_ready dt_added dt_neg dt_min exp_t ln_t relu_t g_sum g_ready a_exp a_neg sums_ready
gc_ready last_diff decay_tok beta_exp chunk_decay
conv_start conv_tap conv_done qkv_done sq_made sq_summed qk_root qk_inverse qk_scale qk_rows qk_done
mbqk_done tok_ready tok_done
gb_ready diff_made eg_made qdec_done neg_made pos_made decay_row decay_col kk_ready qk_ready amat_done
dec_masked attn_done kT_ready kbe_done kdec_done vT_ready vbeta_done zw_done
level_made level_turned q_ready q_copied dy_ready y_mat dx_ready x_mat wt_ready wt_done u_ready u_done
ws_ready vnew_done kv_ready s_done o_ready o_done o_square o_sum o_root o_inverse o_scaled o_gated
oT_ready oT_hi oT_lo
s_ready s_biased s_max p_done pT_ready pT_copied pv_ready p_inverse mb_done
gate_dn gate_mb merge_dn merge_mb merge_done out_done""".split()


def hybrid_layer(nc, x_in, ffn, w_in, conv_w, a_log, dt_bias, dn_norm_w, w_dn, w_mb, w_out, norms, out):
    ctx = ExitStack()
    with ctx:
        sem = {n: ctx.enter_context(nc.semaphore(n)) for n in SEMAPHORES}
        raw_in = [ctx.enter_context(nc.semaphore(f"raw_in{i}")) for i in range(RING)]
        x_in_sem = [ctx.enter_context(nc.semaphore(f"x_in{i}")) for i in range(NT)]
        base = nc.sbuf_base + (-nc.sbuf_base) % 32

        def at(name, kb, shape, dt=F32):
            return nc.alloc_sbuf_tensor_at(name, shape, dt, offset=base + int(kb * KB))

        raw = at("raw", 0, [P, RING, D])
        w_hi = at("w_hi", 16, [P, RING, D], F32R)
        w_lo = at("w_lo", 32, [P, RING, D], F32R)
        hT_hi = at("hT_hi", 48, [P, NK, T], F32R)
        hT_lo = at("hT_lo", 64, [P, NK, T], F32R)
        wpost = at("wpost", 88, [P, D])
        wpre = at("wpre", 92, [P, D])
        ident = at("ident", 96, [P, P])
        upper = at("upper", 96.5, [P, P])
        same = at("same", 97, [P, P])
        half = at("half", 97.5, [P, 2, P])
        level = at("level", 98.5, [P, LEVELS, P])
        alibi = at("alibi", 101.5, [P, T])
        one_col = at("one_col", 103.5, [P, 8, 8])
        normw = at("normw", 103.75, [P, HD])
        convw = at("convw", 104.25, [P, 4, 12])
        convw_rows = at("convw_rows", 182, [4 * 12, P])
        eps1 = at("eps1", 104.5, [P, 1])
        eps4 = at("eps4", 104.5625, [P, 1])
        y_ss = at("y_ss", 104.625, [P, 3, NT])
        y_rt = at("y_rt", 104.6875, [P, 3, NT])
        y_iv = at("y_iv", 104.75, [P, 3, NT])
        x_ss = at("x_ss", 104.8125, [P, 3, NT])
        x_rt = at("x_rt", 104.875, [P, 3, NT])
        x_iv = at("x_iv", 104.9375, [P, 3, NT])
        dtb = at("dtb", 105, [P, H])
        alog = at("alog", 105.03125, [P, H])
        nega = at("nega", 105.0625, [P, H])
        nega2 = at("nega2", 105.09375, [P, H])
        qscale = at("qscale", 105.125, [8, 1])
        wba_raw = at("wba_raw", 105.25, [P, NK, 8])
        wba_hi = at("wba_hi", 105.5, [P, NK, 8], F32R)
        wba_lo = at("wba_lo", 105.75, [P, NK, 8], F32R)
        small = at("small", 206, [P, 28, NT * H])
        a_hi = at("a_hi", 80, [P, 2, T], F32R)
        a_lo = at("a_lo", 84, [P, 2, T], F32R)
        x = at("x", 106, [P, NT, D])
        hnat = at("hnat", 122, [P, 2, D])
        junk = at("junk", 130, [P, D])
        fact = at("fact", 134, [P, NF * T])
        silu = at("silu", 178, [P, 2, T])
        vnew = at("vnew", 80, [P, 2, T])
        state = at("state", 84, [P, H * HD])
        mbv = at("mbv", 106, [P, NT, MBW])
        z = at("z", 114, [P, NT, DNW])
        attnT = at("attnT", 122, [P, 2, T])
        kdec = at("kdec", 126, [P, 2, T])
        qdec = at("qdec", 130, [P, 2, T])
        qkT = at("qkT", 134, [P, 2 * H, T])
        v = at("v", 150, [P, NT, DNW])
        vT = at("vT", 198, [P, H, T])
        mbqk = at("mbqk", 158, [P, 8, T])
        amat = at("amat", 174, [P, 2, T])
        xmat = at("xmat", 178, [P, 2, T])
        ymat = at("ymat", 182, [P, 2, T])
        qmat = at("qmat", 186, [P, 2, T])
        cmat = at("cmat", 190, [P, 2, T])
        kbe = at("kbe", 194, [P, 2, T])
        cacc = at("cacc", 174, [P, 2, T])
        sq = at("sq", 178, [P, 2, T])
        qk_rt = at("qk_rt", 182, [8, T])
        qk_iv = at("qk_iv", 184, [8, T])
        logit = at("logit", 122, [P, 2, T])
        prob = at("prob", 126, [P, 2, T])
        probT = at("probT", 130, [P, 2, T])
        omb = at("omb", 198, [P, NT, MBW])
        oT_hi_t = at("oT_hi_t", 174, [P, 8, T], F32R)
        oT_lo_t = at("oT_lo_t", 134, [P, 8, T], F32R)
        sig = at("sig", 190, [P, 2, 2, T])
        prod = at("prod", 150, [P, 2, T])
        merged = at("merged", 158, [P, NK * T])
        x_keep = nc.dram_tensor("x_keep", (T, D), F32, kind="Internal").ap()

        ps = ctx.enter_context(nc.psum_tensor("ps", [P, 8, T], F32))

        (BETA0, BETA1, BETA, DTA, DTN, DTM, EXPT, LNT, RELU, GSUM, G, GC, LASTD, DECT, EGC, BEG,
         CD0, CD1, OSS, ORT, OIV) = range(21)
        PM, PS, PI = 21, 23, 25

        def row(r, n=1):
            return small[:, r:r + n, :].rearrange("p a b -> p (a b)")

        def row_th(r):
            return small[:, r, :].rearrange("p (t h) -> p t h", h=H)

        def heads(ap):
            return ap.rearrange("p (h d) -> p h d", h=H)

        def per_head(r, t):
            return small[:, r, t * H:(t + 1) * H].unsqueeze(2).to_broadcast([P, H, HD])

        def over_heads(ap):
            return ap.unsqueeze(1).to_broadcast([P, H, P])

        def ybank(i):
            return (2 * i + 4) % 8

        def wait_y(eng, st, i):
            if i < NT - 1:
                eng.wait_ge(sem["y_ready"], st * (NT - 1) + i + 1)
            else:
                eng.wait_ge(sem["slab_used"], (S_QKV, S_FFN2, N_SLABS)[st])

        def slab(first, j, i=0):
            return first + j + 4 * i, (first + j) % RING, (first + j) // RING + i

        block = ctx.enter_context(nc.Block())

        @block.sync
        def _(sp):
            def load(number, slot, src, dst=None):
                if dst is None:
                    dst, src = (a.rearrange("p (h n) -> p h n", h=2) for a in (raw[:, slot, :], src))
                m = dst.shape[1] // 2
                for hf in range(2):
                    sp.dma_start(dst[:, hf * m:(hf + 1) * m, :], src[:, hf * m:(hf + 1) * m, :]).then_inc(raw_in[slot], 16)

            def free(number, first=False):
                if not first:
                    sp.wait_ge(sem["slab_lo"], number - RING + 1)

            def col_tile(w, col):
                return w[:, bass.ds(col, P)].rearrange("(k p) n -> p k n", p=P)

            def k_view(slot, k=NK):
                return raw[:, slot, :].rearrange("p (k n) -> p k n", k=k)

            def ffn_loads(f, s0):
                wg, wu, wd = ffn[f]

                def pair(i, first=False):
                    for j in range(4):
                        s, slot, _ = slab(s0, j, i)
                        free(s, first)
                        load(s, slot, col_tile((wg, wu)[j % 2], (2 * i + j // 2) * P), k_view(slot))
                pair(0, f == 0)
                with sp.Fori(1, NF // 2) as i:
                    pair(i)

                def down(j, i=0):
                    s, slot, _ = slab(s0 + 2 * NF, j, i)
                    free(s)
                    load(s, slot, wd[bass.ds((j + 4 * i) * P, P), :])
                down(0)
                with sp.Fori(0, (NF - 2) // 4) as i:
                    for j in range(1, 5):
                        down(j, i)
                down(NF - 1)

            for i in range(NT):
                sp.dma_start(x[:, i, :], x_in[i * P:(i + 1) * P, :]).then_inc(x_in_sem[i], 16)
            ffn_loads(0, 0)
            for j in range(12):
                s, slot, _ = slab(S_QKV, j)
                free(s)
                load(s, slot, col_tile(w_in, j * P), k_view(slot))
            for j in range(8):
                s, slot, _ = slab(S_MBQK, j)
                free(s)
                load(s, slot, col_tile(w_in, COL_MBQ + j * P), k_view(slot))
            for first, col in ((S_Z, COL_Z), (S_MBV, COL_MBV)):
                for j in range(4):
                    s, slot, _ = slab(first, j)
                    free(s)
                    load(s, slot, w_in[2 * j * P:(2 * j + 2) * P, col:col + T]
                         .rearrange("(k p) n -> p k n", p=P), k_view(slot, 2))
            for n in range(NK):
                for j in range(3):
                    s, slot, _ = slab(S_MERGE, 3 * n + j)
                    free(s)
                    if j < 2:
                        load(s, slot, col_tile(w_in, (COL_GDN, COL_GMB)[j] + n * P), k_view(slot))
                    else:
                        v2 = raw[:, slot, :].rearrange("p (b k n) -> p b k n", b=2, k=4)
                        for b, w in enumerate((w_dn, w_mb)):
                            src = w[:, n * P:(n + 1) * P].rearrange("(k p) n -> p k n", p=P)
                            sp.dma_start(v2[:, b], src).then_inc(raw_in[slot], 16)
            for k in range(NK):
                s, slot, _ = slab(S_OUT, k)
                free(s)
                load(s, slot, w_out[k * P:(k + 1) * P, :])
            ffn_loads(1, S_FFN2)
            for i in range(NT):
                sp.wait_ge(sem["x_done"], 2 * NT + i + 1)
                sp.dma_start(out[i * P:(i + 1) * P, :], x[:, i, :]).then_inc(sem["out_done"], 16)
            sp.wait_ge(sem["out_done"], 16 * NT)

        def split_hi(act, number, slot, use, first=False):
            act.wait_ge(raw_in[slot], 32 * (use + 1))
            if not first:
                act.wait_ge(sem["slab_used"], number - RING + 1)
            act.activation(w_hi[:, slot, :], raw[:, slot, :], ACT.Copy).then_inc(sem["slab_hi"], 1)

        def split_lo(dve, number, slot, use):
            dve.wait_ge(sem["slab_hi"], number + 1)
            dve.tensor_tensor(w_lo[:, slot, :], raw[:, slot, :], w_hi[:, slot, :].bitcast(F32),
                              ALU.subtract).then_inc(sem["slab_lo"], 1)

        @block.gpsimd
        def _(pool):
            def const(ins):
                const.n += 1
                ins.then_inc(sem["const_made"], 1)
                pool.wait_ge(sem["const_made"], const.n)
            const.n = 0
            const(pool.memset(eps1[:], EPS))
            const(pool.memset(eps4[:], 4 * EPS))
            const(pool.memset(ident[:], 0.0))
            const(pool.affine_select(out=ident[:], in_=ident[:], compare_op=ALU.not_equal, fill=1.0, base=0,
                                     pattern=[[-1, P]], channel_multiplier=1))
            pool.dma_start(wpre[:], norms[0][0].partition_broadcast(P)).then_inc(sem["wpre_in"], 16)
            pool.dma_start(wba_raw[:], w_in[:, COL_BA:COL_BA + 8].rearrange("(k p) n -> p k n", p=P)).then_inc(sem["const_in"], 16)
            pool.dma_start(dtb[:], dt_bias.partition_broadcast(P)).then_inc(sem["const_in"], 16)
            pool.dma_start(alog[:], a_log.partition_broadcast(P)).then_inc(sem["const_in"], 16)
            pool.dma_start(normw[:], dn_norm_w.partition_broadcast(P)).then_inc(sem["const_in"], 16)
            pool.dma_start(convw_rows[:], conv_w.rearrange("k (j p) -> (k j) p", p=P)).then_inc(sem["const_in"], 16)
            pool.dma_start(wpost[:], norms[0][1].partition_broadcast(P)).then_inc(sem["wpost_in"], 16)

            const(pool.memset(upper[:], 1.0))
            const(pool.affine_select(out=upper[:], in_=upper[:], compare_op=ALU.is_ge, fill=0.0, base=0,
                                     pattern=[[1, P]], channel_multiplier=-1))
            const(pool.memset(upper[0:C, C:P], 0.0))
            const(pool.memset(same[:], 0.0))
            const(pool.memset(same[0:C, 0:C], 1.0))
            const(pool.memset(same[C:P, C:P], 1.0))
            const(pool.memset(half[:], 0.0))
            const(pool.memset(half[0:C, 0, :], 1.0))
            const(pool.memset(half[C:P, 1, :], 1.0))
            const(pool.memset(one_col[:], 0.0))
            for j in range(8):
                const(pool.memset(one_col[:, j, j:j + 1], 1.0))
            const(pool.memset(qscale[:], 1.0))
            const(pool.memset(qscale[0:H, :], float(HD) ** -0.5))
            const(pool.memset(level[:], 0.0))
            for l in range(LEVELS):
                b = 1 << l
                left = level[:, l, :].rearrange("p (n two b) -> p n two b", two=2, b=b)[:, :, 0, :]
                const(pool.memset(left, 1.0))
                const(pool.affine_select(out=left, in_=left, compare_op=ALU.is_ge, fill=0.0, base=-b,
                                         pattern=[[-2 * b, P // (2 * b)], [0, b]], channel_multiplier=1))
                const(pool.affine_select(out=left, in_=left, compare_op=ALU.is_ge, fill=0.0, base=2 * b - 1,
                                         pattern=[[2 * b, P // (2 * b)], [0, b]], channel_multiplier=-1))
            const(pool.iota(alibi[:], pattern=[[1, T]], base=-(T - P), channel_multiplier=-1,
                            allow_small_or_imprecise_dtypes=True))
            const(pool.affine_select(out=alibi[:], in_=alibi[:], compare_op=ALU.is_ge, fill=-1e30,
                                     base=T - P, pattern=[[-1, T]], channel_multiplier=1))
            assert const.n == N_CONST, const.n

            pool.wait_ge(sem["h_done"], NT)
            pool.dma_start(wpre[:], norms[1][0].partition_broadcast(P)).then_inc(sem["wpre_in"], 16)
            pool.wait_ge(sem["x_done"], NT)
            pool.dma_start(wpost[:], norms[1][1].partition_broadcast(P)).then_inc(sem["wpost_in"], 16)
            pool.wait_ge(sem["h_done"], 2 * NT)
            pool.dma_start(x_keep.rearrange("(t p) d -> p t d", p=P), x[:]).then_inc(sem["x_kept"], 16)
            pool.dma_start(wpre[:], norms[2][0].partition_broadcast(P)).then_inc(sem["wpre_in"], 16)
            for j in range(8):
                pool.wait_ge(sem["qkv_done"], j + 1)
                if j >= 2:
                    pool.wait_ge(sem["sq_summed"], j - 1)
                pool.tensor_tensor(sq[:, j % 2, :], qkT[:, j, :], qkT[:, j, :], ALU.mult).then_inc(sem["sq_made"], 1)
            pool.wait_ge(sem["const_in"], 16 * N_ROWS)
            for t in range(NT):
                pool.wait_ge(sem["tok_done"], t + 1)
                pool.tensor_tensor(heads(z[:, t, :]), heads(z[:, t, :]), over_heads(normw[:]), ALU.mult).then_inc(sem["zw_done"], 1)
            for pair in range(2):
                for l in range(LEVELS):
                    for q in range(2):
                        t = 2 * pair + q
                        n = (pair * LEVELS + l) * 2 + q
                        pool.wait_ge(sem["amat_done"], t + 1)
                        if l == 0:
                            pool.wait_ge(sem["decay_row"], t + 1)
                        elif l == 1:
                            pool.wait_ge(sem["x_mat"], pair * 10 + q + 1)
                            pool.wait_ge(sem["level_turned"], pair * 2 + q + 1)
                        else:
                            pool.wait_ge(sem["q_ready"], pair * 10 + (l - 2) * 2 + q + 1)
                        pool.tensor_tensor(heads(cmat[:, q, :]), heads(amat[:, q, :]), over_heads(level[:, l, :]),
                                           ALU.mult).then_inc(sem["level_made"], 1)
            pool.wait_ge(sem["mb_done"], MH)
            pool.wait_ge(sem["o_gated"], NT)
            pool.wait_ge(sem["x_kept"], 16)
            pool.wait_ge(sem["pv_ready"], MH)
            pool.dma_start(x[:], x_keep.rearrange("(t p) d -> p t d", p=P)).then_inc(sem["x_back"], 16)
            pool.wait_ge(sem["x_done"], 2 * NT)
            pool.dma_start(wpost[:], norms[2][1].partition_broadcast(P)).then_inc(sem["wpost_in"], 16)

        @block.scalar
        def _(act):
            A = act.activation
            ahead = [0]

            def hi_next(first=False):
                if ahead[0] < N_SLABS:
                    s, slot, use = slab(ahead[0], 0)
                    split_hi(act, s, slot, use, first)
                    ahead[0] += 1

            def post(st, i):
                y = ps[:, ybank(i):ybank(i) + 2, :]
                wait_y(act, st, i)
                if st or i:
                    act.wait_ge(sem["y_square"], st * NT + i)
                act.wait_ge(sem["x_square"], min((st + 1) * NT + max(i - 1, 0), 3 * NT))
                A(junk[:].rearrange("p (a b) -> p a b", a=2), y, ACT.Square, accum_out=y_ss[:, st, i:i + 1]).then_inc(sem["y_square"], 1)
                act.wait_ge(sem["y_square"], st * NT + i + 1)
                k = 1.0 if st == 1 else 4.0
                A(y_rt[:, st, i:i + 1], y_ss[:, st, i:i + 1], ACT.Sqrt, scale=k / D,
                  bias=(eps1 if st == 1 else eps4)[:]).then_inc(sem["y_root"], 1)

            def pre(st, i):
                if st:
                    act.wait_ge(sem["x_done"], (st - 1) * NT + i + 1)
                    act.wait_ge(sem["y_square"], (st - 1) * NT + min(i + 2, NT))
                else:
                    act.wait_ge(x_in_sem[i], 16)
                    if i == 0:
                        act.wait_ge(sem["const_made"], 2)
                if i:
                    act.wait_ge(sem["x_square"], st * NT + i)
                A(junk[:], x[:, i, :], ACT.Square, accum_out=x_ss[:, st, i:i + 1]).then_inc(sem["x_square"], 1)
                act.wait_ge(sem["x_square"], st * NT + i + 1)
                A(x_rt[:, st, i:i + 1], x_ss[:, st, i:i + 1], ACT.Sqrt, scale=1.0 / D, bias=eps1[:]).then_inc(sem["x_root"], 1)

            def turned(st, i):
                for hf in range(2):
                    act.wait_ge(sem["h_turned"], (st * NT + i) * 2 + hf + 1)
                    A(hT_hi[:, 4 * hf:4 * hf + 4, i * P:(i + 1) * P],
                      ps[:, ybank(i) + hf, :].rearrange("p (k n) -> p k n", k=4), ACT.Copy).then_inc(sem["hT_hi"], 1)

            def boundary(post_st, pre_st):
                for i in range(NT + 2):
                    if post_st is not None and i < NT:
                        post(post_st, i)
                    if pre_st is not None and 1 <= i <= NT:
                        pre(pre_st, i - 1)
                    if pre_st is not None and i >= 2:
                        turned(pre_st, i - 2)

            def split_act(src, fin, k, slot, used):
                if used is not None:
                    act.wait_ge(sem["slab_used"], used)
                A(a_hi[:, slot, :], src, ACT.Copy).then_inc(sem["split_hi"], 1)

            def ffn_stage(f, s0):
                def tile(i, j):
                    for q in range(2):
                        s, slot, use = slab(s0, AHEAD + 2 * j + q, i)
                        split_hi(act, s, slot, use, first=isinstance(i, int) and i == 0 and s < RING)
                    act.wait_ge(sem["slab_used"], s0 + 4 * i + 2 * j + 1)
                    if not (isinstance(i, int) and i == 0 and f == 0):
                        act.wait_ge(sem["ffn_act"], f * NF + 2 * i + j - 1)
                    A(silu[:, j, :], ps[:, 2 * j, :], ACT.Silu).then_inc(sem["ffn_silu"], 1)
                for j in range(2):
                    tile(0, j)
                with act.Fori(1, NF // 2) as i:
                    for j in range(2):
                        tile(i, j)
                act.wait_ge(sem["ffn_act"], (f + 1) * NF)
                s1 = s0 + 2 * NF
                split_act(fact[:, 0:T], f, 0, 0, None)

                def step(j, i=0, last=False):
                    s, slot, use = slab(s1, j + AHEAD, i)
                    if not isinstance(s, int) or s < N_SLABS:
                        split_hi(act, s, slot, use)
                    k = j + 4 * i
                    A_src = fact[:, bass.ds((k + 1) * T, T)]
                    split_act(A_src, f, k + 1, (j + 1) % 2, s1 + k)
                step(0)
                with act.Fori(0, (NF - 2) // 4 - 1) as i:
                    for j in range(1, 5):
                        step(j, i)
                for k in range(NF - 5, NF - 1):
                    step(k)
                ahead[0] = s1 + NF + AHEAD - 1
                hi_next()

            hi_next(True)
            hi_next(True)
            boundary(None, 0)
            act.wait_ge(sem["const_in"], 16 * N_ROWS)
            A(wba_hi[:], wba_raw[:], ACT.Copy).then_inc(sem["ba_hi"], 1)
            A(nega[:], alog[:], ACT.Exp).then_inc(sem["a_exp"], 1)
            ffn_stage(0, 0)
            boundary(0, 1)

            ab = ps[:, 4, 0:NT * 8].rearrange("p (t c) -> p t c", c=8)
            act.wait_ge(sem["ba_ready"], 1)
            A(row_th(BETA0), ab[:, :, 0:H], ACT.Exp, scale=-1.0).then_inc(sem["exp_b"], 1)
            act.wait_ge(sem["dt_min"], 1)
            A(row(EXPT), row(DTM), ACT.Exp).then_inc(sem["exp_t"], 1)
            act.wait_ge(sem["exp_t"], 1)
            A(row(LNT), row(EXPT), ACT.Ln, bias=1.0).then_inc(sem["ln_t"], 1)

            def finish_qkv(j):
                act.wait_ge(sem["conv_done"], j + 1)
                dst = qkT[:, j, :] if j < 8 else vT[:, j - 8, :]
                A(dst, cacc[:, j % 2, :], ACT.Silu).then_inc(sem["qkv_done"], 1)

            for j in range(12):
                hi_next()
                if j:
                    finish_qkv(j - 1)
                act.wait_ge(sem["slab_used"], S_QKV + j + 1)
                if j >= 2:
                    act.wait_ge(sem["qkv_done"], j - 1)
                A(cacc[:, j % 2, :], ps[:, j % 4, :], ACT.Copy, scale=convw[:, 3, j:j + 1]).then_inc(sem["conv_start"], 1)
            finish_qkv(11)
            act.wait_ge(sem["sq_summed"], 8)
            A(qk_rt[:], ps[0:8, 5, :], ACT.Sqrt, bias=eps1[0:8, :]).then_inc(sem["qk_root"], 1)
            act.wait_ge(sem["beta_ready"], 1)
            act.wait_ge(sem["gc_ready"], 1)
            A(row(EGC), row(GC), ACT.Exp).then_inc(sem["decay_tok"], 1)
            act.wait_ge(sem["last_diff"], 1)
            A(row(DECT), row(LASTD), ACT.Exp).then_inc(sem["decay_tok"], 1)
            A(row(CD0, 2), ps[:, 6, 32:64], ACT.Exp).then_inc(sem["chunk_decay"], 1)

            for j in range(8):
                hi_next()
                act.wait_ge(sem["slab_used"], S_MBQK + j + 1)
                A(mbqk[:, j, :], ps[:, j % 4, :], ACT.Copy, scale=(float(MD) ** -0.5 if j < 4 else 1.0)).then_inc(sem["mbqk_done"], 1)
            for g, (dst, func) in enumerate(((z, ACT.Silu), (mbv, ACT.Copy))):
                for j in range(4):
                    hi_next()
                act.wait_ge(sem["x_kept"], 16)
                for t in range(NT):
                    if t < NT - 1:
                        act.wait_ge(sem["tok_ready"], g * (NT - 1) + t + 1)
                    else:
                        act.wait_ge(sem["slab_used"], (S_MBV, S_MERGE)[g])
                    A(dst[:, t, :], ps[:, 4 * g + t, :], func).then_inc(sem["tok_done"], 1)

            for pair in range(2):
                tiles = [(q, 2 * pair + q, 4 - 4 * q) for q in range(2)]
                for q, t, b in tiles:
                    act.wait_ge(sem["diff_made"], t + 1)
                    if pair:
                        act.wait_ge(sem["wt_ready"], 2 * (pair - 1) + q + 1)
                        act.wait_ge(sem["u_ready"], 2 * (pair - 1) + q + 1)
                    A(ymat[:, q, :], ps[:, b, :], ACT.Exp).then_inc(sem["eg_made"], 1)
                for q, t, b in tiles:
                    act.wait_ge(sem["pos_made"], t + 1)
                    A(cmat[:, q, :], cmat[:, q, :], ACT.Exp).then_inc(sem["decay_row"], 1)
                    A(qmat[:, q, :], qmat[:, q, :], ACT.Exp).then_inc(sem["decay_col"], 1)
                for l in range(1, LEVELS):
                    for q, t, b in tiles:
                        act.wait_ge(sem["q_ready"], (pair * 5 + l - 1) * 2 + q + 1)
                        if l == 1:
                            act.wait_ge(sem["dec_masked"], t + 1)
                            act.wait_ge(sem["attn_done"], t + 1)
                        else:
                            act.wait_ge(sem["dx_ready"], (pair * 4 + l - 2) * 2 + q + 1)
                        A(qmat[:, q, :], ps[:, b + 1, :], ACT.Copy).then_inc(sem["q_copied"], 1)
                for q, t, b in tiles:
                    act.wait_ge(sem["wt_ready"], t + 1)
                    A(kbe[:, q, :], ps[:, b, :], ACT.Copy).then_inc(sem["wt_done"], 1)
                for q, t, b in tiles:
                    act.wait_ge(sem["o_ready"], 2 * t + 2)
                    A(v[:, t, :], ps[:, b + 3, :], ACT.Copy).then_inc(sem["o_done"], 1)
            for t in range(NT):
                act.wait_ge(sem["o_done"], t + 1)
                act.wait_ge(sem["dx_ready"], 16)
                if t >= 2:
                    act.wait_ge(sem["o_sum"], t - 1)
                A(xmat[:, t % 2, :], v[:, t, :], ACT.Square).then_inc(sem["o_square"], 1)
            act.wait_ge(sem["o_sum"], NT)
            A(row(ORT), row(OSS), ACT.Sqrt, scale=1.0 / HD, bias=eps1[:]).then_inc(sem["o_root"], 1)

            def branch_hi(g, t):
                act.wait_ge(sem["oT_ready"], g * NT + t + 1)
                A(oT_hi_t[:, 4 * g:4 * g + 4, t * P:(t + 1) * P],
                  ps[:, t, :].rearrange("p (k n) -> p k n", k=4), ACT.Copy).then_inc(sem["oT_hi"], 1)
            for t in range(NT):
                branch_hi(0, t)

            for u in range(MH * NT):
                h, i = divmod(u, NT)
                w = (i + 1) * P
                act.wait_ge(sem["s_max"], u + 1)
                if u >= 2:
                    act.wait_ge(sem["pT_ready"], u - 1)
                A(prob[:, u % 2, 0:w], logit[:, u % 2, 0:w], ACT.Exp, bias=row(PM, 2)[:, u:u + 1],
                  accum_out=row(PS, 2)[:, u:u + 1]).then_inc(sem["p_done"], 1)
                act.wait_ge(sem["pT_ready"], u + 1)
                A(probT[:, u % 2, 0:w], ps[:, 6, 0:w], ACT.Copy).then_inc(sem["pT_copied"], 1)
            for t in range(NT):
                branch_hi(1, t)

            for n in range(NK):
                for j in range(3):
                    hi_next()
                b = 4 * (n % 2)
                act.wait_ge(sem["slab_used"], S_MERGE + 3 * n + 1)
                if n >= 2:
                    act.wait_ge(sem["merge_mb"], n - 1)
                A(sig[:, n % 2, 0, :], ps[:, b, :], ACT.Sigmoid).then_inc(sem["gate_dn"], 1)
                act.wait_ge(sem["slab_used"], S_MERGE + 3 * n + 2)
                A(sig[:, n % 2, 1, :], ps[:, b + 1, :], ACT.Sigmoid).then_inc(sem["gate_mb"], 1)
            for k in range(NK + 1):
                if k:
                    hi_next()
                if k < NK:
                    act.wait_ge(sem["merge_done"], k + 1)
                    split_act(merged[:, k * T:(k + 1) * T], 1, k, k % 2, S_OUT + k - 1 if k else None)
            boundary(1, 2)
            ffn_stage(1, S_FFN2)
            boundary(2, None)

        @block.vector
        def _(dve):
            ahead = [0]

            def lo_next():
                if ahead[0] < N_SLABS:
                    split_lo(dve, *slab(ahead[0], 0))
                    ahead[0] += 1

            def post(st, i):
                y = ps[:, ybank(i):ybank(i) + 2, :]
                dve.wait_ge(sem["y_root"], st * NT + i + 1)
                dve.reciprocal(y_iv[:, st, i:i + 1], y_rt[:, st, i:i + 1]).then_inc(sem["y_inverse"], 1)
                dve.wait_ge(sem["y_inverse"], st * NT + i + 1)
                dve.wait_ge(sem["wpost_in"], 16 * (st + 1))
                if st or i:
                    dve.wait_ge(sem["x_done"], st * NT + i)
                if i == 0 and st == 1:
                    dve.wait_ge(sem["x_back"], 16)
                dve.scalar_tensor_tensor(hnat[:, 1, :].rearrange("p (a b) -> p a b", a=2), y, y_iv[:, st, i:i + 1],
                                         wpost[:].rearrange("p (a b) -> p a b", a=2), ALU.mult, ALU.mult).then_inc(sem["y_scaled"], 1)
                dve.wait_ge(sem["y_scaled"], st * NT + i + 1)
                dve.tensor_tensor(x[:, i, :], x[:, i, :], hnat[:, 1, :], ALU.add).then_inc(sem["x_done"], 1)

            def pre(st, i):
                dve.wait_ge(sem["x_root"], st * NT + i + 1)
                dve.reciprocal(x_iv[:, st, i:i + 1], x_rt[:, st, i:i + 1]).then_inc(sem["x_inverse"], 1)
                dve.wait_ge(sem["x_inverse"], st * NT + i + 1)
                if i == 0:
                    dve.wait_ge(sem["wpre_in"], 16 * (st + 1))
                if i or st:
                    dve.wait_ge(sem["h_turned"], 2 * (st * NT + i))
                dve.scalar_tensor_tensor(hnat[:, 0, :], x[:, i, :], x_iv[:, st, i:i + 1], wpre[:],
                                         ALU.mult, ALU.mult).then_inc(sem["h_done"], 1)

            def turned(st, i):
                for hf in range(2):
                    n = (st * NT + i) * 2 + hf + 1
                    dve.wait_ge(sem["hT_hi"], n)
                    dst = (slice(None), slice(4 * hf, 4 * hf + 4), slice(i * P, (i + 1) * P))
                    dve.tensor_tensor(hT_lo[dst], ps[:, ybank(i) + hf, :].rearrange("p (k n) -> p k n", k=4), hT_hi[dst].bitcast(F32), ALU.subtract).then_inc(sem["hT_lo"], 1)

            def boundary(post_st, pre_st):
                for i in range(NT + 2):
                    if post_st is not None and i < NT:
                        post(post_st, i)
                    if pre_st is not None and 1 <= i <= NT:
                        pre(pre_st, i - 1)
                    if pre_st is not None and i >= 2:
                        turned(pre_st, i - 2)

            def split_act(src, n, slot):
                dve.wait_ge(sem["split_hi"], n)
                dve.tensor_tensor(a_lo[:, slot, :], src, a_hi[:, slot, :].bitcast(F32), ALU.subtract).then_inc(sem["split_lo"], 1)

            def ffn_stage(f, s0):
                def tile(i, j):
                    for q in range(2):
                        split_lo(dve, *slab(s0, AHEAD + 2 * j + q, i))
                    n = f * NF + 2 * i + j + 1
                    dve.wait_ge(sem["ffn_silu"], n)
                    dve.wait_ge(sem["slab_used"], s0 + 4 * i + 2 * j + 2)
                    dve.tensor_tensor(fact[:, bass.ds((2 * i + j) * T, T)], silu[:, j, :], ps[:, 2 * j + 1, :],
                                      ALU.mult).then_inc(sem["ffn_act"], 1)
                for j in range(2):
                    tile(0, j)
                with dve.Fori(1, NF // 2) as i:
                    for j in range(2):
                        tile(i, j)
                dve.wait_ge(sem["ffn_act"], (f + 1) * NF)
                s1 = s0 + 2 * NF
                first = FINS[2 * f]
                split_act(fact[:, 0:T], first + 1, 0)

                def step(j, i=0):
                    s, slot, use = slab(s1, j + AHEAD, i)
                    if not isinstance(s, int) or s < N_SLABS:
                        split_lo(dve, s, slot, use)
                    k = j + 4 * i
                    split_act(fact[:, bass.ds((k + 1) * T, T)], first + k + 2, (j + 1) % 2)
                step(0)
                with dve.Fori(0, (NF - 2) // 4 - 1) as i:
                    for j in range(1, 5):
                        step(j, i)
                for k in range(NF - 5, NF - 1):
                    step(k)
                ahead[0] = s1 + NF + AHEAD - 1
                lo_next()

            lo_next()
            lo_next()
            boundary(None, 0)
            dve.wait_ge(sem["ba_hi"], 1)
            dve.wait_ge(sem["convw_ready"], 1)
            dve.tensor_copy(convw[:].rearrange("p k j -> p (k j)"), ps[:, 3, 0:48]).then_inc(sem["convw_done"], 1)
            dve.tensor_tensor(wba_lo[:], wba_raw[:], wba_hi[:].bitcast(F32), ALU.subtract).then_inc(sem["ba_lo"], 1)
            ffn_stage(0, 0)
            boundary(0, 1)

            ab = ps[:, 4, 0:NT * 8].rearrange("p (t c) -> p t c", c=8)
            dve.wait_ge(sem["exp_b"], 1)
            dve.tensor_tensor(row_th(DTA), ab[:, :, H:2 * H], dtb[:].unsqueeze(1).to_broadcast([P, NT, H]), ALU.add).then_inc(sem["dt_added"], 1)
            dve.tensor_scalar(row(BETA1), row(BETA0), 1.0, None, ALU.add).then_inc(sem["beta_sum"], 1)
            dve.wait_ge(sem["dt_added"], 1)
            dve.tensor_scalar(row(DTN), row(DTA), -1.0, None, ALU.mult).then_inc(sem["dt_neg"], 1)
            dve.wait_ge(sem["dt_neg"], 1)
            dve.tensor_tensor(row(DTM), row(DTA), row(DTN), ALU.min).then_inc(sem["dt_min"], 1)
            dve.wait_ge(sem["beta_sum"], 1)
            dve.reciprocal(row(BETA), row(BETA1)).then_inc(sem["beta_ready"], 1)
            dve.tensor_scalar(row(RELU), row(DTA), 0.0, None, ALU.max).then_inc(sem["relu_t"], 1)
            dve.wait_ge(sem["a_exp"], 1)
            dve.tensor_scalar(nega2[:], nega[:], -1.0, None, ALU.mult).then_inc(sem["a_neg"], 1)
            dve.wait_ge(sem["relu_t"], 1)
            dve.wait_ge(sem["ln_t"], 1)
            dve.tensor_tensor(row(GSUM), row(RELU), row(LNT), ALU.add).then_inc(sem["g_sum"], 1)
            dve.wait_ge(sem["g_sum"], 1)
            dve.wait_ge(sem["a_neg"], 1)
            dve.tensor_tensor(row_th(G), row_th(GSUM), nega2[:].unsqueeze(1).to_broadcast([P, NT, H]), ALU.mult).then_inc(sem["g_ready"], 1)

            for j in range(12):
                lo_next()
                dve.wait_ge(sem["conv_start"], j + 1)
                for k in range(1, 4):
                    acc = cacc[:, j % 2, k:T]
                    dve.scalar_tensor_tensor(acc, ps[:, j % 4, 0:T - k], convw[:, 3 - k, j:j + 1], acc, ALU.mult,
                                             ALU.add).then_inc(sem["conv_done" if k == 3 else "conv_tap"], 1)
                    if k < 3:
                        dve.wait_ge(sem["conv_tap"], 2 * j + k)
                if j == 2:
                    dve.wait_ge(sem["sums_ready"], 1)
                    dve.tensor_copy(row(GC), ps[:, 6, 0:16]).then_inc(sem["gc_ready"], 1)
                    dve.wait_ge(sem["gc_ready"], 1)
                    dve.tensor_tensor(row(LASTD), ps[:, 6, 16:32], row(GC), ALU.subtract).then_inc(sem["last_diff"], 1)
            dve.wait_ge(sem["qk_root"], 1)
            dve.reciprocal(qk_iv[:], qk_rt[:]).then_inc(sem["qk_inverse"], 1)
            dve.wait_ge(sem["qk_inverse"], 1)
            dve.tensor_scalar(qk_iv[:], qk_iv[:], qscale[:, 0:1], None, ALU.mult).then_inc(sem["qk_scale"], 1)
            dve.wait_ge(sem["decay_tok"], 1)
            dve.tensor_tensor(row(BEG), row(EGC), row(BETA), ALU.mult).then_inc(sem["beta_exp"], 1)
            for j in range(8):
                lo_next()
                dve.wait_ge(sem["qk_rows"], j + 1)
                dve.tensor_tensor(qkT[:, j, :], qkT[:, j, :], ps[:, 4 + j % 4, :], ALU.mult).then_inc(sem["qk_done"], 1)
            for j in range(8):
                lo_next()

            for pair in range(2):
                tiles = [(q, 2 * pair + q, 4 - 4 * q) for q in range(2)]
                for q, t, b in tiles:
                    dve.wait_ge(sem["gb_ready"], t + 1)
                    if pair:
                        dve.wait_ge(sem["dx_ready"], 2 * 4 * (pair - 1) + 8)
                        dve.wait_ge(sem["dy_ready"], 2 * 5 * (pair - 1) + 10)
                    dve.tensor_tensor(heads(xmat[:, q, :]), heads(ps[:, b, :]), per_head(GC, t), ALU.subtract).then_inc(sem["diff_made"], 1)
                for q, t, b in tiles:
                    dve.wait_ge(sem["diff_made"], t + 1)
                    if pair:
                        dve.wait_ge(sem["q_ready"], pair * 10)
                    dve.tensor_scalar(cmat[:, q, :], xmat[:, q, :], -1.0, 0.0, ALU.mult, ALU.min).then_inc(sem["neg_made"], 1)
                    dve.tensor_scalar(qmat[:, q, :], xmat[:, q, :], 0.0, None, ALU.min).then_inc(sem["pos_made"], 1)
                for q, t, b in tiles:
                    dve.wait_ge(sem["eg_made"], t + 1)
                    if pair:
                        dve.wait_ge(sem["o_ready"], 4)
                    dve.tensor_tensor(heads(qdec[:, q, :]), qkT[:, 0:H, t * P:(t + 1) * P], heads(ymat[:, q, :]), ALU.mult).then_inc(sem["qdec_done"], 1)
                for q, t, b in tiles:
                    dve.wait_ge(sem["kk_ready"], t + 1)
                    dve.wait_ge(sem["decay_row"], t + 1)
                    for h in range(H):
                        hs = slice(h * HD, (h + 1) * HD)
                        ins = dve.scalar_tensor_tensor(amat[:, q, hs], cmat[:, q, hs], row(BETA)[:, t * H + h:t * H + h + 1],
                                                       ps[:, b + 1, hs], ALU.mult, ALU.mult)
                    ins.then_inc(sem["amat_done"], 1)
                for q, t, b in tiles:
                    dve.wait_ge(sem["decay_col"], t + 1)
                    dve.tensor_tensor(heads(qmat[:, q, :]), heads(qmat[:, q, :]), over_heads(upper[:]), ALU.mult).then_inc(sem["dec_masked"], 1)
                for q, t, b in tiles:
                    dve.wait_ge(sem["qk_ready"], t + 1)
                    dve.wait_ge(sem["dec_masked"], t + 1)
                    dve.tensor_tensor(attnT[:, q, :], qmat[:, q, :], ps[:, b + 2, :], ALU.mult).then_inc(sem["attn_done"], 1)
                for q, t, b in tiles:
                    dve.wait_ge(sem["kT_ready"], t + 1)
                    dve.wait_ge(sem["beta_exp"], 1)
                    dve.wait_ge(sem["decay_tok"], 2)
                    if pair:
                        dve.wait_ge(sem["ws_ready"], 3)
                    dve.tensor_tensor(heads(kbe[:, q, :]), heads(ps[:, b + 3, :]), per_head(BEG, t), ALU.mult).then_inc(sem["kbe_done"], 1)
                    dve.tensor_tensor(heads(kdec[:, q, :]), heads(ps[:, b + 3, :]), per_head(DECT, t), ALU.mult).then_inc(sem["kdec_done"], 1)
                for q, t, b in tiles:
                    dve.wait_ge(sem["vT_ready"], t + 1)
                    dve.tensor_tensor(heads(v[:, t, :]), heads(ps[:, b, :]), per_head(BETA, t), ALU.mult).then_inc(sem["vbeta_done"], 1)
                for q, t, b in tiles:
                    dve.wait_ge(sem["level_made"], pair * 12 + q + 1)
                    dve.wait_ge(sem["qdec_done"], t + 1)
                    dve.tensor_tensor(heads(xmat[:, q, :]), over_heads(ident[:]), heads(cmat[:, q, :]), ALU.subtract).then_inc(sem["x_mat"], 1)
                    dve.wait_ge(sem["level_turned"], t + 1)
                    dve.tensor_tensor(heads(ymat[:, q, :]), over_heads(ident[:]), heads(ps[:, b + 1, :]), ALU.subtract).then_inc(sem["y_mat"], 1)
                for l in range(1, LEVELS):
                    for q, t, b in tiles:
                        dve.wait_ge(sem["dy_ready"], (pair * 5 + l - 1) * 2 + q + 1)
                        dve.wait_ge(sem["y_mat"], (pair * 6 + l - 1) * 2 + q + 1)
                        dve.tensor_tensor(ymat[:, q, :], ymat[:, q, :], ps[:, b + 2, :], ALU.subtract).then_inc(sem["y_mat"], 1)
                        if l < LEVELS - 1:
                            dve.wait_ge(sem["dx_ready"], (pair * 4 + l - 1) * 2 + q + 1)
                            dve.wait_ge(sem["x_mat"], (pair * 5 + l - 1) * 2 + q + 1)
                            dve.tensor_tensor(xmat[:, q, :], xmat[:, q, :], ps[:, b + 3, :], ALU.subtract).then_inc(sem["x_mat"], 1)
                for q, t, b in tiles:
                    dve.wait_ge(sem["u_ready"], t + 1)
                    dve.tensor_copy(v[:, t, :], ps[:, b + 1, :]).then_inc(sem["u_done"], 1)
                for q, t, b in tiles:
                    for hf in range(2):
                        c = 2 * t + hf
                        r = slice(hf * C, (hf + 1) * C)
                        dve.wait_ge(sem["u_done"], t + 1)
                        if t >= 2:
                            dve.wait_ge(sem["o_ready"], 2 * (t - 2) + hf + 1)
                        if c == 0:
                            dve.tensor_copy(vnew[r, q, :], v[r, t, :]).then_inc(sem["vnew_done"], 1)
                        else:
                            dve.wait_ge(sem["ws_ready"], c)
                            dve.tensor_tensor(vnew[r, q, :], v[r, t, :], ps[r, b + 2, :], ALU.subtract).then_inc(sem["vnew_done"], 1)
                        if c == 2 * NT - 1:
                            break
                        dve.wait_ge(sem["kv_ready"], c + 1)
                        if c == 0:
                            dve.tensor_copy(state[:], ps[:, b, :]).then_inc(sem["s_done"], 1)
                        else:
                            dve.wait_ge(sem["s_done"], c)
                            for h in range(H):
                                hs = slice(h * HD, (h + 1) * HD)
                                cd = row(CD0 + hf)[:, t * H + h:t * H + h + 1]
                                ins = dve.scalar_tensor_tensor(state[:, hs], state[:, hs], cd, ps[:, b, hs], ALU.mult, ALU.add)
                            ins.then_inc(sem["s_done"], 1)
            for t in range(NT):
                dve.wait_ge(sem["o_square"], t + 1)
                dve.tensor_reduce(small[:, OSS, t * H:(t + 1) * H], heads(xmat[:, t % 2, :]), AX.X, ALU.add).then_inc(sem["o_sum"], 1)
            dve.wait_ge(sem["o_root"], 1)
            dve.reciprocal(row(OIV), row(ORT)).then_inc(sem["o_inverse"], 1)
            dve.wait_ge(sem["o_inverse"], 1)
            for t in range(NT):
                dve.tensor_tensor(heads(v[:, t, :]), heads(v[:, t, :]), per_head(OIV, t), ALU.mult).then_inc(sem["o_scaled"], 1)
                dve.wait_ge(sem["o_scaled"], t + 1)
                dve.wait_ge(sem["zw_done"], t + 1)
                dve.tensor_tensor(v[:, t, :], v[:, t, :], z[:, t, :], ALU.mult).then_inc(sem["o_gated"], 1)

            def branch_lo(g, t):
                dve.wait_ge(sem["oT_hi"], g * NT + t + 1)
                dst = (slice(None), slice(4 * g, 4 * g + 4), slice(t * P, (t + 1) * P))
                dve.tensor_tensor(oT_lo_t[dst], ps[:, t, :].rearrange("p (k n) -> p k n", k=4), oT_hi_t[dst].bitcast(F32), ALU.subtract).then_inc(sem["oT_lo"], 1)
            for t in range(NT):
                branch_lo(0, t)

            def mb_out(h):
                dve.reciprocal(row(PI, 2)[:, h * NT:(h + 1) * NT], row(PS, 2)[:, h * NT:(h + 1) * NT]).then_inc(sem["p_inverse"], 1)
                dve.wait_ge(sem["p_inverse"], h + 1)
                dve.wait_ge(sem["pv_ready"], h + 1)
                dve.tensor_tensor(omb[:, :, h * MD:(h + 1) * MD], ps[:, 7, 0:NT * MD].rearrange("p (t d) -> p t d", d=MD), row(PI, 2)[:, h * NT:(h + 1) * NT].unsqueeze(2).to_broadcast([P, NT, MD]), ALU.mult).then_inc(sem["mb_done"], 1)

            for u in range(MH * NT):
                h, i = divmod(u, NT)
                w = (i + 1) * P
                dve.wait_ge(sem["s_ready"], u + 1)
                if u >= 2:
                    dve.wait_ge(sem["p_done"], u - 1)
                slope = 2.0 ** (-8.0 * (h + 1) / MH)
                dve.scalar_tensor_tensor(logit[:, u % 2, 0:w], alibi[:, T - w:T], slope, ps[:, 4 + u % 2, 0:w],
                                         ALU.mult, ALU.add).then_inc(sem["s_biased"], 1)
                dve.wait_ge(sem["s_biased"], u + 1)
                dve.tensor_reduce(row(PM, 2)[:, u:u + 1], logit[:, u % 2, 0:w], AX.X, ALU.max, negate=True).then_inc(sem["s_max"], 1)
                if h and i == 1:
                    dve.wait_ge(sem["p_done"], h * NT)
                    mb_out(h - 1)
            dve.wait_ge(sem["p_done"], MH * NT)
            mb_out(MH - 1)
            for t in range(NT):
                branch_lo(1, t)

            for n in range(NK):
                for j in range(3):
                    lo_next()
                b = 4 * (n % 2)
                dve.wait_ge(sem["gate_dn"], n + 1)
                dve.wait_ge(sem["slab_used"], S_MERGE + 3 * n + 3)
                dve.tensor_tensor(prod[:, 0, :], sig[:, n % 2, 0, :], ps[:, b + 2, :], ALU.mult).then_inc(sem["merge_dn"], 1)
                dve.wait_ge(sem["gate_mb"], n + 1)
                dve.tensor_tensor(prod[:, 1, :], sig[:, n % 2, 1, :], ps[:, b + 3, :], ALU.mult).then_inc(sem["merge_mb"], 1)
                dve.wait_ge(sem["merge_mb"], n + 1)
                dve.tensor_tensor(merged[:, n * T:(n + 1) * T], prod[:, 0, :], prod[:, 1, :], ALU.add).then_inc(sem["merge_done"], 1)
                dve.wait_ge(sem["merge_done"], n + 1)
            for k in range(NK + 1):
                if k:
                    lo_next()
                if k < NK:
                    split_act(merged[:, k * T:(k + 1) * T], FINS[1] + k + 1, k % 2)
            boundary(1, 2)
            ffn_stage(1, S_FFN2)
            boundary(2, None)

        @block.tensor
        def _(pe):
            def products(out, pairs, first=True, last=True):
                n = len(pairs)
                for k, (s_hi, s_lo, m_hi, m_lo) in enumerate(pairs):
                    pe.matmul(out, s_hi, m_hi, start=first and k == 0, stop=False)
                    pe.matmul(out, s_hi, m_lo, start=False, stop=False)
                    mm = pe.matmul(out, s_lo, m_hi, start=False, stop=last and k == n - 1)
                return mm

            def kslice(slot, k):
                return w_hi[:, slot, k * P:(k + 1) * P], w_lo[:, slot, k * P:(k + 1) * P]

            def project(bank, slot):
                return products(ps[:, bank, :], [(*kslice(slot, k), hT_hi[:, k, :], hT_lo[:, k, :]) for k in range(NK)])

            def turn(st):
                if st == 0:
                    pe.wait_ge(sem["const_made"], 4)
                for i in range(NT):
                    pe.wait_ge(sem["h_done"], st * NT + i + 1)
                    for hf in range(2):
                        for k in range(4):
                            mm = pe.transpose(ps[:, ybank(i) + hf, k * P:(k + 1) * P],
                                              hnat[:, 0, (4 * hf + k) * P:(4 * hf + k + 1) * P], ident[:])
                        mm.then_inc(sem["h_turned"], 1)
                pe.wait_ge(sem["hT_lo"], 2 * NT * (st + 1))

            def contract(s, slot, k_slot, n, first=False, last=False):
                pe.wait_ge(sem["split_lo"], n)
                pe.wait_ge(sem["slab_lo"], s + 1)
                for i in range(NT):
                    ts = slice(i * P, (i + 1) * P)
                    for hf in range(2):
                        cs = slice(hf * T, (hf + 1) * T)
                        mm = products(ps[:, ybank(i) + hf, :],
                                      [(a_hi[:, k_slot, ts], a_lo[:, k_slot, ts], w_hi[:, slot, cs], w_lo[:, slot, cs])],
                                      first, last)
                    if last and i < NT - 1:
                        mm.then_inc(sem["y_ready"], 1)
                mm.then_inc(sem["slab_used"], 1)

            def ffn_stage(f, s0):
                def tile(i, j, first=False):
                    for q, name in enumerate(("ffn_silu", "ffn_act")):
                        s, slot, _ = slab(s0, 2 * j + q, i)
                        pe.wait_ge(sem["slab_lo"], s + 1)
                        if not first:
                            pe.wait_ge(sem[name], f * NF + 2 * i + j - 1)
                        project(2 * j + q, slot).then_inc(sem["slab_used"], 1)
                for j in range(2):
                    tile(0, j, True)
                with pe.Fori(1, NF // 2) as i:
                    for j in range(2):
                        tile(i, j)
                s1, fin = s0 + 2 * NF, FINS[2 * f]
                pe.wait_ge(sem["ffn_act"], (f + 1) * NF)
                contract(*slab(s1, 0)[:2], 0, fin + 1, first=True)
                with pe.Fori(0, (NF - 2) // 4) as i:
                    for j in range(1, 5):
                        contract(*slab(s1, j, i)[:2], j % 2, fin + j + 4 * i + 1)
                k = NF - 1
                contract(*slab(s1, k)[:2], k % 2, fin + k + 1, last=True)

            def copy_product(out, lhsT, rhs, start=True, stop=True, skip=False):
                return pe.matmul(out, lhsT, rhs, start=start, stop=stop, skip_group_check=skip)

            turn(0)
            pe.wait_ge(sem["const_in"], 16 * N_ROWS)
            pe.transpose(ps[:, 3, 0:48], convw_rows[:], ident[0:48, 0:48]).then_inc(sem["convw_ready"], 1)
            pe.wait_ge(sem["convw_done"], 1)
            ffn_stage(0, 0)
            turn(1)

            pe.wait_ge(sem["ba_lo"], 1)
            for t in range(NT):
                ts = slice(t * P, (t + 1) * P)
                mm = products(ps[:, 4, t * 8:(t + 1) * 8],
                              [(hT_hi[:, k, ts], hT_lo[:, k, ts], wba_hi[:, k, :], wba_lo[:, k, :]) for k in range(NK)])
            mm.then_inc(sem["ba_ready"], 1)

            def sum_squares(j):
                pe.wait_ge(sem["sq_made"], j + 1)
                pe.matmul(ps[0:8, 5, :], one_col[:, j, :], sq[:, j % 2, :], start=j == 0, stop=j == 7).then_inc(sem["sq_summed"], 1)

            for j in range(12):
                s, slot, _ = slab(S_QKV, j)
                pe.wait_ge(sem["slab_lo"], s + 1)
                if j >= 4:
                    pe.wait_ge(sem["conv_done"], j - 3)
                project(j % 4, slot).then_inc(sem["slab_used"], 1)
                if j == 1:
                    pe.wait_ge(sem["const_made"], N_CONST)
                    pe.wait_ge(sem["g_ready"], 1)
                    for n, m in enumerate((upper[:], same[:], half[:, 0, :], half[:, 1, :])):
                        mm = pe.matmul(ps[:, 6, n * 16:(n + 1) * 16], m, row(G), start=True, stop=True)
                    mm.then_inc(sem["sums_ready"], 1)
                if 2 <= j < 10:
                    sum_squares(j - 2)

            for j in range(8):
                s, slot, _ = slab(S_MBQK, j)
                pe.wait_ge(sem["slab_lo"], s + 1)
                if j < 4:
                    pe.wait_ge(sem["conv_done"], 9 + j)
                else:
                    pe.wait_ge(sem["mbqk_done"], j - 3)
                project(j % 4, slot).then_inc(sem["slab_used"], 1)
                if j == 0:
                    pe.wait_ge(sem["qk_scale"], 1)
                    pe.wait_ge(sem["chunk_decay"], 1)
                    pe.wait_ge(sem["last_diff"], 1)
                if j >= 4:
                    pe.wait_ge(sem["qk_done"], j - 3)
                pe.matmul(ps[:, 4 + j % 4, :], ident[0:8, j:j + 1].to_broadcast([8, P]), qk_iv[:], start=True,
                          stop=True).then_inc(sem["qk_rows"], 1)

            for g in range(2):
                for p in range(4):
                    s, slot, _ = slab((S_Z, S_MBV)[g], p)
                    pe.wait_ge(sem["slab_lo"], s + 1)
                    for t in range(NT):
                        if p == 0:
                            pe.wait_ge(sem[("mbqk_done", "qk_done")[g]], 5 + t)
                        ts = slice(t * P, (t + 1) * P)
                        mm = products(ps[:, 4 * g + t, :],
                                      [(hT_hi[:, 2 * p + k, ts], hT_lo[:, 2 * p + k, ts], w_hi[:, slot, k * T:(k + 1) * T],
                                        w_lo[:, slot, k * T:(k + 1) * T]) for k in range(2)], p == 0, p == 3)
                        if p == 3 and t < NT - 1:
                            mm.then_inc(sem["tok_ready"], 1)
                    mm.then_inc(sem["slab_used"], 1)

            def four(out_bank, lhsT, rhs, transpose=False):
                for h in range(H):
                    hs = slice(h * HD, (h + 1) * HD)
                    if transpose:
                        mm = pe.transpose(ps[:, out_bank, hs], lhsT(h, hs), ident[:])
                    else:
                        mm = pe.matmul(ps[:, out_bank, hs], lhsT(h, hs), rhs(h, hs), start=True, stop=True)
                return mm

            for pair in range(2):
                tiles = [(q, 2 * pair + q, 4 - 4 * q, slice((2 * pair + q) * P, (2 * pair + q + 1) * P)) for q in range(2)]
                for q, t, b, ts in tiles:
                    if pair:
                        pe.wait_ge(sem["s_done"], 4)
                        pe.wait_ge(sem["wt_done"], 2)
                    elif q == 0:
                        pe.wait_ge(sem["tok_done"], 8)
                    four(b, lambda h, hs: row(G)[:, t * H + h:t * H + h + 1].to_broadcast([P, P]), lambda h, hs: upper[:]).then_inc(sem["gb_ready"], 1)
                for q, t, b, ts in tiles:
                    pe.wait_ge(sem["qk_done"], 8)
                    if pair:
                        pe.wait_ge(sem["u_done"], 2)
                    four(b + 1, lambda h, hs: qkT[:, H + h, ts], lambda h, hs: qkT[:, H + h, ts]).then_inc(sem["kk_ready"], 1)
                for q, t, b, ts in tiles:
                    if pair:
                        pe.wait_ge(sem["vnew_done"], 4)
                    four(b + 2, lambda h, hs: qkT[:, H + h, ts], lambda h, hs: qkT[:, h, ts]).then_inc(sem["qk_ready"], 1)
                for q, t, b, ts in tiles:
                    if pair:
                        pe.wait_ge(sem["o_done"], q + 1)
                    four(b + 3, lambda h, hs: qkT[:, H + h, ts], None, True).then_inc(sem["kT_ready"], 1)
                for q, t, b, ts in tiles:
                    pe.wait_ge(sem["eg_made"], t + 1)
                    pe.wait_ge(sem["qkv_done"], 12)
                    four(b, lambda h, hs: vT[:, h, ts], None, True).then_inc(sem["vT_ready"], 1)
                for q, t, b, ts in tiles:
                    pe.wait_ge(sem["level_made"], pair * 12 + q + 1)
                    four(b + 1, lambda h, hs: cmat[:, q, hs], None, True).then_inc(sem["level_turned"], 1)
                for l in range(1, LEVELS):
                    for q, t, b, ts in tiles:
                        pe.wait_ge(sem["level_made"], pair * 12 + l * 2 + q + 1)
                        pe.wait_ge(sem["y_mat"], (pair * 6 + l - 1) * 2 + q + 1)
                        four(b + 1, lambda h, hs: cmat[:, q, hs], lambda h, hs: ymat[:, q, hs]).then_inc(sem["q_ready"], 1)
                    for q, t, b, ts in tiles:
                        pe.wait_ge(sem["q_copied"], (pair * 5 + l - 1) * 2 + q + 1)
                        pe.wait_ge(sem["x_mat"], (pair * 5 + l - 1) * 2 + q + 1)
                        if l == 1:
                            pe.wait_ge(sem["attn_done"], t + 1)
                            pe.wait_ge(sem["kdec_done"], t + 1)
                        four(b + 2, lambda h, hs: xmat[:, q, hs], lambda h, hs: qmat[:, q, hs]).then_inc(sem["dy_ready"], 1)
                        if l < LEVELS - 1:
                            four(b + 3, lambda h, hs: qmat[:, q, hs], lambda h, hs: xmat[:, q, hs]).then_inc(sem["dx_ready"], 1)
                for q, t, b, ts in tiles:
                    pe.wait_ge(sem["y_mat"], pair * 12 + 10 + q + 1)
                    pe.wait_ge(sem["kbe_done"], t + 1)
                    pe.wait_ge(sem["vbeta_done"], t + 1)
                    four(b, lambda h, hs: kbe[:, q, hs], lambda h, hs: ymat[:, q, hs]).then_inc(sem["wt_ready"], 1)
                    four(b + 1, lambda h, hs: ymat[:, q, hs], lambda h, hs: v[:, t, hs]).then_inc(sem["u_ready"], 1)
                for q, t, b, ts in tiles:
                    for hf in range(2):
                        c = 2 * t + hf
                        r = slice(hf * C, (hf + 1) * C)
                        cols = [slice(h * HD + hf * C, h * HD + (hf + 1) * C) for h in range(H)]
                        pe.wait_ge(sem["wt_done"], t + 1)
                        if c:
                            pe.wait_ge(sem["s_done"], c)
                            if hf == 0:
                                pe.wait_ge(sem["y_mat"], pair * 12 + 10 + q + 1)
                            for h in range(H):
                                hs = slice(h * HD, (h + 1) * HD)
                                mm = pe.matmul(ps[r, b + 2, hs], kbe[:, q, cols[h]], state[:, hs], start=True, stop=True)
                            mm.then_inc(sem["ws_ready"], 1)
                            for h in range(H):
                                hs = slice(h * HD, (h + 1) * HD)
                                pe.matmul(ps[r, b + 3, hs], qdec[:, q, cols[h]], state[:, hs], start=h == 0, stop=False,
                                          skip_group_check=True)
                        pe.wait_ge(sem["vnew_done"], c + 1)
                        if c < 2 * NT - 1:
                            for h in range(H):
                                hs = slice(h * HD, (h + 1) * HD)
                                mm = pe.matmul(ps[:, b, hs], kdec[r, q, hs], vnew[r, q, hs], start=True, stop=True)
                            mm.then_inc(sem["kv_ready"], 1)
                        for h in range(H):
                            hs = slice(h * HD, (h + 1) * HD)
                            mm = pe.matmul(ps[r, b + 3, hs], attnT[r, q, cols[h]], vnew[r, q, hs], start=c == 0, stop=True,
                                           skip_group_check=True)
                        mm.then_inc(sem["o_ready"], 1)

            def branch_turn(g, src):
                for t in range(NT):
                    if g == 0:
                        pe.wait_ge(sem["o_gated"], t + 1)
                    four(t, lambda h, hs: src[:, t, hs], None, True).then_inc(sem["oT_ready"], 1)

            branch_turn(0, v)

            def scores(u):
                h, i = divmod(u, NT)
                r = slice((h % 2) * MD, (h % 2 + 1) * MD)
                if u >= 2:
                    pe.wait_ge(sem["s_biased"], u - 1)
                pe.matmul(ps[:, 4 + u % 2, 0:(i + 1) * P], mbqk[r, h // 2, i * P:(i + 1) * P],
                          mbqk[r, 4 + h // 2, 0:(i + 1) * P], start=True, stop=True).then_inc(sem["s_ready"], 1)

            pe.wait_ge(sem["oT_lo"], NT)
            scores(0)
            for u in range(MH * NT):
                h, i = divmod(u, NT)
                if u + 1 < MH * NT:
                    scores(u + 1)
                pe.wait_ge(sem["p_done"], u + 1)
                if u:
                    pe.wait_ge(sem["pT_copied"], u)
                for j in range(i + 1):
                    mm = pe.transpose(ps[:, 6, j * P:(j + 1) * P], prob[:, u % 2, j * P:(j + 1) * P], ident[:])
                mm.then_inc(sem["pT_ready"], 1)
                pe.wait_ge(sem["pT_copied"], u + 1)
                if i == 0 and h:
                    pe.wait_ge(sem["mb_done"], h)
                for j in range(i + 1):
                    mm = pe.matmul(ps[:, 7, i * MD:(i + 1) * MD], probT[:, u % 2, j * P:(j + 1) * P],
                                   mbv[:, j, h * MD:(h + 1) * MD], start=j == 0, stop=j == i)
                if i == NT - 1:
                    mm.then_inc(sem["pv_ready"], 1)
            pe.wait_ge(sem["mb_done"], MH)
            branch_turn(1, omb)
            pe.wait_ge(sem["oT_lo"], 2 * NT)

            for n in range(NK):
                b = 4 * (n % 2)
                for j in range(3):
                    s, slot, _ = slab(S_MERGE, 3 * n + j)
                    pe.wait_ge(sem["slab_lo"], s + 1)
                    if n < 2:
                        pass
                    elif j == 0:
                        pe.wait_ge(sem["gate_dn"], n - 1)
                    elif j == 1:
                        pe.wait_ge(sem["gate_mb"], n - 1)
                    else:
                        pe.wait_ge(sem["merge_mb"], n - 1)
                    if j < 2:
                        mm = project(b + j, slot)
                    else:
                        for g in range(2):
                            mm = products(ps[:, b + 2 + g, :], [(*kslice(slot, 4 * g + k), oT_hi_t[:, 4 * g + k, :], oT_lo_t[:, 4 * g + k, :])
                                                                for k in range(4)])
                    mm.then_inc(sem["slab_used"], 1)
            pe.wait_ge(sem["merge_mb"], NK)
            for k in range(NK):
                contract(*slab(S_OUT, k)[:2], k % 2, FINS[1] + k + 1, k == 0, k == NK - 1)
            turn(2)
            ffn_stage(1, S_FFN2)


N_ROWS = 5
N_CONST = 4 + 3 + 3 + 3 + 1 + 8 + 2 + 1 + 3 * LEVELS + 2


_INS = ["x", "ffn1_pre_w", "ffn1_w_gate", "ffn1_w_up", "ffn1_w_down", "ffn1_post_w", "mix_pre_w", "w_in",
        "dn_conv_w", "dn_a_log", "dn_dt_bias", "dn_norm_w", "w_branch_dn", "w_branch_mb", "w_out", "mix_post_w",
        "ffn2_pre_w", "ffn2_w_gate", "ffn2_w_up", "ffn2_w_down", "ffn2_post_w"]


def build(nc, a, out):
    hybrid_layer(nc, a["x"],
                 [(a["ffn1_w_gate"], a["ffn1_w_up"], a["ffn1_w_down"]), (a["ffn2_w_gate"], a["ffn2_w_up"], a["ffn2_w_down"])],
                 a["w_in"], a["dn_conv_w"], a["dn_a_log"], a["dn_dt_bias"], a["dn_norm_w"],
                 a["w_branch_dn"], a["w_branch_mb"], a["w_out"],
                 [(a["ffn1_pre_w"], a["ffn1_post_w"]), (a["mix_pre_w"], a["mix_post_w"]), (a["ffn2_pre_w"], a["ffn2_post_w"])],
                 out)


def kernel(**inputs):
    import numpy as _np
    import concourse.bacc as _bacc
    from concourse import mybir as _mybir
    from concourse.bass_utils import run_bass_kernel_spmd as _run

    nc = _bacc.Bacc("TRN2", target_bir_lowering=False, num_devices=1)
    arrays, args = {}, {}
    for name in _INS:
        arr = _np.ascontiguousarray(inputs[name])
        arrays[f"in_{name}_dram"] = arr
        args[name] = nc.dram_tensor(f"in_{name}_dram", arr.shape, _mybir.dt.from_np(arr.dtype), kind="ExternalInput").ap()[0]
    out = nc.dram_tensor("out_0_dram", (1, T, D), F32, kind="ExternalOutput").ap()[0]
    build(nc, args, out)
    r = _run(nc, [arrays], core_ids=[0])
    return r.results[0]["out_0_dram"]
```

```python
from contextlib import ExitStack

import concourse.bass as bass
from concourse import mybir

F32 = mybir.dt.float32
F32R = mybir.dt.float32r
ALU = mybir.AluOpType
ACT = mybir.ActivationFunctionType
AX = mybir.AxisListType

P = 128
T, D, FF = 512, 1024, 2816
NT, NK, NF = T // P, D // P, FF // P
H, HD = 4, 128
C = 64
MH, MD = 8, 64
EPS = 1e-6
DNW, MBW = H * HD, MH * MD
COL_Z = 3 * DNW
COL_BA = COL_Z + DNW
COL_MBQ = COL_BA + 2 * H
COL_MBV = COL_MBQ + 2 * MBW
COL_GDN = COL_MBV + MBW
COL_GMB = COL_GDN + D

RING = 4
AHEAD = 2
N_FFN = 3 * NF
S_QKV = N_FFN
S_SIDE = S_QKV + 12
S_GATE = S_SIDE + 16
S_BRANCH = S_GATE + 16
S_OUT = S_BRANCH + NK
S_FFN2 = S_OUT + NK
N_SLABS = S_FFN2 + N_FFN
SIDE = ([("qk", j, COL_MBQ + j * P) for j in range(4)] + [("z", j, COL_Z + j * P) for j in range(4)]
        + [("qk", j, COL_MBQ + j * P) for j in range(4, 8)] + [("v", j, COL_MBV + j * P) for j in range(4)])
N_UNITS = MH * NT
STEPS = [[] for _ in range(32)]
_m = 0
for _f in range(4, 29):
    for _ in range(2 if 10 <= _f <= 27 and _f % 2 == 0 else 1):
        if _m < N_UNITS + 2:
            STEPS[_f].append(_m)
            _m += 1
assert _m == N_UNITS + 2
DN_CLOSE = {19 + t: t for t in range(4)}
MB_CLOSE = {29: (0, 1), 30: (2,), 31: (3,)}
LEVELS = 6
FINS = (0, NF, NF + NK)
KB = 1024

SEMAPHORES = """slab_hi slab_lo slab_used const_in const_made ffn_silu ffn_act
split_hi split_lo y_ready y_square y_root y_inverse y_scaled x_done x_square x_root x_inverse h_done
h_turned hT_hi hT_lo wpost_in wpre_in x_kept x_back ba_hi ba_lo ba_ready convw_ready convw_done
exp_b exp_a beta_sum beta_ready dt_added dt_neg dt_min exp_t ln_t relu_t g_sum g_ready a_exp a_neg sums_ready
gc_ready last_diff decay_tok beta_exp chunk_decay
conv_start conv_tap conv_done qkv_done sq_made sq_summed qk_root qk_inverse qk_scale qk_rows qk_done
vT_ready v_done z_done mbqk_done mbvT_done mbv_turned mbv_done zeros_made
gb_ready diff_made eg_made qdec_done neg_made pos_made decay_row decay_col kk_ready qk_ready amat_done
dec_masked attn_done kT_ready kbe_done kdec_done
level_made turned_0 x0_made xc_made y_mat q_ready q_copied q_blocks dy_ready dx_ready x_mat x_blocks
wt_ready wt_done u_ready u_done
ws_ready vnew_done kv_ready s_done o_ready o_done o_square o_sum o_root o_inverse o_scaled
oT_ready o_gated oT_hi oT_lo
s_ready s_biased s_max p_done pT_ready pT_copied pv_ready p_inverse mb_done gate_kept
gate_dn gate_mb merge_dn merge_mb merge_done out_done""".split()


def hybrid_layer(nc, x_in, ffn, w_in, conv_w, a_log, dt_bias, dn_norm_w, w_dn, w_mb, w_out, norms, out):
    ctx = ExitStack()
    with ctx:
        sem = {n: ctx.enter_context(nc.semaphore(n)) for n in SEMAPHORES}
        raw_in = [ctx.enter_context(nc.semaphore(f"raw_in{i}")) for i in range(RING)]
        x_in_sem = [ctx.enter_context(nc.semaphore(f"x_in{i}")) for i in range(NT)]
        base = nc.sbuf_base + (-nc.sbuf_base) % 32

        def at(name, kb, shape, dt=F32):
            return nc.alloc_sbuf_tensor_at(name, shape, dt, offset=base + int(kb * KB))

        raw = at("raw", 0, [P, RING, D])
        w_hi = at("w_hi", 16, [P, RING, D], F32R)
        w_lo = at("w_lo", 32, [P, RING, D], F32R)
        hT_hi = at("hT_hi", 48, [P, NK, T], F32R)
        hT_lo = at("hT_lo", 64, [P, NK, T], F32R)
        wpost = at("wpost", 88, [P, D])
        wpre = at("wpre", 92, [P, D])
        ident = at("ident", 96, [P, P])
        upper = at("upper", 96.5, [P, P])
        same = at("same", 97, [P, P])
        half = at("half", 97.5, [P, 2, P])
        level = at("level", 98.5, [P, LEVELS, P])
        alibi = at("alibi", 101.5, [P, T])
        one_col = at("one_col", 103.5, [P, 8, 8])
        ident_c = at("ident_c", 103.75, [P, C])
        normw = at("normw", 104, [P, 1])
        convw = at("convw", 104.25, [P, 4, 12])
        convw_rows = at("convw_rows", 182, [4 * 12, P])
        eps1 = at("eps1", 104.5, [P, 1])
        eps4 = at("eps4", 104.5625, [P, 1])
        y_ss = at("y_ss", 104.625, [P, 3, NT])
        y_rt = at("y_rt", 104.6875, [P, 3, NT])
        y_iv = at("y_iv", 104.75, [P, 3, NT])
        x_ss = at("x_ss", 104.8125, [P, 3, NT])
        x_rt = at("x_rt", 104.875, [P, 3, NT])
        x_iv = at("x_iv", 104.9375, [P, 3, NT])
        dtb = at("dtb", 105, [P, H])
        alog = at("alog", 105.03125, [P, H])
        nega = at("nega", 105.0625, [P, H])
        nega2 = at("nega2", 105.09375, [P, H])
        qscale = at("qscale", 105.125, [8, 1])
        wba_raw = at("wba_raw", 105.25, [P, NK, 8])
        wba_hi = at("wba_hi", 105.5, [P, NK, 8], F32R)
        wba_lo = at("wba_lo", 105.75, [P, NK, 8], F32R)
        small = at("small", 206, [P, 28, NT * H])
        a_hi = at("a_hi", 80, [P, 2, T], F32R)
        a_lo = at("a_lo", 84, [P, 2, T], F32R)
        x = at("x", 106, [P, NT, D])
        hnat = at("hnat", 122, [P, 2, D])
        junk = at("junk", 130, [P, D])
        fact = at("fact", 134, [P, NF * T])
        silu = at("silu", 178, [P, 2, T])
        state = at("state", 80, [P, H * HD])
        vnew = at("vnew", 82, [P, T])
        wq = at("wq", 106, [P, NT, H, 2 * P])
        attnT = at("attnT", 122, [P, NT, T])
        kdec = at("kdec", 130, [P, NT, T])
        qkT = at("qkT", 138, [P, 2 * H, T])
        v = at("v", 154, [P, NT, DNW])
        zT = at("zT", 162, [P, H, T])
        mbqk = at("mbqk", 170, [P, 8, T])
        mbv = at("mbv", 186, [P, NT, MBW])
        cacc = at("cacc", 194, [P, 2, T])
        sq = at("sq", 198, [P, 2, T])
        qk_rt = at("qk_rt", 84, [8, T])
        qk_iv = at("qk_iv", 86, [8, T])
        vT = at("vT", 88, [P, 2, T])
        amat = at("amat", 194, [P, 2 * H, P])
        cmat = at("cmat", 198, [P, 2 * H, P])
        q_bd = at("q_bd", 202, [P, 2 * H, P])
        x_bd = at("x_bd", 84, [P, 2 * H, P])
        x_c = at("x_c", 88, [P, 2 * H, C])
        y_c = at("y_c", 90, [P, 2 * H, C])
        q_c = at("q_c", 92, [P, 2 * H, C])
        mbvT = at("mbvT", 94, [P, T])
        probT = at("probT", 84, [P, 2, T])
        logit = at("logit", 88, [P, 2, T])
        omb = at("omb", 106, [P, NT, MBW])
        gates = [at(f"gate{g}", 138 + 2 * g if g < 8 else 194 + 2 * (g - 8) if g < 14 else 92 + 2 * (g - 14), [P, T])
                 for g in range(16)]
        prod = at("prod", 130, [P, 2, T])
        odn_hi = at("odn_hi", 114, [P, H, T], F32R)
        odn_lo = at("odn_lo", 122, [P, H, T], F32R)
        omb_hi = at("omb_hi", 170, [P, 4, T], F32R)
        omb_lo = at("omb_lo", 178, [P, 4, T], F32R)
        merged = at("merged", 154, [P, NK * T])
        x_keep = nc.dram_tensor("x_keep", (T, D), F32, kind="Internal").ap()

        ps = ctx.enter_context(nc.psum_tensor("ps", [P, 8, T], F32))

        (BETA0, BETA1, BETA, DTA, DTN, DTM, EXPT, LNT, RELU, GSUM, G, GC, LASTD, DECT, EGC, BEG,
         CD0, CD1, OSS, ORT, OIV) = range(21)
        PM, PS, PI = 21, 23, 25

        def row(r, n=1):
            return small[:, r:r + n, :].rearrange("p a b -> p (a b)")

        def row_th(r):
            return small[:, r, :].rearrange("p (t h) -> p t h", h=H)

        def heads(ap):
            return ap.rearrange("p (h d) -> p h d", h=H)

        def per_head(r, t, n=1):
            return small[:, r, t * H:(t + n) * H].unsqueeze(2).to_broadcast([P, n * H, HD])

        def over(ap, n):
            return ap.unsqueeze(1).to_broadcast([P, n, ap.shape[-1]])

        def banks(b, n=2):
            return ps[:, b:b + n, :].rearrange("p b (h d) -> p (b h) d", d=P)

        def ybank(i):
            return (2 * i + 4) % 8

        def wait_y(eng, st, i):
            if i < NT - 1:
                eng.wait_ge(sem["y_ready"], st * (NT - 1) + i + 1)
            else:
                eng.wait_ge(sem["slab_used"], (S_QKV, S_FFN2, N_SLABS)[st])

        def slab(first, j, i=0):
            return first + j + 4 * i, (first + j) % RING, (first + j) // RING + i

        block = ctx.enter_context(nc.Block())

        @block.sync
        def _(sp):
            def load(number, slot, src, dst=None):
                if dst is None:
                    dst, src = (a.rearrange("p (h n) -> p h n", h=2) for a in (raw[:, slot, :], src))
                m = dst.shape[1] // 2
                for hf in range(2):
                    sp.dma_start(dst[:, hf * m:(hf + 1) * m, :], src[:, hf * m:(hf + 1) * m, :]).then_inc(raw_in[slot], 16)

            def free(number, first=False):
                if not first:
                    sp.wait_ge(sem["slab_lo"], number - RING + 1)

            def col_tile(w, col):
                return w[:, bass.ds(col, P)].rearrange("(k p) n -> p k n", p=P)

            def k_view(slot, k=NK):
                return raw[:, slot, :].rearrange("p (k n) -> p k n", k=k)

            def ffn_loads(f, s0):
                wg, wu, wd = ffn[f]

                def pair(i, first=False):
                    for j in range(4):
                        s, slot, _ = slab(s0, j, i)
                        free(s, first)
                        load(s, slot, col_tile((wg, wu)[j % 2], (2 * i + j // 2) * P), k_view(slot))
                pair(0, f == 0)
                with sp.Fori(1, NF // 2) as i:
                    pair(i)

                def down(j, i=0):
                    s, slot, _ = slab(s0 + 2 * NF, j, i)
                    free(s)
                    load(s, slot, wd[bass.ds((j + 4 * i) * P, P), :])
                down(0)
                with sp.Fori(0, (NF - 2) // 4) as i:
                    for j in range(1, 5):
                        down(j, i)
                down(NF - 1)

            for i in range(NT):
                sp.dma_start(x[:, i, :], x_in[i * P:(i + 1) * P, :]).then_inc(x_in_sem[i], 16)
            ffn_loads(0, 0)
            for j in range(12):
                s, slot, _ = slab(S_QKV, j)
                free(s)
                load(s, slot, col_tile(w_in, j * P), k_view(slot))
            cols = [c for _, _, c in SIDE] + [(COL_GDN, COL_GMB)[g % 2] + g // 2 * P for g in range(16)]
            for j, col in enumerate(cols):
                s, slot, _ = slab(S_SIDE, j)
                free(s)
                load(s, slot, col_tile(w_in, col), k_view(slot))
            for n in range(NK):
                s, slot, _ = slab(S_BRANCH, n)
                free(s)
                v2 = raw[:, slot, :].rearrange("p (b k n) -> p b k n", b=2, k=4)
                for b, w in enumerate((w_dn, w_mb)):
                    src = w[:, n * P:(n + 1) * P].rearrange("(k p) n -> p k n", p=P)
                    sp.dma_start(v2[:, b], src).then_inc(raw_in[slot], 16)
            for k in range(NK):
                s, slot, _ = slab(S_OUT, k)
                free(s)
                load(s, slot, w_out[k * P:(k + 1) * P, :])
            ffn_loads(1, S_FFN2)
            for i in range(NT):
                sp.wait_ge(sem["x_done"], 2 * NT + i + 1)
                sp.dma_start(out[i * P:(i + 1) * P, :], x[:, i, :]).then_inc(sem["out_done"], 16)
            sp.wait_ge(sem["out_done"], 16 * NT)

        def split_hi(act, number, slot, use, first=False):
            act.wait_ge(raw_in[slot], 32 * (use + 1))
            if not first:
                act.wait_ge(sem["slab_used"], number - RING + 1)
            act.activation(w_hi[:, slot, :], raw[:, slot, :], ACT.Copy).then_inc(sem["slab_hi"], 1)

        def split_lo(dve, number, slot, use):
            dve.wait_ge(sem["slab_hi"], number + 1)
            dve.tensor_tensor(w_lo[:, slot, :], raw[:, slot, :], w_hi[:, slot, :].bitcast(F32),
                              ALU.subtract).then_inc(sem["slab_lo"], 1)

        @block.gpsimd
        def _(pool):
            def const(ins):
                const.n += 1
                ins.then_inc(sem["const_made"], 1)
                pool.wait_ge(sem["const_made"], const.n)
            const.n = 0
            const(pool.memset(eps1[:], EPS))
            const(pool.memset(eps4[:], 4 * EPS))
            const(pool.memset(ident[:], 0.0))
            const(pool.affine_select(out=ident[:], in_=ident[:], compare_op=ALU.not_equal, fill=1.0, base=0,
                                     pattern=[[-1, P]], channel_multiplier=1))
            pool.dma_start(wpre[:], norms[0][0].partition_broadcast(P)).then_inc(sem["wpre_in"], 16)
            pool.dma_start(wba_raw[:], w_in[:, COL_BA:COL_BA + 8].rearrange("(k p) n -> p k n", p=P)).then_inc(sem["const_in"], 16)
            pool.dma_start(dtb[:], dt_bias.partition_broadcast(P)).then_inc(sem["const_in"], 16)
            pool.dma_start(alog[:], a_log.partition_broadcast(P)).then_inc(sem["const_in"], 16)
            pool.dma_start(normw[:], dn_norm_w.unsqueeze(1)).then_inc(sem["const_in"], 16)
            pool.dma_start(convw_rows[:], conv_w.rearrange("k (j p) -> (k j) p", p=P)).then_inc(sem["const_in"], 16)
            pool.dma_start(wpost[:], norms[0][1].partition_broadcast(P)).then_inc(sem["wpost_in"], 16)

            const(pool.tensor_tensor(ident_c[:], ident[:, 0:C], ident[:, C:P], ALU.add))
            const(pool.memset(upper[:], 1.0))
            const(pool.affine_select(out=upper[:], in_=upper[:], compare_op=ALU.is_ge, fill=0.0, base=0,
                                     pattern=[[1, P]], channel_multiplier=-1))
            const(pool.memset(upper[0:C, C:P], 0.0))
            const(pool.memset(same[:], 0.0))
            const(pool.memset(same[0:C, 0:C], 1.0))
            const(pool.memset(same[C:P, C:P], 1.0))
            const(pool.memset(half[:], 0.0))
            const(pool.memset(half[0:C, 0, :], 1.0))
            const(pool.memset(half[C:P, 1, :], 1.0))
            const(pool.memset(one_col[:], 0.0))
            for j in range(8):
                const(pool.memset(one_col[:, j, j:j + 1], 1.0))
            const(pool.memset(qscale[:], 1.0))
            const(pool.memset(qscale[0:H, :], float(HD) ** -0.5))
            const(pool.memset(level[:], 0.0))
            for l in range(LEVELS):
                b = 1 << l
                left = level[:, l, :].rearrange("p (n two b) -> p n two b", two=2, b=b)[:, :, 0, :]
                const(pool.memset(left, 1.0))
                const(pool.affine_select(out=left, in_=left, compare_op=ALU.is_ge, fill=0.0, base=-b,
                                         pattern=[[-2 * b, P // (2 * b)], [0, b]], channel_multiplier=1))
                const(pool.affine_select(out=left, in_=left, compare_op=ALU.is_ge, fill=0.0, base=2 * b - 1,
                                         pattern=[[2 * b, P // (2 * b)], [0, b]], channel_multiplier=-1))
            const(pool.iota(alibi[:], pattern=[[1, T]], base=-(T - P), channel_multiplier=-1,
                            allow_small_or_imprecise_dtypes=True))
            const(pool.affine_select(out=alibi[:], in_=alibi[:], compare_op=ALU.is_ge, fill=-1e30,
                                     base=T - P, pattern=[[-1, T]], channel_multiplier=1))
            assert const.n == N_CONST, const.n

            pool.wait_ge(sem["h_done"], NT)
            pool.dma_start(wpre[:], norms[1][0].partition_broadcast(P)).then_inc(sem["wpre_in"], 16)
            pool.wait_ge(sem["h_done"], 2 * NT)
            pool.dma_start(x_keep.rearrange("(t p) d -> p t d", p=P), x[:]).then_inc(sem["x_kept"], 16)
            for j in range(8):
                pool.wait_ge(sem["qkv_done"], j + 1)
                if j >= 2:
                    pool.wait_ge(sem["sq_summed"], j - 1)
                pool.tensor_tensor(sq[:, j % 2, :], qkT[:, j, :], qkT[:, j, :], ALU.mult).then_inc(sem["sq_made"], 1)
            pool.wait_ge(sem["sq_summed"], 8)
            pool.memset(q_bd[:], 0.0).then_inc(sem["zeros_made"], 1)
            for pair in range(2):
                for l in range(LEVELS):
                    pool.wait_ge(sem["amat_done"], pair + 1)
                    if l == 1:
                        pool.wait_ge(sem["turned_0"], pair + 1)
                        pool.wait_ge(sem["x0_made"], pair + 1)
                    elif l > 1:
                        pool.wait_ge(sem["q_ready"], 5 * pair + l - 1)
                    pool.tensor_tensor(cmat[:], amat[:], over(level[:, l, :], 2 * H), ALU.mult).then_inc(sem["level_made"], 1)
            pool.wait_ge(sem["pv_ready"], MH)
            pool.dma_start(wpost[:], norms[1][1].partition_broadcast(P)).then_inc(sem["wpost_in"], 16)
            pool.wait_ge(sem["merge_done"], NK)
            pool.dma_start(wpre[:], norms[2][0].partition_broadcast(P)).then_inc(sem["wpre_in"], 16)
            pool.wait_ge(sem["x_kept"], 16)
            pool.wait_ge(sem["slab_used"], S_OUT)
            pool.dma_start(x[:], x_keep.rearrange("(t p) d -> p t d", p=P)).then_inc(sem["x_back"], 16)
            pool.wait_ge(sem["x_done"], 2 * NT)
            pool.dma_start(wpost[:], norms[2][1].partition_broadcast(P)).then_inc(sem["wpost_in"], 16)

        @block.scalar
        def _(act):
            A = act.activation
            ahead = [0]

            def hi_next(first=False):
                if ahead[0] < N_SLABS:
                    s, slot, use = slab(ahead[0], 0)
                    split_hi(act, s, slot, use, first)
                    ahead[0] += 1

            def post(st, i):
                y = ps[:, ybank(i):ybank(i) + 2, :]
                wait_y(act, st, i)
                if st or i:
                    act.wait_ge(sem["y_square"], st * NT + i)
                act.wait_ge(sem["x_square"], min((st + 1) * NT + max(i - 1, 0), 3 * NT))
                A(junk[:].rearrange("p (a b) -> p a b", a=2), y, ACT.Square, accum_out=y_ss[:, st, i:i + 1]).then_inc(sem["y_square"], 1)
                act.wait_ge(sem["y_square"], st * NT + i + 1)
                k = 1.0 if st == 1 else 4.0
                A(y_rt[:, st, i:i + 1], y_ss[:, st, i:i + 1], ACT.Sqrt, scale=k / D,
                  bias=(eps1 if st == 1 else eps4)[:]).then_inc(sem["y_root"], 1)

            def pre(st, i):
                if st:
                    act.wait_ge(sem["x_done"], (st - 1) * NT + i + 1)
                    act.wait_ge(sem["y_square"], (st - 1) * NT + min(i + 2, NT))
                else:
                    act.wait_ge(x_in_sem[i], 16)
                    if i == 0:
                        act.wait_ge(sem["const_made"], 2)
                if i:
                    act.wait_ge(sem["x_square"], st * NT + i)
                A(junk[:], x[:, i, :], ACT.Square, accum_out=x_ss[:, st, i:i + 1]).then_inc(sem["x_square"], 1)
                act.wait_ge(sem["x_square"], st * NT + i + 1)
                A(x_rt[:, st, i:i + 1], x_ss[:, st, i:i + 1], ACT.Sqrt, scale=1.0 / D, bias=eps1[:]).then_inc(sem["x_root"], 1)

            def turned(st, i):
                for hf in range(2):
                    act.wait_ge(sem["h_turned"], (st * NT + i) * 2 + hf + 1)
                    A(hT_hi[:, 4 * hf:4 * hf + 4, i * P:(i + 1) * P],
                      ps[:, ybank(i) + hf, :].rearrange("p (k n) -> p k n", k=4), ACT.Copy).then_inc(sem["hT_hi"], 1)

            def boundary(post_st, pre_st):
                for i in range(NT + 2):
                    if post_st is not None and i < NT:
                        post(post_st, i)
                    if pre_st is not None and 1 <= i <= NT:
                        pre(pre_st, i - 1)
                    if pre_st is not None and i >= 2:
                        turned(pre_st, i - 2)

            def split_act(src, fin, k, slot, used):
                if used is not None:
                    act.wait_ge(sem["slab_used"], used)
                A(a_hi[:, slot, :], src, ACT.Copy).then_inc(sem["split_hi"], 1)

            def ffn_stage(f, s0):
                def tile(i, j):
                    for q in range(2):
                        s, slot, use = slab(s0, AHEAD + 2 * j + q, i)
                        split_hi(act, s, slot, use, first=isinstance(i, int) and i == 0 and s < RING)
                    act.wait_ge(sem["slab_used"], s0 + 4 * i + 2 * j + 1)
                    if not (isinstance(i, int) and i == 0 and f == 0):
                        act.wait_ge(sem["ffn_act"], f * NF + 2 * i + j - 1)
                    A(silu[:, j, :], ps[:, 2 * j, :], ACT.Silu).then_inc(sem["ffn_silu"], 1)
                for j in range(2):
                    tile(0, j)
                with act.Fori(1, NF // 2) as i:
                    for j in range(2):
                        tile(i, j)
                act.wait_ge(sem["ffn_act"], (f + 1) * NF)
                s1 = s0 + 2 * NF
                split_act(fact[:, 0:T], f, 0, 0, None)

                def step(j, i=0, last=False):
                    s, slot, use = slab(s1, j + AHEAD, i)
                    if not isinstance(s, int) or s < N_SLABS:
                        split_hi(act, s, slot, use)
                    k = j + 4 * i
                    A_src = fact[:, bass.ds((k + 1) * T, T)]
                    split_act(A_src, f, k + 1, (j + 1) % 2, s1 + k)
                step(0)
                with act.Fori(0, (NF - 2) // 4 - 1) as i:
                    for j in range(1, 5):
                        step(j, i)
                for k in range(NF - 5, NF - 1):
                    step(k)
                ahead[0] = s1 + NF + AHEAD - 1
                hi_next()

            hi_next(True)
            hi_next(True)
            boundary(None, 0)
            act.wait_ge(sem["const_in"], 16 * N_ROWS)
            A(wba_hi[:], wba_raw[:], ACT.Copy).then_inc(sem["ba_hi"], 1)
            A(nega[:], alog[:], ACT.Exp).then_inc(sem["a_exp"], 1)
            ffn_stage(0, 0)
            boundary(0, 1)

            ab = ps[:, 4, 0:NT * 8].rearrange("p (t c) -> p t c", c=8)
            act.wait_ge(sem["ba_ready"], 1)
            A(row_th(BETA0), ab[:, :, 0:H], ACT.Exp, scale=-1.0).then_inc(sem["exp_b"], 1)
            act.wait_ge(sem["dt_min"], 1)
            A(row(EXPT), row(DTM), ACT.Exp).then_inc(sem["exp_t"], 1)
            act.wait_ge(sem["exp_t"], 1)
            A(row(LNT), row(EXPT), ACT.Ln, bias=1.0).then_inc(sem["ln_t"], 1)

            def finish_qkv(j):
                act.wait_ge(sem["conv_done"], j + 1)
                if j >= 10:
                    act.wait_ge(sem["vT_ready"], j - 9)
                dst = qkT[:, j, :] if j < 8 else vT[:, j % 2, :]
                A(dst, cacc[:, j % 2, :], ACT.Silu).then_inc(sem["qkv_done"], 1)

            for j in range(12):
                hi_next()
                if j:
                    finish_qkv(j - 1)
                act.wait_ge(sem["slab_used"], S_QKV + j + 1)
                if j >= 2:
                    act.wait_ge(sem["qkv_done"], j - 1)
                A(cacc[:, j % 2, :], ps[:, j % 2, :], ACT.Copy, scale=convw[:, 3, j:j + 1]).then_inc(sem["conv_start"], 1)
                if j == 9:
                    act.wait_ge(sem["sq_summed"], 8)
                    A(qk_rt[:], ps[0:8, 5, :], ACT.Sqrt, bias=eps1[0:8, :]).then_inc(sem["qk_root"], 1)
            finish_qkv(11)
            act.wait_ge(sem["beta_ready"], 1)
            act.wait_ge(sem["gc_ready"], 1)
            A(row(EGC), row(GC), ACT.Exp).then_inc(sem["decay_tok"], 1)
            act.wait_ge(sem["last_diff"], 1)
            A(row(DECT), row(LASTD), ACT.Exp).then_inc(sem["decay_tok"], 1)
            A(row(CD0, 2), ps[:, 4, 96:128], ACT.Exp).then_inc(sem["chunk_decay"], 1)

            def side_post(n):
                kind, j, _ = SIDE[n]
                act.wait_ge(sem["slab_used"], S_SIDE + n + 1)
                y = ps[:, n % 2, :]
                if kind == "qk":
                    A(mbqk[:, j, :], y, ACT.Copy, scale=(float(MD) ** -0.5 if j < 4 else 1.0)).then_inc(sem["mbqk_done"], 1)
                elif kind == "z":
                    A(zT[:, j, :], y, ACT.Silu).then_inc(sem["z_done"], 1)
                else:
                    if j:
                        act.wait_ge(sem["mbv_turned"], j)
                    A(mbvT[:], y, ACT.Copy).then_inc(sem["mbvT_done"], 1)

            def side(f):
                if f % 2 == 0:
                    hi_next()
                elif f > 2:
                    side_post(f // 2 - 1)

            side(0)
            side(1)
            for pair in range(2):
                f = 2 + 15 * pair
                pt = slice(2 * pair, 2 * pair + 2)
                side(f)
                act.wait_ge(sem["diff_made"], pair + 1)
                act.wait_ge(sem["x_kept"], 16)
                A(wq[:, pt, :, C:C + P], ps[:, 2:4, :].rearrange("p q (h d) -> p q h d", h=H), ACT.Exp).then_inc(sem["eg_made"], 1)
                act.wait_ge(sem["neg_made"], pair + 1)
                A(cmat[:], cmat[:], ACT.Exp).then_inc(sem["decay_row"], 1)
                act.wait_ge(sem["pos_made"], pair + 1)
                A(attnT[:, pt, :], attnT[:, pt, :], ACT.Exp).then_inc(sem["decay_col"], 1)
                side(f + 1)
                side(f + 2)
                for l in range(1, LEVELS):
                    n = 5 * pair + l
                    side(f + 1 + 2 * l)
                    act.wait_ge(sem["q_ready"], n)
                    if n > 1:
                        act.wait_ge(sem["dy_ready"], n - 1)
                        act.wait_ge(sem["dx_ready"], 4 * pair + min(l - 1, 4))
                    A(q_c[:], ps[:, 4, :].rearrange("p (e d) -> p e d", d=C), ACT.Copy).then_inc(sem["q_copied"], 1)
                    if l < LEVELS - 1:
                        act.wait_ge(sem["zeros_made"], 1)
                        if n > 1:
                            act.wait_ge(sem["q_blocks"], 2 * (4 * pair + l - 1))
                        for hf in range(2):
                            r = slice(hf * C, (hf + 1) * C)
                            A(q_bd[r, :, r], ps[r, 4, :].rearrange("p (e d) -> p e d", d=C), ACT.Copy).then_inc(sem["q_blocks"], 1)
                    side(f + 2 + 2 * l)
                side(f + 13)
                side(f + 14)
                for q in range(2):
                    t = 2 * pair + q
                    act.wait_ge(sem["wt_ready"], t + 1)
                    dst = wq[:, t, :, :].rearrange("p h (c d) -> p h c d", d=C)[:, :, 0:4:3, :]
                    A(dst, ps[:, 2 + q, :].rearrange("p (h c d) -> p h c d", h=H, c=2), ACT.Copy).then_inc(sem["wt_done"], 1)
            side_post(15)

            def gate_post(g):
                act.wait_ge(sem["slab_used"], S_GATE + g + 1)
                A(gates[g][:], ps[:, g % 2, :], ACT.Copy).then_inc(sem["gate_kept"], 1)

            for f in range(32):
                if f % 2 == 0:
                    hi_next()
                elif f > 2:
                    gate_post(f // 2 - 1)
                if f < 16 and f % 2 == 1:
                    c = f // 2
                    r, ro = slice(c % 2 * C, (c % 2 + 1) * C), slice((1 - c % 2) * C, (2 - c % 2) * C)
                    act.wait_ge(sem["o_ready"], c + 1)
                    A(v[r, c // 2, :], ps[ro, 2 + c % 2, :], ACT.Copy).then_inc(sem["o_done"], 1)
                for m in STEPS[f]:
                    if m < N_UNITS:
                        i = m % NT
                        w = (i + 1) * P
                        act.wait_ge(sem["s_max"], m + 1)
                        A(logit[:, m % 2, 0:w], logit[:, m % 2, 0:w], ACT.Exp, bias=row(PM, 2)[:, m:m + 1],
                          accum_out=row(PS, 2)[:, m:m + 1]).then_inc(sem["p_done"], 1)
                    if 1 <= m <= N_UNITS:
                        w = ((m - 1) % NT + 1) * P
                        act.wait_ge(sem["pT_ready"], m)
                        A(probT[:, (m - 1) % 2, 0:w], ps[:, 7, 0:w], ACT.Copy).then_inc(sem["pT_copied"], 1)
                if f == 17:
                    for t in range(NT):
                        if t >= 2:
                            act.wait_ge(sem["o_sum"], t - 1)
                        act.wait_ge(sem["o_done"], 2 * t + 2)
                        A(prod[:, t % 2, :], v[:, t, :], ACT.Square).then_inc(sem["o_square"], 1)
                    act.wait_ge(sem["o_sum"], NT)
                    A(row(ORT), row(OSS), ACT.Sqrt, scale=1.0 / HD, bias=eps1[:]).then_inc(sem["o_root"], 1)
                if f in DN_CLOSE:
                    t = DN_CLOSE[f]
                    act.wait_ge(sem["o_gated"], t + 1)
                    A(odn_hi[:, :, t * P:(t + 1) * P], prod[:, t % 2, :].rearrange("p (k n) -> p k n", k=4),
                      ACT.Copy).then_inc(sem["oT_hi"], 1)
                for t in MB_CLOSE.get(f, ()):
                    act.wait_ge(sem["oT_ready"], NT + t + 1)
                    A(omb_hi[:, :, t * P:(t + 1) * P], ps[:, 2 + t, :].rearrange("p (k n) -> p k n", k=4),
                      ACT.Copy).then_inc(sem["oT_hi"], 1)
            gate_post(15)

            for n in range(NK):
                hi_next()
                for g, name in ((2 * n, "gate_dn"), (2 * n + 1, "gate_mb")):
                    act.wait_ge(sem["gate_kept"], g + 1)
                    A(gates[g][:], gates[g][:], ACT.Sigmoid).then_inc(sem[name], 1)
            for k in range(NK + 1):
                if k:
                    hi_next()
                if k < NK:
                    act.wait_ge(sem["merge_done"], k + 1)
                    split_act(merged[:, k * T:(k + 1) * T], 1, k, k % 2, S_OUT + k - 1 if k else None)
            boundary(1, 2)
            ffn_stage(1, S_FFN2)
            boundary(2, None)

        @block.vector
        def _(dve):
            ahead = [0]

            def lo_next():
                if ahead[0] < N_SLABS:
                    split_lo(dve, *slab(ahead[0], 0))
                    ahead[0] += 1

            def post(st, i):
                y = ps[:, ybank(i):ybank(i) + 2, :]
                dve.wait_ge(sem["y_root"], st * NT + i + 1)
                dve.reciprocal(y_iv[:, st, i:i + 1], y_rt[:, st, i:i + 1]).then_inc(sem["y_inverse"], 1)
                dve.wait_ge(sem["y_inverse"], st * NT + i + 1)
                dve.wait_ge(sem["wpost_in"], 16 * (st + 1))
                if st or i:
                    dve.wait_ge(sem["x_done"], st * NT + i)
                if i == 0 and st == 1:
                    dve.wait_ge(sem["x_back"], 16)
                dve.scalar_tensor_tensor(hnat[:, 1, :].rearrange("p (a b) -> p a b", a=2), y, y_iv[:, st, i:i + 1],
                                         wpost[:].rearrange("p (a b) -> p a b", a=2), ALU.mult, ALU.mult).then_inc(sem["y_scaled"], 1)
                dve.wait_ge(sem["y_scaled"], st * NT + i + 1)
                dve.tensor_tensor(x[:, i, :], x[:, i, :], hnat[:, 1, :], ALU.add).then_inc(sem["x_done"], 1)

            def pre(st, i):
                dve.wait_ge(sem["x_root"], st * NT + i + 1)
                dve.reciprocal(x_iv[:, st, i:i + 1], x_rt[:, st, i:i + 1]).then_inc(sem["x_inverse"], 1)
                dve.wait_ge(sem["x_inverse"], st * NT + i + 1)
                if i == 0:
                    dve.wait_ge(sem["wpre_in"], 16 * (st + 1))
                if i or st:
                    dve.wait_ge(sem["h_turned"], 2 * (st * NT + i))
                dve.scalar_tensor_tensor(hnat[:, 0, :], x[:, i, :], x_iv[:, st, i:i + 1], wpre[:],
                                         ALU.mult, ALU.mult).then_inc(sem["h_done"], 1)

            def turned(st, i):
                for hf in range(2):
                    n = (st * NT + i) * 2 + hf + 1
                    dve.wait_ge(sem["hT_hi"], n)
                    dst = (slice(None), slice(4 * hf, 4 * hf + 4), slice(i * P, (i + 1) * P))
                    dve.tensor_tensor(hT_lo[dst], ps[:, ybank(i) + hf, :].rearrange("p (k n) -> p k n", k=4), hT_hi[dst].bitcast(F32), ALU.subtract).then_inc(sem["hT_lo"], 1)

            def boundary(post_st, pre_st):
                for i in range(NT + 2):
                    if post_st is not None and i < NT:
                        post(post_st, i)
                    if pre_st is not None and 1 <= i <= NT:
                        pre(pre_st, i - 1)
                    if pre_st is not None and i >= 2:
                        turned(pre_st, i - 2)

            def split_act(src, n, slot):
                dve.wait_ge(sem["split_hi"], n)
                dve.tensor_tensor(a_lo[:, slot, :], src, a_hi[:, slot, :].bitcast(F32), ALU.subtract).then_inc(sem["split_lo"], 1)

            def ffn_stage(f, s0):
                def tile(i, j):
                    for q in range(2):
                        split_lo(dve, *slab(s0, AHEAD + 2 * j + q, i))
                    n = f * NF + 2 * i + j + 1
                    dve.wait_ge(sem["ffn_silu"], n)
                    dve.wait_ge(sem["slab_used"], s0 + 4 * i + 2 * j + 2)
                    dve.tensor_tensor(fact[:, bass.ds((2 * i + j) * T, T)], silu[:, j, :], ps[:, 2 * j + 1, :],
                                      ALU.mult).then_inc(sem["ffn_act"], 1)
                for j in range(2):
                    tile(0, j)
                with dve.Fori(1, NF // 2) as i:
                    for j in range(2):
                        tile(i, j)
                dve.wait_ge(sem["ffn_act"], (f + 1) * NF)
                s1 = s0 + 2 * NF
                first = FINS[2 * f]
                split_act(fact[:, 0:T], first + 1, 0)

                def step(j, i=0):
                    s, slot, use = slab(s1, j + AHEAD, i)
                    if not isinstance(s, int) or s < N_SLABS:
                        split_lo(dve, s, slot, use)
                    k = j + 4 * i
                    split_act(fact[:, bass.ds((k + 1) * T, T)], first + k + 2, (j + 1) % 2)
                step(0)
                with dve.Fori(0, (NF - 2) // 4 - 1) as i:
                    for j in range(1, 5):
                        step(j, i)
                for k in range(NF - 5, NF - 1):
                    step(k)
                ahead[0] = s1 + NF + AHEAD - 1
                lo_next()

            lo_next()
            lo_next()
            boundary(None, 0)
            dve.wait_ge(sem["ba_hi"], 1)
            dve.wait_ge(sem["convw_ready"], 1)
            dve.tensor_copy(convw[:].rearrange("p k j -> p (k j)"), ps[:, 3, 0:48]).then_inc(sem["convw_done"], 1)
            dve.tensor_tensor(wba_lo[:], wba_raw[:], wba_hi[:].bitcast(F32), ALU.subtract).then_inc(sem["ba_lo"], 1)
            ffn_stage(0, 0)
            boundary(0, 1)

            ab = ps[:, 4, 0:NT * 8].rearrange("p (t c) -> p t c", c=8)
            dve.wait_ge(sem["exp_b"], 1)
            dve.tensor_tensor(row_th(DTA), ab[:, :, H:2 * H], dtb[:].unsqueeze(1).to_broadcast([P, NT, H]), ALU.add).then_inc(sem["dt_added"], 1)
            dve.tensor_scalar(row(BETA1), row(BETA0), 1.0, None, ALU.add).then_inc(sem["beta_sum"], 1)
            dve.wait_ge(sem["dt_added"], 1)
            dve.tensor_scalar(row(DTN), row(DTA), -1.0, None, ALU.mult).then_inc(sem["dt_neg"], 1)
            dve.wait_ge(sem["dt_neg"], 1)
            dve.tensor_tensor(row(DTM), row(DTA), row(DTN), ALU.min).then_inc(sem["dt_min"], 1)
            dve.wait_ge(sem["beta_sum"], 1)
            dve.reciprocal(row(BETA), row(BETA1)).then_inc(sem["beta_ready"], 1)
            dve.tensor_scalar(row(RELU), row(DTA), 0.0, None, ALU.max).then_inc(sem["relu_t"], 1)
            dve.wait_ge(sem["a_exp"], 1)
            dve.tensor_scalar(nega2[:], nega[:], -1.0, None, ALU.mult).then_inc(sem["a_neg"], 1)
            dve.wait_ge(sem["relu_t"], 1)
            dve.wait_ge(sem["ln_t"], 1)
            dve.tensor_tensor(row(GSUM), row(RELU), row(LNT), ALU.add).then_inc(sem["g_sum"], 1)
            dve.wait_ge(sem["g_sum"], 1)
            dve.wait_ge(sem["a_neg"], 1)
            dve.tensor_tensor(row_th(G), row_th(GSUM), nega2[:].unsqueeze(1).to_broadcast([P, NT, H]), ALU.mult).then_inc(sem["g_ready"], 1)

            def v_heads(h):
                dve.wait_ge(sem["vT_ready"], h + 1)
                dve.wait_ge(sem["beta_ready"], 1)
                dve.tensor_tensor(v[:, :, h * HD:(h + 1) * HD], ps[:, 6 + h % 2, :].rearrange("p (t d) -> p t d", d=HD),
                                  row_th(BETA)[:, :, h:h + 1].to_broadcast([P, NT, HD]), ALU.mult).then_inc(sem["v_done"], 1)

            for j in range(12):
                lo_next()
                dve.wait_ge(sem["conv_start"], j + 1)
                for k in range(1, 4):
                    acc = cacc[:, j % 2, k:T]
                    dve.scalar_tensor_tensor(acc, ps[:, j % 2, 0:T - k], convw[:, 3 - k, j:j + 1], acc, ALU.mult,
                                             ALU.add).then_inc(sem["conv_done" if k == 3 else "conv_tap"], 1)
                    if k < 3:
                        dve.wait_ge(sem["conv_tap"], 2 * j + k)
                if j == 2:
                    dve.wait_ge(sem["sums_ready"], 1)
                    dve.tensor_copy(row(GC), ps[:, 4, 64:80]).then_inc(sem["gc_ready"], 1)
                    dve.wait_ge(sem["gc_ready"], 1)
                    dve.tensor_tensor(row(LASTD), ps[:, 4, 80:96], row(GC), ALU.subtract).then_inc(sem["last_diff"], 1)
                if j == 10:
                    dve.wait_ge(sem["qk_root"], 1)
                    dve.reciprocal(qk_iv[:], qk_rt[:]).then_inc(sem["qk_inverse"], 1)
                if j == 11:
                    dve.wait_ge(sem["qk_inverse"], 1)
                    dve.tensor_scalar(qk_iv[:], qk_iv[:], qscale[:, 0:1], None, ALU.mult).then_inc(sem["qk_scale"], 1)
                    v_heads(0)
                    v_heads(1)

            def side(f):
                if f % 2 == 0:
                    lo_next()
                if f in (29, 31):
                    keep_mbv(f // 2 - 14)

            def keep_mbv(j):
                dve.wait_ge(sem["mbv_turned"], j + 1)
                dve.tensor_copy(mbv[:, :, j * P:(j + 1) * P], ps[:, 7, :].rearrange("p (t d) -> p t d", d=P)).then_inc(sem["mbv_done"], 1)

            def qk_norm(j):
                dve.wait_ge(sem["qk_rows"], j + 1)
                dve.tensor_tensor(qkT[:, j, :], qkT[:, j, :], ps[:, 2 + j % 4, :], ALU.mult).then_inc(sem["qk_done"], 1)

            side(0)
            v_heads(2)
            for j in range(4):
                qk_norm(j)
            side(1)
            v_heads(3)
            for j in range(4, 8):
                qk_norm(j)
            dve.wait_ge(sem["decay_tok"], 1)
            dve.tensor_tensor(row(BEG), row(EGC), row(BETA), ALU.mult).then_inc(sem["beta_exp"], 1)
            for pair in range(2):
                f = 2 + 15 * pair
                pt = slice(2 * pair, 2 * pair + 2)
                side(f)
                dve.wait_ge(sem["gb_ready"], pair + 1)
                if pair:
                    dve.wait_ge(sem["level_made"], LEVELS)
                dve.tensor_tensor(amat[:], banks(2), per_head(GC, 2 * pair, 2), ALU.subtract).then_inc(sem["diff_made"], 1)
                dve.wait_ge(sem["diff_made"], pair + 1)
                if pair:
                    dve.wait_ge(sem["wt_ready"], 2)
                dve.tensor_scalar(cmat[:], amat[:], -1.0, 0.0, ALU.mult, ALU.min).then_inc(sem["neg_made"], 1)
                dve.wait_ge(sem["x_kept"], 16)
                dve.tensor_scalar(attnT[:, pt, :].rearrange("p q (h d) -> p (q h) d", h=H), amat[:], 0.0, None,
                                  ALU.min).then_inc(sem["pos_made"], 1)
                dve.wait_ge(sem["eg_made"], pair + 1)
                dst = wq[:, pt, :, C:C + P]
                for q in range(2):
                    t = 2 * pair + q
                    dve.tensor_tensor(wq[:, t, :, C:C + P], wq[:, t, :, C:C + P], qkT[:, 0:H, t * P:(t + 1) * P],
                                      ALU.mult).then_inc(sem["qdec_done"], 1)
                dve.wait_ge(sem["kk_ready"], pair + 1)
                dve.wait_ge(sem["decay_row"], pair + 1)
                dve.wait_ge(sem["pos_made"], pair + 1)
                for e in range(2 * H):
                    ins = dve.scalar_tensor_tensor(amat[:, e, :], cmat[:, e, :], row(BETA)[:, 2 * pair * H + e:2 * pair * H + e + 1],
                                                   banks(4)[:, e, :], ALU.mult, ALU.mult)
                ins.then_inc(sem["amat_done"], 1)
                side(f + 1)
                dve.wait_ge(sem["decay_col"], pair + 1)
                at_p = attnT[:, pt, :].rearrange("p q (h d) -> p (q h) d", h=H)
                dve.tensor_tensor(at_p, at_p, over(upper[:], 2 * H), ALU.mult).then_inc(sem["dec_masked"], 1)
                dve.wait_ge(sem["level_made"], LEVELS * pair + 1)
                dve.tensor_tensor(x_bd[:], over(ident[:], 2 * H), cmat[:], ALU.subtract).then_inc(sem["x0_made"], 1)
                dve.wait_ge(sem["qk_ready"], pair + 1)
                dve.wait_ge(sem["dec_masked"], pair + 1)
                dve.tensor_tensor(at_p, at_p, banks(6), ALU.mult).then_inc(sem["attn_done"], 1)
                dve.wait_ge(sem["x0_made"], pair + 1)
                for hf in range(2):
                    r = slice(hf * C, (hf + 1) * C)
                    dve.tensor_copy(x_c[r, :, :], x_bd[r, :, r]).then_inc(sem["xc_made"], 1)
                side(f + 2)
                dve.wait_ge(sem["turned_0"], pair + 1)
                dve.tensor_tensor(y_c[:], over(ident_c[:], 2 * H), ps[:, 4, :].rearrange("p (e d) -> p e d", d=C),
                                  ALU.subtract).then_inc(sem["y_mat"], 1)
                for l in range(1, LEVELS):
                    n = 5 * pair + l
                    side(f + 1 + 2 * l)
                    side(f + 2 + 2 * l)
                    dve.wait_ge(sem["dy_ready"], n)
                    dve.wait_ge(sem["y_mat"], 6 * pair + l)
                    dve.tensor_tensor(y_c[:], y_c[:], ps[:, 5, :].rearrange("p (e d) -> p e d", d=C),
                                      ALU.subtract).then_inc(sem["y_mat"], 1)
                    if l < LEVELS - 1:
                        dve.wait_ge(sem["dx_ready"], 4 * pair + l)
                        if l > 1:
                            dve.wait_ge(sem["x_blocks"], 2 * (5 * pair + l - 1))
                        else:
                            dve.wait_ge(sem["xc_made"], 2 * pair + 2)
                        dve.tensor_tensor(x_c[:], x_c[:], ps[:, 6, :].rearrange("p (e d) -> p e d", d=C),
                                          ALU.subtract).then_inc(sem["x_mat"], 1)
                        dve.wait_ge(sem["x_mat"], 4 * pair + l)
                    else:
                        dve.wait_ge(sem["y_mat"], 6 * pair + LEVELS)
                    last = y_c if l == LEVELS - 1 else x_c
                    for hf in range(2):
                        r = slice(hf * C, (hf + 1) * C)
                        dve.tensor_copy(x_bd[r, :, r], last[r, :, :]).then_inc(sem["x_blocks"], 1)
                side(f + 13)
                dve.wait_ge(sem["kT_ready"], pair + 1)
                dve.wait_ge(sem["beta_exp"], 1)
                dve.wait_ge(sem["decay_tok"], 2)
                dve.tensor_tensor(cmat[:], banks(2), per_head(BEG, 2 * pair, 2), ALU.mult).then_inc(sem["kbe_done"], 1)
                dve.tensor_tensor(kdec[:, pt, :].rearrange("p q (h d) -> p (q h) d", h=H), banks(2), per_head(DECT, 2 * pair, 2),
                                  ALU.mult).then_inc(sem["kdec_done"], 1)
                side(f + 14)
                for q in range(2):
                    t = 2 * pair + q
                    dve.wait_ge(sem["u_ready"], t + 1)
                    dve.tensor_copy(v[:, t, :], ps[:, 4 + q, :]).then_inc(sem["u_done"], 1)
            keep_mbv(2)
            keep_mbv(3)

            def mb_out(h):
                dve.wait_ge(sem["p_done"], h * NT + NT)
                dve.reciprocal(row(PI, 2)[:, h * NT:(h + 1) * NT], row(PS, 2)[:, h * NT:(h + 1) * NT]).then_inc(sem["p_inverse"], 1)
                dve.wait_ge(sem["p_inverse"], h + 1)
                dve.wait_ge(sem["pv_ready"], h + 1)
                dve.wait_ge(sem["o_ready"], 4)
                dve.tensor_tensor(omb[:, :, h * MD:(h + 1) * MD], ps[:, 6, 0:NT * MD].rearrange("p (t d) -> p t d", d=MD),
                                  row(PI, 2)[:, h * NT:(h + 1) * NT].unsqueeze(2).to_broadcast([P, NT, MD]),
                                  ALU.mult).then_inc(sem["mb_done"], 1)

            for f in range(32):
                if f % 2 == 0:
                    lo_next()
                if f < 16:
                    c = f // 2
                    t, hf = divmod(c, 2)
                    r = slice(hf * C, (hf + 1) * C)
                if f < 16 and f % 2 == 0:
                    dve.wait_ge(sem["u_done"], t + 1)
                    if c >= 2:
                        dve.wait_ge(sem["o_ready"], c - 1)
                    if c == 0:
                        dve.tensor_copy(vnew[r, :], v[r, t, :]).then_inc(sem["vnew_done"], 1)
                    else:
                        dve.wait_ge(sem["ws_ready"], c)
                        dve.tensor_tensor(vnew[r, :], v[r, t, :], ps[r, 2 + hf, :], ALU.subtract).then_inc(sem["vnew_done"], 1)
                elif f < 15:
                    dve.wait_ge(sem["kv_ready"], c + 1)
                    if c == 0:
                        dve.tensor_copy(state[:], ps[:, 4, :]).then_inc(sem["s_done"], 1)
                    else:
                        dve.wait_ge(sem["s_done"], c)
                        for h in range(H):
                            hs = slice(h * HD, (h + 1) * HD)
                            cd = row(CD0 + hf)[:, t * H + h:t * H + h + 1]
                            ins = dve.scalar_tensor_tensor(state[:, hs], state[:, hs], cd, ps[:, 4, hs], ALU.mult, ALU.add)
                        ins.then_inc(sem["s_done"], 1)
                for m in STEPS[f]:
                    if m < N_UNITS:
                        h, i = divmod(m, NT)
                        w = (i + 1) * P
                        dve.wait_ge(sem["s_ready"], m + 1)
                        if m >= 2:
                            dve.wait_ge(sem["pT_ready"], m - 1)
                        slope = 2.0 ** (-8.0 * (h + 1) / MH)
                        dve.scalar_tensor_tensor(logit[:, m % 2, 0:w], alibi[:, T - w:T], slope, ps[:, 5, 0:w],
                                                 ALU.mult, ALU.add).then_inc(sem["s_biased"], 1)
                        dve.wait_ge(sem["s_biased"], m + 1)
                        dve.tensor_reduce(row(PM, 2)[:, m:m + 1], logit[:, m % 2, 0:w], AX.X, ALU.max, negate=True).then_inc(sem["s_max"], 1)
                    if m >= 5 and m % NT == 1:
                        mb_out(m // NT - 1)
                if f == 17:
                    for t in range(NT):
                        dve.wait_ge(sem["o_square"], t + 1)
                        dve.tensor_reduce(small[:, OSS, t * H:(t + 1) * H], heads(prod[:, t % 2, :]), AX.X, ALU.add).then_inc(sem["o_sum"], 1)
                if f == 18:
                    dve.wait_ge(sem["o_root"], 1)
                    dve.reciprocal(row(OIV), row(ORT)).then_inc(sem["o_inverse"], 1)
                    dve.wait_ge(sem["o_inverse"], 1)
                    for t in range(NT):
                        dve.tensor_tensor(heads(v[:, t, :]), heads(v[:, t, :]), per_head(OIV, t), ALU.mult).then_inc(sem["o_scaled"], 1)
                if f in DN_CLOSE:
                    t = DN_CLOSE[f]
                    dve.wait_ge(sem["oT_ready"], t + 1)
                    dve.wait_ge(sem["z_done"], 4)
                    if t >= 2:
                        dve.wait_ge(sem["oT_lo"], t - 1)
                    else:
                        dve.wait_ge(sem["o_sum"], NT)
                    dve.scalar_tensor_tensor(heads(prod[:, t % 2, :]), heads(ps[:, 2 + t % 2, :]), normw[:, 0:1],
                                             zT[:, :, t * P:(t + 1) * P], ALU.mult, ALU.mult).then_inc(sem["o_gated"], 1)
                    dve.wait_ge(sem["oT_hi"], t + 1)
                    dve.tensor_tensor(odn_lo[:, :, t * P:(t + 1) * P], heads(prod[:, t % 2, :]),
                                      odn_hi[:, :, t * P:(t + 1) * P].bitcast(F32), ALU.subtract).then_inc(sem["oT_lo"], 1)
                for t in MB_CLOSE.get(f, ()):
                    dve.wait_ge(sem["oT_hi"], NT + t + 1)
                    dve.tensor_tensor(omb_lo[:, :, t * P:(t + 1) * P], heads(ps[:, 2 + t, :]),
                                      omb_hi[:, :, t * P:(t + 1) * P].bitcast(F32), ALU.subtract).then_inc(sem["oT_lo"], 1)

            for n in range(NK):
                lo_next()
                b = 2 * (n % 2)
                dve.wait_ge(sem["slab_used"], S_BRANCH + n + 1)
                dve.wait_ge(sem["gate_dn"], n + 1)
                if n:
                    dve.wait_ge(sem["merge_done"], n)
                dve.tensor_tensor(prod[:, 0, :], gates[2 * n][:], ps[:, b, :], ALU.mult).then_inc(sem["merge_dn"], 1)
                dve.wait_ge(sem["gate_mb"], n + 1)
                dve.tensor_tensor(prod[:, 1, :], gates[2 * n + 1][:], ps[:, b + 1, :], ALU.mult).then_inc(sem["merge_mb"], 1)
                dve.wait_ge(sem["merge_mb"], n + 1)
                dve.tensor_tensor(merged[:, n * T:(n + 1) * T], prod[:, 0, :], prod[:, 1, :], ALU.add).then_inc(sem["merge_done"], 1)
            dve.wait_ge(sem["merge_done"], NK)
            for k in range(NK + 1):
                if k:
                    lo_next()
                if k < NK:
                    split_act(merged[:, k * T:(k + 1) * T], FINS[1] + k + 1, k % 2)
            boundary(1, 2)
            ffn_stage(1, S_FFN2)
            boundary(2, None)

        @block.tensor
        def _(pe):
            def products(out, pairs, first=True, last=True):
                n = len(pairs)
                for k, (s_hi, s_lo, m_hi, m_lo) in enumerate(pairs):
                    pe.matmul(out, s_hi, m_hi, start=first and k == 0, stop=False)
                    pe.matmul(out, s_hi, m_lo, start=False, stop=False)
                    mm = pe.matmul(out, s_lo, m_hi, start=False, stop=last and k == n - 1)
                return mm

            def kslice(slot, k):
                return w_hi[:, slot, k * P:(k + 1) * P], w_lo[:, slot, k * P:(k + 1) * P]

            def project(bank, slot):
                return products(ps[:, bank, :], [(*kslice(slot, k), hT_hi[:, k, :], hT_lo[:, k, :]) for k in range(NK)])

            def turn(st):
                if st == 0:
                    pe.wait_ge(sem["const_made"], 4)
                for i in range(NT):
                    pe.wait_ge(sem["h_done"], st * NT + i + 1)
                    for hf in range(2):
                        for k in range(4):
                            mm = pe.transpose(ps[:, ybank(i) + hf, k * P:(k + 1) * P],
                                              hnat[:, 0, (4 * hf + k) * P:(4 * hf + k + 1) * P], ident[:])
                        mm.then_inc(sem["h_turned"], 1)
                pe.wait_ge(sem["hT_lo"], 2 * NT * (st + 1))

            def contract(s, slot, k_slot, n, first=False, last=False):
                pe.wait_ge(sem["split_lo"], n)
                pe.wait_ge(sem["slab_lo"], s + 1)
                for i in range(NT):
                    ts = slice(i * P, (i + 1) * P)
                    for hf in range(2):
                        cs = slice(hf * T, (hf + 1) * T)
                        mm = products(ps[:, ybank(i) + hf, :],
                                      [(a_hi[:, k_slot, ts], a_lo[:, k_slot, ts], w_hi[:, slot, cs], w_lo[:, slot, cs])],
                                      first, last)
                    if last and i < NT - 1:
                        mm.then_inc(sem["y_ready"], 1)
                mm.then_inc(sem["slab_used"], 1)

            def ffn_stage(f, s0):
                def tile(i, j, first=False):
                    for q, name in enumerate(("ffn_silu", "ffn_act")):
                        s, slot, _ = slab(s0, 2 * j + q, i)
                        pe.wait_ge(sem["slab_lo"], s + 1)
                        if not first:
                            pe.wait_ge(sem[name], f * NF + 2 * i + j - 1)
                        project(2 * j + q, slot).then_inc(sem["slab_used"], 1)
                for j in range(2):
                    tile(0, j, True)
                with pe.Fori(1, NF // 2) as i:
                    for j in range(2):
                        tile(i, j)
                s1, fin = s0 + 2 * NF, FINS[2 * f]
                pe.wait_ge(sem["ffn_act"], (f + 1) * NF)
                contract(*slab(s1, 0)[:2], 0, fin + 1, first=True)
                with pe.Fori(0, (NF - 2) // 4) as i:
                    for j in range(1, 5):
                        contract(*slab(s1, j, i)[:2], j % 2, fin + j + 4 * i + 1)
                k = NF - 1
                contract(*slab(s1, k)[:2], k % 2, fin + k + 1, last=True)

            def copy_product(out, lhsT, rhs, start=True, stop=True, skip=False):
                return pe.matmul(out, lhsT, rhs, start=start, stop=stop, skip_group_check=skip)

            turn(0)
            pe.wait_ge(sem["const_in"], 16 * N_ROWS)
            pe.transpose(ps[:, 3, 0:48], convw_rows[:], ident[0:48, 0:48]).then_inc(sem["convw_ready"], 1)
            pe.wait_ge(sem["convw_done"], 1)
            ffn_stage(0, 0)
            turn(1)

            pe.wait_ge(sem["ba_lo"], 1)
            for t in range(NT):
                ts = slice(t * P, (t + 1) * P)
                mm = products(ps[:, 4, t * 8:(t + 1) * 8],
                              [(hT_hi[:, k, ts], hT_lo[:, k, ts], wba_hi[:, k, :], wba_lo[:, k, :]) for k in range(NK)])
            mm.then_inc(sem["ba_ready"], 1)

            def sum_squares(j):
                pe.wait_ge(sem["sq_made"], j + 1)
                pe.matmul(ps[0:8, 5, :], one_col[:, j, :], sq[:, j % 2, :], start=j == 0, stop=j == 7).then_inc(sem["sq_summed"], 1)

            def turn_v(h):
                pe.wait_ge(sem["qkv_done"], 8 + h + 1)
                if h >= 2:
                    pe.wait_ge(sem["v_done"], h - 1)
                for t in range(NT):
                    mm = pe.transpose(ps[:, 6 + h % 2, t * P:(t + 1) * P], vT[:, h % 2, t * P:(t + 1) * P], ident[:])
                mm.then_inc(sem["vT_ready"], 1)

            def half_slab(first, f):
                s, slot, _ = slab(first, f // 2)
                if f % 2 == 0:
                    pe.wait_ge(sem["slab_lo"], s + 1)
                mm = products(ps[:, f // 2 % 2, :], [(*kslice(slot, k), hT_hi[:, k, :], hT_lo[:, k, :])
                                                     for k in range(4 * (f % 2), 4 * (f % 2) + 4)], f % 2 == 0, f % 2 == 1)
                if f % 2:
                    mm.then_inc(sem["slab_used"], 1)

            for j in range(12):
                s, slot, _ = slab(S_QKV, j)
                pe.wait_ge(sem["slab_lo"], s + 1)
                if j >= 2:
                    pe.wait_ge(sem["conv_done"], j - 1)
                project(j % 2, slot).then_inc(sem["slab_used"], 1)
                if j == 1:
                    pe.wait_ge(sem["const_made"], N_CONST)
                    pe.wait_ge(sem["g_ready"], 1)
                    for n, m in enumerate((upper[:], same[:], half[:, 0, :], half[:, 1, :])):
                        mm = pe.matmul(ps[:, 4, 64 + n * 16:80 + n * 16], m, row(G), start=True, stop=True)
                    mm.then_inc(sem["sums_ready"], 1)
                if 2 <= j < 10:
                    sum_squares(j - 2)
                if j >= 10:
                    turn_v(j - 10)

            POSTED = {"qk": "mbqk_done", "z": "z_done", "v": "mbvT_done"}

            def side(f):
                n = f // 2
                if f % 2 == 0:
                    if n < 2:
                        pe.wait_ge(sem["conv_done"], 11 + n)
                    else:
                        kind, j, _ = SIDE[n - 2]
                        pe.wait_ge(sem[POSTED[kind]], j + 1)
                half_slab(S_SIDE, f)
                if f in (28, 30):
                    turn_mbv(f // 2 - 14)

            def turn_mbv(j):
                pe.wait_ge(sem["mbvT_done"], j + 1)
                if j:
                    pe.wait_ge(sem["mbv_done"], j)
                else:
                    pe.wait_ge(sem["attn_done"], 2)
                for t in range(NT):
                    mm = pe.transpose(ps[:, 7, t * P:(t + 1) * P], mbvT[:, t * P:(t + 1) * P], ident[:])
                mm.then_inc(sem["mbv_turned"], 1)

            def four(out_bank, lhsT, rhs, transpose=False):
                for h in range(H):
                    hs = slice(h * HD, (h + 1) * HD)
                    if transpose:
                        mm = pe.transpose(ps[:, out_bank, hs], lhsT(h, hs), ident[:])
                    else:
                        mm = pe.matmul(ps[:, out_bank, hs], lhsT(h, hs), rhs(h, hs), start=True, stop=True)
                return mm

            def columns(bank, lhsT, rhs):
                for e in range(2 * H):
                    mm = pe.matmul(ps[:, bank, e * C:(e + 1) * C], lhsT(e), rhs(e), start=True, stop=True)
                return mm

            side(0)
            turn_v(2)
            pe.wait_ge(sem["qk_scale"], 1)
            pe.wait_ge(sem["chunk_decay"], 1)
            for j in range(4):
                pe.matmul(ps[:, 2 + j, :], ident[0:8, j:j + 1].to_broadcast([8, P]), qk_iv[:], start=True,
                          stop=True).then_inc(sem["qk_rows"], 1)
            side(1)
            turn_v(3)
            for j in range(4, 8):
                pe.wait_ge(sem["qk_done"], j - 3)
                pe.matmul(ps[:, j - 2, :], ident[0:8, j:j + 1].to_broadcast([8, P]), qk_iv[:], start=True,
                          stop=True).then_inc(sem["qk_rows"], 1)
            for pair in range(2):
                f = 2 + 15 * pair
                tiles = [(2 * pair + q, q, slice((2 * pair + q) * P, (2 * pair + q + 1) * P)) for q in range(2)]
                side(f)
                pe.wait_ge(sem["qk_done"], 8)
                if pair:
                    pe.wait_ge(sem["wt_done"], 2)
                    pe.wait_ge(sem["u_done"], 2)
                for t, q, ts in tiles:
                    mm = four(2 + q, lambda h, hs: row(G)[:, t * H + h:t * H + h + 1].to_broadcast([P, P]), lambda h, hs: upper[:])
                mm.then_inc(sem["gb_ready"], 1)
                for t, q, ts in tiles:
                    mm = four(4 + q, lambda h, hs: qkT[:, H + h, ts], lambda h, hs: qkT[:, H + h, ts])
                mm.then_inc(sem["kk_ready"], 1)
                side(f + 1)
                pe.wait_ge(sem["v_done"], 4)
                for t, q, ts in tiles:
                    mm = four(6 + q, lambda h, hs: qkT[:, H + h, ts], lambda h, hs: qkT[:, h, ts])
                mm.then_inc(sem["qk_ready"], 1)
                side(f + 2)
                pe.wait_ge(sem["level_made"], LEVELS * pair + 1)
                columns(4, lambda e: cmat[:, e, :], lambda e: ident_c[:]).then_inc(sem["turned_0"], 1)
                for l in range(1, LEVELS):
                    side(f + 1 + 2 * l)
                    pe.wait_ge(sem["level_made"], LEVELS * pair + l + 1)
                    pe.wait_ge(sem["y_mat"], LEVELS * pair + l)
                    columns(4, lambda e: cmat[:, e, :], lambda e: y_c[:, e, :]).then_inc(sem["q_ready"], 1)
                    side(f + 2 + 2 * l)
                    pe.wait_ge(sem["q_copied"], 5 * pair + l)
                    if l > 1:
                        pe.wait_ge(sem["x_blocks"], 2 * (5 * pair + l - 1))
                    else:
                        pe.wait_ge(sem["xc_made"], 2 * pair + 2)
                        pe.wait_ge(sem["attn_done"], pair + 1)
                    columns(5, lambda e: x_bd[:, e, :], lambda e: q_c[:, e, :]).then_inc(sem["dy_ready"], 1)
                    if l < LEVELS - 1:
                        pe.wait_ge(sem["q_blocks"], 2 * (4 * pair + l))
                        columns(6, lambda e: q_bd[:, e, :], lambda e: x_c[:, e, :]).then_inc(sem["dx_ready"], 1)
                side(f + 13)
                for t, q, ts in tiles:
                    mm = four(2 + q, lambda h, hs: qkT[:, H + h, ts], None, True)
                mm.then_inc(sem["kT_ready"], 1)
                side(f + 14)
                pe.wait_ge(sem["x_blocks"], 2 * (5 * pair + 5))
                pe.wait_ge(sem["kdec_done"], pair + 1)
                for t, q, ts in tiles:
                    four(2 + q, lambda h, hs: cmat[:, q * H + h, :], lambda h, hs: x_bd[:, q * H + h, :]).then_inc(sem["wt_ready"], 1)
                    four(4 + q, lambda h, hs: x_bd[:, q * H + h, :], lambda h, hs: v[:, t, hs]).then_inc(sem["u_ready"], 1)
            turn_mbv(2)
            turn_mbv(3)

            def scores(m):
                h, i = divmod(m, NT)
                r = slice((h % 2) * MD, (h % 2 + 1) * MD)
                if m:
                    pe.wait_ge(sem["s_biased"], m)
                pe.matmul(ps[:, 5, 0:(i + 1) * P], mbqk[r, h // 2, i * P:(i + 1) * P],
                          mbqk[r, 4 + h // 2, 0:(i + 1) * P], start=True, stop=True).then_inc(sem["s_ready"], 1)

            def turn_p(m):
                i = m % NT
                pe.wait_ge(sem["p_done"], m + 1)
                if m:
                    pe.wait_ge(sem["pT_copied"], m)
                for j in range(i + 1):
                    mm = pe.transpose(ps[:, 7, j * P:(j + 1) * P], logit[:, m % 2, j * P:(j + 1) * P], ident[:])
                mm.then_inc(sem["pT_ready"], 1)

            def times_v(m):
                h, i = divmod(m, NT)
                pe.wait_ge(sem["pT_copied"], m + 1)
                if i == 0 and h:
                    pe.wait_ge(sem["mb_done"], h)
                for j in range(i + 1):
                    mm = pe.matmul(ps[:, 6, i * MD:(i + 1) * MD], probT[:, m % 2, j * P:(j + 1) * P],
                                   mbv[:, j, h * MD:(h + 1) * MD], start=j == 0, stop=j == i)
                if i == NT - 1:
                    mm.then_inc(sem["pv_ready"], 1)

            for f in range(32):
                if f % 2 == 0:
                    if f < 4:
                        pe.wait_ge(sem["mbvT_done"], 3 + f // 2)
                    else:
                        pe.wait_ge(sem["gate_kept"], f // 2 - 1)
                half_slab(S_GATE, f)
                if f < 16:
                    c = f // 2
                    t, hf = divmod(c, 2)
                    r, ro = slice(hf * C, (hf + 1) * C), slice((1 - hf) * C, (2 - hf) * C)
                if f < 16 and f % 2 == 0:
                    pe.wait_ge(sem["wt_done"], NT)
                    pe.wait_ge(sem["u_done"], NT)
                    if c:
                        pe.wait_ge(sem["s_done"], c)
                        if c >= 2:
                            pe.wait_ge(sem["o_done"], c - 1)
                        for h in range(H):
                            hs = slice(h * HD, (h + 1) * HD)
                            mm = pe.matmul(ps[:, 2 + hf, hs], wq[:, t, h, hf * P:(hf + 1) * P], state[:, hs], start=h == 0,
                                           stop=False, skip_group_check=True)
                        mm.then_inc(sem["ws_ready"], 1)
                elif f < 16:
                    pe.wait_ge(sem["vnew_done"], c + 1)
                    if c < 2 * NT - 1:
                        for h in range(H):
                            hs = slice(h * HD, (h + 1) * HD)
                            mm = pe.matmul(ps[:, 4, hs], kdec[r, t, hs], vnew[r, hs], start=True, stop=True)
                        mm.then_inc(sem["kv_ready"], 1)
                    for h in range(H):
                        hs = slice(h * HD, (h + 1) * HD)
                        mm = pe.matmul(ps[ro, 2 + hf, hs], attnT[r, t, h * HD + hf * C:h * HD + (hf + 1) * C], vnew[r, hs],
                                       start=c == 0, stop=True, skip_group_check=True)
                    mm.then_inc(sem["o_ready"], 1)
                for m in STEPS[f]:
                    if m == 0:
                        pe.wait_ge(sem["mbqk_done"], 8)
                        pe.wait_ge(sem["mbv_done"], 4)
                    if m < N_UNITS:
                        scores(m)
                    if 2 <= m:
                        times_v(m - 2)
                    if 1 <= m <= N_UNITS:
                        turn_p(m - 1)
                if f in DN_CLOSE:
                    t = DN_CLOSE[f]
                    pe.wait_ge(sem["o_scaled"], t + 1)
                    if t >= 2:
                        pe.wait_ge(sem["o_gated"], t - 1)
                    four(2 + t % 2, lambda h, hs: v[:, t, hs], None, True).then_inc(sem["oT_ready"], 1)
                for t in MB_CLOSE.get(f, ()):
                    pe.wait_ge(sem["mb_done"], MH)
                    pe.wait_ge(sem["o_gated"], NT)
                    four(2 + t, lambda h, hs: omb[:, t, hs], None, True).then_inc(sem["oT_ready"], 1)

            for n in range(NK):
                b = 2 * (n % 2)
                s, slot, _ = slab(S_BRANCH, n)
                pe.wait_ge(sem["slab_lo"], s + 1)
                if n == 0:
                    pe.wait_ge(sem["gate_kept"], 16)
                if n >= 2:
                    pe.wait_ge(sem["merge_mb"], n - 1)
                pe.wait_ge(sem["oT_lo"], 2 * NT)
                products(ps[:, b, :], [(*kslice(slot, k), odn_hi[:, k, :], odn_lo[:, k, :]) for k in range(4)])
                products(ps[:, b + 1, :], [(*kslice(slot, 4 + k), omb_hi[:, k, :], omb_lo[:, k, :]) for k in range(4)]).then_inc(sem["slab_used"], 1)
            pe.wait_ge(sem["merge_mb"], NK)
            for k in range(NK):
                contract(*slab(S_OUT, k)[:2], k % 2, FINS[1] + k + 1, k == 0, k == NK - 1)
            turn(2)
            ffn_stage(1, S_FFN2)


N_ROWS = 5
N_CONST = 4 + 1 + 3 + 3 + 3 + 1 + 8 + 2 + 1 + 3 * LEVELS + 2


_INS = ["x", "ffn1_pre_w", "ffn1_w_gate", "ffn1_w_up", "ffn1_w_down", "ffn1_post_w", "mix_pre_w", "w_in",
        "dn_conv_w", "dn_a_log", "dn_dt_bias", "dn_norm_w", "w_branch_dn", "w_branch_mb", "w_out", "mix_post_w",
        "ffn2_pre_w", "ffn2_w_gate", "ffn2_w_up", "ffn2_w_down", "ffn2_post_w"]


def build(nc, a, out):
    hybrid_layer(nc, a["x"],
                 [(a["ffn1_w_gate"], a["ffn1_w_up"], a["ffn1_w_down"]), (a["ffn2_w_gate"], a["ffn2_w_up"], a["ffn2_w_down"])],
                 a["w_in"], a["dn_conv_w"], a["dn_a_log"], a["dn_dt_bias"], a["dn_norm_w"],
                 a["w_branch_dn"], a["w_branch_mb"], a["w_out"],
                 [(a["ffn1_pre_w"], a["ffn1_post_w"]), (a["mix_pre_w"], a["mix_post_w"]), (a["ffn2_pre_w"], a["ffn2_post_w"])],
                 out)


def kernel(**inputs):
    import numpy as _np
    import concourse.bacc as _bacc
    from concourse import mybir as _mybir
    from concourse.bass_utils import run_bass_kernel_spmd as _run

    nc = _bacc.Bacc("TRN2", target_bir_lowering=False, num_devices=1)
    arrays, args = {}, {}
    for name in _INS:
        arr = _np.ascontiguousarray(inputs[name])
        arrays[f"in_{name}_dram"] = arr
        args[name] = nc.dram_tensor(f"in_{name}_dram", arr.shape, _mybir.dt.from_np(arr.dtype), kind="ExternalInput").ap()[0]
    out = nc.dram_tensor("out_0_dram", (1, T, D), F32, kind="ExternalOutput").ap()[0]
    build(nc, args, out)
    r = _run(nc, [arrays], core_ids=[0])
    return r.results[0]["out_0_dram"]
```

```python
from contextlib import ExitStack

import concourse.bass as bass
from concourse import mybir

F32 = mybir.dt.float32
F32R = mybir.dt.float32r
ALU = mybir.AluOpType
ACT = mybir.ActivationFunctionType
AX = mybir.AxisListType

P = 128
T, D, FF = 512, 1024, 2816
NT, NK, NF = T // P, D // P, FF // P
H, HD = 4, 128
C = 64
MH, MD = 8, 64
EPS = 1e-6
DNW, MBW = H * HD, MH * MD
COL_Z = 3 * DNW
COL_BA = COL_Z + DNW
COL_MBQ = COL_BA + 2 * H
COL_MBV = COL_MBQ + 2 * MBW
COL_GDN = COL_MBV + MBW
COL_GMB = COL_GDN + D

RING = 4
AHEAD = 2
N_FFN = 3 * NF
S_QKV = N_FFN
S_SIDE = S_QKV + 12
S_GATE = S_SIDE + 16
S_BRANCH = S_GATE + 16
S_OUT = S_BRANCH + NK
S_FFN2 = S_OUT + NK
N_SLABS = S_FFN2 + N_FFN
SIDE = ([("qk", j, COL_MBQ + j * P) for j in range(4)] + [("z", j, COL_Z + j * P) for j in range(4)]
        + [("qk", j, COL_MBQ + j * P) for j in range(4, 8)] + [("v", j, COL_MBV + j * P) for j in range(4)])
N_UNITS = MH * NT
STEPS = [[] for _ in range(64)]
for _m in range(N_UNITS + 3):
    STEPS[6 + _m * (58 - 6) // (N_UNITS + 3)].append(_m)
SQUARES = {9: 0, 11: 1, 13: 2, 16: 3}
DN_CLOSE = {19 + t: t for t in range(4)}
MB_CLOSE = {29: (0, 1), 30: (2,), 31: (3,)}
BRANCH_BANKS = (6, 0)
ROW_BANKS = (5, 2, 4, 3)
LEVELS = 6
FINS = (0, NF, NF + NK)
KB = 1024

TURNED = [(i, hf) for hf in range(2) for i in range(2)] + [(i, hf) for i in (2, 3) for hf in range(2)]

SEMAPHORES = """slab_hi slab_lo slab_used const_in const_made ffn_silu ffn_act
split_hi split_lo y_ready y_square y_root y_inverse y_scaled x_done x_square x_root x_inverse h_done
h_turned hT_hi hT_lo wpost_in wpre_in wpre_first x_kept x_back ba_hi ba_lo ba_summed ba_kept ba_ready convw_ready convw_done
exp_b beta_sum beta_ready dt_added dt_neg dt_min exp_t ln_t relu_t g_sum g_ready a_exp a_neg sums_ready
gc_ready last_diff decay_tok beta_exp chunk_decay
conv_start conv_tap conv_done qkv_done sq_made sq_hi_made sq_lo_made sq_summed col_made qk_root qk_inverse qk_scale iv_split sel_made qk_rows qk_done
vT_ready v_done z_done mbqk_done mbvT_done mbv_turned mbv_done
gb_ready diff_made eg_made qdec_done neg_made pos_made decay_row decay_col kk_ready qk_ready amat_done
dec_masked attn_done kT_ready kbe_done kdec_done
level_made turned_0 x0_made xc_made y_mat q_ready q_copied dy_ready dx_ready x_mat x_blocks
wt_ready wt_done u_ready u_done
ws_ready vnew_done kv_ready s_done o_ready o_done o_square o_sum o_root o_inverse o_scaled
oT_ready o_gated oT_hi oT_lo
s_ready s_biased s_max p_done pT_ready pT_copied pv_ready p_inverse mb_done gate_kept
gate_dn gate_mb merge_dn merge_mb merge_done out_done""".split()


def hybrid_layer(nc, x_in, ffn, w_in, conv_w, a_log, dt_bias, dn_norm_w, w_dn, w_mb, w_out, norms, out):
    ctx = ExitStack()
    with ctx:
        sem = {n: ctx.enter_context(nc.semaphore(n)) for n in SEMAPHORES}
        raw_in = [ctx.enter_context(nc.semaphore(f"raw_in{i}")) for i in range(RING)]
        x_in_sem = [ctx.enter_context(nc.semaphore(f"x_in{i}")) for i in range(NT)]
        base = nc.sbuf_base + (-nc.sbuf_base) % 32

        def at(name, kb, shape, dt=F32):
            return nc.alloc_sbuf_tensor_at(name, shape, dt, offset=base + int(kb * KB))

        raw = at("raw", 0, [P, RING, D])
        w_hi = at("w_hi", 16, [P, RING, D], F32R)
        w_lo = at("w_lo", 32, [P, RING, D], F32R)
        hT_hi = at("hT_hi", 48, [P, NK, T], F32R)
        hT_lo = at("hT_lo", 64, [P, NK, T], F32R)
        wpost = at("wpost", 88, [P, D])
        wpre = at("wpre", 92, [P, D])
        ident = at("ident", 96, [P, P])
        upper = at("upper", 96.5, [P, P])
        same = at("same", 97, [P, P])
        half = at("half", 97.5, [P, 2, P])
        level = at("level", 98.5, [P, LEVELS, P])
        alibi = at("alibi", 101.5, [P, T])
        one_col = at("one_col", 103.5, [P, 8, 8])
        ident_c = at("ident_c", 103.75, [P, C])
        normw = at("normw", 104, [P, 1])
        convw = at("convw", 104.25, [P, 4, 12])
        convw_rows = at("convw_rows", 198, [4 * 12, P])
        eps1 = at("eps1", 104.5, [P, 1])
        warm = at("warm", 104.53125, [P, 1])
        eps4 = at("eps4", 104.5625, [P, 1])
        y_ss = at("y_ss", 104.625, [P, 3, NT])
        y_rt = at("y_rt", 104.6875, [P, 3, NT])
        y_iv = at("y_iv", 104.75, [P, 3, NT])
        x_ss = at("x_ss", 104.8125, [P, 3, NT])
        x_rt = at("x_rt", 104.875, [P, 3, NT])
        x_iv = at("x_iv", 104.9375, [P, 3, NT])
        dtb = at("dtb", 105, [P, H])
        alog = at("alog", 105.03125, [P, H])
        nega = at("nega", 105.0625, [P, H])
        nega2 = at("nega2", 105.09375, [P, H])
        qscale = at("qscale", 105.125, [8, 1])
        sel = at("sel", 105.15625, [8, 8], F32R)
        wba_raw = at("wba_raw", 105.25, [P, NK, 8])
        one_col_r = at("one_col_r", 105.25, [P, 8, 8], F32R)
        wba_hi = at("wba_hi", 105.5, [P, NK, 8], F32R)
        wba_lo = at("wba_lo", 105.75, [P, NK, 8], F32R)
        small = at("small", 206, [P, 28, NT * H])
        a_hi = at("a_hi", 182, [P, RING, T], F32R)
        a_lo = at("a_lo", 190, [P, RING, T], F32R)
        x = at("x", 106, [P, NT, D])
        hnat = at("hnat", 122, [P, 2, D])
        junk = at("junk", 130, [P, D])
        fact = at("fact", 134, [P, NF * T])
        silu = at("silu", 178, [P, 2, T])
        scaled = at("scaled", 178, [P, D])
        state = at("state", 80, [P, H * HD])
        vnew = at("vnew", 82, [P, T])
        wq = at("wq", 106, [P, NT, H, 2 * P])
        attnT = at("attnT", 122, [P, NT, T])
        kdec = at("kdec", 130, [P, NT, T])
        qkT = at("qkT", 138, [P, 2 * H, T])
        v = at("v", 154, [P, NT, DNW])
        zT = at("zT", 162, [P, H, T])
        mbqk = at("mbqk", 170, [P, 8, T])
        mbv = at("mbv", 186, [P, NT, MBW])
        cacc = at("cacc", 194, [P, 2, T])
        sq = at("sq", 198, [P, 2, T])
        sq_lo = at("sq_lo", 198, [P, 2, T], F32R)
        sq_hi = at("sq_hi", 202, [P, 2, T], F32R)
        qk_rt = at("qk_rt", 84, [8, T])
        qk_iv = at("qk_iv", 86, [8, T])
        baT = at("baT", 86, [2 * H, T])
        iv_hi = at("iv_hi", 92, [8, T], F32R)
        iv_lo = at("iv_lo", 94, [8, T], F32R)
        vT = at("vT", 88, [P, 2, T])
        amat = at("amat", 194, [P, 2 * H, P])
        cmat = at("cmat", 198, [P, 2 * H, P])
        x_bd = at("x_bd", 84, [P, 2 * H, P])
        x_c = at("x_c", 88, [P, 2 * H, C])
        y_c = at("y_c", 90, [P, 2 * H, C])
        q_c = at("q_c", 92, [P, 2 * H, C])
        mbvT = at("mbvT", 94, [P, T])
        probT = at("probT", 84, [P, 2, T])
        logit = at("logit", 88, [P, 3, T])
        omb = at("omb", 106, [P, NT, MBW])
        gates = [at(f"gate{g}", 138 + 2 * g if g < 8 else 194 + 2 * (g - 8) if g < 14 else 92 + 2 * (g - 14), [P, T])
                 for g in range(16)]
        prod = at("prod", 130, [P, 2, T])
        odn_hi = at("odn_hi", 114, [P, H, T], F32R)
        odn_lo = at("odn_lo", 122, [P, H, T], F32R)
        omb_hi = at("omb_hi", 170, [P, 4, T], F32R)
        omb_lo = at("omb_lo", 178, [P, 4, T], F32R)
        merged = at("merged", 154, [P, NK * T])
        m_hi = at("m_hi", 138, [P, RING, T], F32R)
        m_lo = at("m_lo", 146, [P, RING, T], F32R)
        x_keep = nc.dram_tensor("x_keep", (T, D), F32, kind="Internal").ap()

        ps = ctx.enter_context(nc.psum_tensor("ps", [P, 8, T], F32))

        (BETA0, BETA1, BETA, DTA, DTN, DTM, EXPT, LNT, RELU, GSUM, G, GC, LASTD, DECT, EGC, BEG,
         CD0, CD1, OSS, ORT, OIV) = range(21)
        PM, PS, PI = 21, 23, 25

        def row(r, n=1):
            return small[:, r:r + n, :].rearrange("p a b -> p (a b)")

        def row_th(r):
            return small[:, r, :].rearrange("p (t h) -> p t h", h=H)

        def heads(ap):
            return ap.rearrange("p (h d) -> p h d", h=H)

        def per_head(r, t, n=1):
            return small[:, r, t * H:(t + n) * H].unsqueeze(2).to_broadcast([P, n * H, HD])

        def over(ap, n):
            return ap.unsqueeze(1).to_broadcast([P, n, ap.shape[-1]])

        def banks(b, n=2):
            return ps[:, b:b + n, :].rearrange("p b (h d) -> p (b h) d", d=P)

        def ybank(i):
            return 2 * i

        def wait_y(eng, st, i):
            if i < NT - 1:
                eng.wait_ge(sem["y_ready"], st * (NT - 1) + i + 1)
            else:
                eng.wait_ge(sem["slab_used"], (S_QKV, S_FFN2, N_SLABS)[st])

        def slab(first, j, i=0):
            return first + j + 4 * i, (first + j) % RING, (first + j) // RING + i

        block = ctx.enter_context(nc.Block())

        @block.sync
        def _(sp):
            def load(number, slot, src, dst=None):
                if dst is None:
                    dst, src = (a.rearrange("p (h n) -> p h n", h=2) for a in (raw[:, slot, :], src))
                m = dst.shape[1] // 2
                for hf in range(2):
                    sp.dma_start(dst[:, hf * m:(hf + 1) * m, :], src[:, hf * m:(hf + 1) * m, :]).then_inc(raw_in[slot], 16)

            def free(number, first=False):
                if not first:
                    sp.wait_ge(sem["slab_lo"], number - RING + 1)

            def col_tile(w, col):
                return w[:, bass.ds(col, P)].rearrange("(k p) n -> p k n", p=P)

            def k_view(slot, k=NK):
                return raw[:, slot, :].rearrange("p (k n) -> p k n", k=k)

            def ffn_loads(f, s0):
                wg, wu, wd = ffn[f]

                def pair(i, first=False):
                    for j in range(4):
                        if first and 0 < j < 3:
                            load_x(j + 1)
                        s, slot, _ = slab(s0, j, i)
                        free(s, first)
                        load(s, slot, col_tile((wg, wu)[j % 2], (2 * i + j // 2) * P), k_view(slot))
                pair(0, f == 0)
                with sp.Fori(1, NF // 2) as i:
                    pair(i)

                def down(j, i=0):
                    s, slot, _ = slab(s0 + 2 * NF, j, i)
                    free(s)
                    load(s, slot, wd[bass.ds((j + 4 * i) * P, P), :])
                down(0)
                with sp.Fori(0, (NF - 2) // 4) as i:
                    for j in range(1, 5):
                        down(j, i)
                down(NF - 1)

            def load_x(i):
                sp.dma_start(x[:, i, :], x_in[i * P:(i + 1) * P, :]).then_inc(x_in_sem[i], 16)

            load_x(0)
            load_x(1)
            ffn_loads(0, 0)
            for j in range(12):
                s, slot, _ = slab(S_QKV, j)
                free(s)
                load(s, slot, col_tile(w_in, j * P), k_view(slot))
            cols = [c for _, _, c in SIDE] + [(COL_GDN, COL_GMB)[g % 2] + g // 2 * P for g in range(16)]
            for j, col in enumerate(cols):
                s, slot, _ = slab(S_SIDE, j)
                free(s)
                load(s, slot, col_tile(w_in, col), k_view(slot))
            for n in range(NK):
                s, slot, _ = slab(S_BRANCH, n)
                free(s)
                v2 = raw[:, slot, :].rearrange("p (b k n) -> p b k n", b=2, k=4)
                for b, w in enumerate((w_dn, w_mb)):
                    src = w[:, n * P:(n + 1) * P].rearrange("(k p) n -> p k n", p=P)
                    sp.dma_start(v2[:, b], src).then_inc(raw_in[slot], 16)
            for k in range(NK):
                s, slot, _ = slab(S_OUT, k)
                free(s)
                load(s, slot, w_out[k * P:(k + 1) * P, :])
            ffn_loads(1, S_FFN2)
            for i in range(NT):
                for q in range(2):
                    cs = slice(q * T, (q + 1) * T)
                    sp.wait_ge(sem["x_done"], 2 * NT + 2 * i + q + 1)
                    sp.dma_start(out[i * P:(i + 1) * P, cs], x[:, i, cs]).then_inc(sem["out_done"], 16)
            sp.wait_ge(sem["out_done"], 16 * 2 * NT)

        def split_hi(act, number, slot, use, first=False):
            act.wait_ge(raw_in[slot], 32 * (use + 1))
            if not first:
                act.wait_ge(sem["slab_used"], number - RING + 1)
            act.activation(w_hi[:, slot, :], raw[:, slot, :], ACT.Copy).then_inc(sem["slab_hi"], 1)

        def split_lo(dve, number, slot, use):
            dve.wait_ge(sem["slab_hi"], number + 1)
            dve.tensor_tensor(w_lo[:, slot, :], raw[:, slot, :], w_hi[:, slot, :].bitcast(F32),
                              ALU.subtract).then_inc(sem["slab_lo"], 1)

        @block.gpsimd
        def _(pool):
            def const(ins):
                const.n += 1
                ins.then_inc(sem["const_made"], 1)
                pool.wait_ge(sem["const_made"], const.n)
            const.n = 0
            const(pool.memset(eps1[:], EPS))
            const(pool.memset(eps4[:], 4 * EPS))
            const(pool.memset(ident[:], 0.0))
            const(pool.affine_select(out=ident[:], in_=ident[:], compare_op=ALU.not_equal, fill=1.0, base=0,
                                     pattern=[[-1, P]], channel_multiplier=1))
            pool.dma_start(wba_raw[:], w_in[:, COL_BA:COL_BA + 8].rearrange("(k p) n -> p k n", p=P)).then_inc(sem["const_in"], 16)
            pool.dma_start(dtb[:], dt_bias.partition_broadcast(P)).then_inc(sem["const_in"], 16)
            pool.dma_start(alog[:], a_log.partition_broadcast(P)).then_inc(sem["const_in"], 16)
            pool.dma_start(normw[:], dn_norm_w.unsqueeze(1)).then_inc(sem["const_in"], 16)
            pool.dma_start(convw_rows[:], conv_w.rearrange("k (j p) -> (k j) p", p=P)).then_inc(sem["const_in"], 16)
            pool.dma_start(wpost[:], norms[0][1].partition_broadcast(P)).then_inc(sem["wpost_in"], 16)

            const(pool.tensor_tensor(ident_c[:], ident[:, 0:C], ident[:, C:P], ALU.add))
            const(pool.memset(upper[:], 1.0))
            const(pool.affine_select(out=upper[:], in_=upper[:], compare_op=ALU.is_ge, fill=0.0, base=0,
                                     pattern=[[1, P]], channel_multiplier=-1))
            const(pool.memset(upper[0:C, C:P], 0.0))
            const(pool.memset(same[:], 0.0))
            const(pool.memset(same[0:C, 0:C], 1.0))
            const(pool.memset(same[C:P, C:P], 1.0))
            const(pool.memset(half[:], 0.0))
            const(pool.memset(half[0:C, 0, :], 1.0))
            const(pool.memset(half[C:P, 1, :], 1.0))
            const(pool.memset(one_col[:], 0.0))
            for j in range(8):
                const(pool.memset(one_col[:, j, j:j + 1], 1.0))
            const(pool.memset(qscale[:], 1.0))
            const(pool.memset(qscale[0:H, :], float(HD) ** -0.5))
            const(pool.memset(level[:], 0.0))
            for l in range(LEVELS):
                b = 1 << l
                left = level[:, l, :].rearrange("p (n two b) -> p n two b", two=2, b=b)[:, :, 0, :]
                const(pool.memset(left, 1.0))
                const(pool.affine_select(out=left, in_=left, compare_op=ALU.is_ge, fill=0.0, base=-b,
                                         pattern=[[-2 * b, P // (2 * b)], [0, b]], channel_multiplier=1))
                const(pool.affine_select(out=left, in_=left, compare_op=ALU.is_ge, fill=0.0, base=2 * b - 1,
                                         pattern=[[2 * b, P // (2 * b)], [0, b]], channel_multiplier=-1))
            const(pool.iota(alibi[:], pattern=[[1, T]], base=-(T - P), channel_multiplier=-1,
                            allow_small_or_imprecise_dtypes=True))
            const(pool.affine_select(out=alibi[:], in_=alibi[:], compare_op=ALU.is_ge, fill=-1e30,
                                     base=T - P, pattern=[[-1, T]], channel_multiplier=1))
            assert const.n == N_CONST, const.n

            pool.wait_ge(sem["h_done"], NT)
            pool.dma_start(wpre[:], norms[1][0].partition_broadcast(P)).then_inc(sem["wpre_in"], 16)
            pool.wait_ge(sem["h_done"], 2 * NT)
            pool.dma_start(x_keep.rearrange("(t p) d -> p t d", p=P), x[:]).then_inc(sem["x_kept"], 16)
            for j in range(8):
                pool.wait_ge(sem["qkv_done"], j + 1)
                if j >= 2:
                    pool.wait_ge(sem["sq_summed"], j - 1)
                pool.tensor_tensor(sq[:, j % 2, :], qkT[:, j, :], qkT[:, j, :], ALU.mult).then_inc(sem["sq_made"], 1)
                pool.wait_ge(sem["sq_hi_made"], j + 1)
                pool.tensor_tensor(sq_lo[:, j % 2, :], sq[:, j % 2, :], sq_hi[:, j % 2, :].bitcast(F32),
                                   ALU.subtract).then_inc(sem["sq_lo_made"], 1)
            for pair in range(2):
                for l in range(LEVELS):
                    pool.wait_ge(sem["amat_done"], pair + 1)
                    if l == 1:
                        pool.wait_ge(sem["turned_0"], pair + 1)
                        pool.wait_ge(sem["x0_made"], pair + 1)
                    elif l > 1:
                        pool.wait_ge(sem["q_ready"], 5 * pair + l - 1)
                    pool.tensor_tensor(cmat[:], amat[:], over(level[:, l, :], 2 * H), ALU.mult).then_inc(sem["level_made"], 1)
            pool.wait_ge(sem["pv_ready"], MH)
            pool.dma_start(wpost[:], norms[1][1].partition_broadcast(P)).then_inc(sem["wpost_in"], 16)
            pool.wait_ge(sem["merge_done"], NK)
            pool.dma_start(wpre[:], norms[2][0].partition_broadcast(P)).then_inc(sem["wpre_in"], 16)
            pool.wait_ge(sem["x_kept"], 16)
            pool.wait_ge(sem["slab_used"], S_OUT)
            pool.dma_start(x[:], x_keep.rearrange("(t p) d -> p t d", p=P)).then_inc(sem["x_back"], 16)
            pool.wait_ge(sem["x_done"], 2 * NT)
            pool.dma_start(wpost[:], norms[2][1].partition_broadcast(P)).then_inc(sem["wpost_in"], 16)

        @block.scalar
        def _(act):
            A = act.activation
            ahead = [0]

            def hi_next(first=False):
                if ahead[0] < N_SLABS:
                    s, slot, use = slab(ahead[0], 0)
                    split_hi(act, s, slot, use, first)
                    ahead[0] += 1

            def post(st, i):
                y = ps[:, ybank(i):ybank(i) + 2, :]
                wait_y(act, st, i)
                if st or i:
                    act.wait_ge(sem["y_square"], st * NT + i)
                act.wait_ge(sem["x_square"], min((st + 1) * NT + i, 3 * NT))
                A(junk[:].rearrange("p (a b) -> p a b", a=2), y, ACT.Square, accum_out=y_ss[:, st, i:i + 1]).then_inc(sem["y_square"], 1)
                act.wait_ge(sem["y_square"], st * NT + i + 1)
                k = 1.0 if st == 1 else 4.0
                A(y_rt[:, st, i:i + 1], y_ss[:, st, i:i + 1], ACT.Sqrt, scale=k / D,
                  bias=(eps1 if st == 1 else eps4)[:]).then_inc(sem["y_root"], 1)

            def pre(st, i):
                if st:
                    act.wait_ge(sem["x_done"], (st - 1) * NT + i + 1)
                    act.wait_ge(sem["y_square"], (st - 1) * NT + i + 1)
                else:
                    act.wait_ge(x_in_sem[i], 16)
                    if i == 0:
                        act.wait_ge(sem["const_made"], 2)
                if i:
                    act.wait_ge(sem["x_square"], st * NT + i)
                A(junk[:], x[:, i, :], ACT.Square, accum_out=x_ss[:, st, i:i + 1]).then_inc(sem["x_square"], 1)
                act.wait_ge(sem["x_square"], st * NT + i + 1)
                A(x_rt[:, st, i:i + 1], x_ss[:, st, i:i + 1], ACT.Sqrt, scale=1.0 / D, bias=eps1[:]).then_inc(sem["x_root"], 1)

            def turned(st, i, hf):
                act.wait_ge(sem["h_turned"], (st * NT + i) * 2 + hf + 1)
                A(hT_hi[:, 4 * hf:4 * hf + 4, i * P:(i + 1) * P],
                  ps[:, ybank(i) + hf, :].rearrange("p (k n) -> p k n", k=4), ACT.Copy).then_inc(sem["hT_hi"], 1)

            def boundary(post_st, pre_st):
                for i in range(NT):
                    if post_st is not None:
                        post(post_st, i)
                    if pre_st is None:
                        continue
                    if i >= 2:
                        hi_next(pre_st == 0)
                    if i == 2:
                        for i_hf in TURNED[:4]:
                            turned(pre_st, *i_hf)
                    pre(pre_st, i)
                    if i >= 2:
                        hi_next(pre_st == 0)
                if pre_st is not None:
                    for i_hf in TURNED[4:]:
                        turned(pre_st, *i_hf)

            def split_act(hi, src, k, used=None):
                if used is not None:
                    act.wait_ge(sem["slab_used"], used)
                A(hi[:, k % RING, :], src, ACT.Copy).then_inc(sem["split_hi"], 1)

            def ffn_stage(f, s0):
                def tile(i, j):
                    if isinstance(i, int) and i == j == 0:
                        ahead[0] = s0 + RING
                    else:
                        for q in range(2):
                            split_hi(act, *slab(s0, AHEAD + 2 * j + q, i))
                    act.wait_ge(sem["slab_used"], s0 + 4 * i + 2 * j + 1)
                    if not (isinstance(i, int) and i == 0 and f == 0):
                        act.wait_ge(sem["ffn_act"], f * NF + 2 * i + j - 1)
                    A(silu[:, j, :], ps[:, 2 * j, :], ACT.Silu).then_inc(sem["ffn_silu"], 1)
                for j in range(2):
                    tile(0, j)
                with act.Fori(1, NF // 2 - 1) as i:
                    for j in range(2):
                        tile(i, j)
                if f == 0:
                    act.wait_ge(sem["const_in"], 16 * N_ROWS)
                    A(wba_hi[:], wba_raw[:], ACT.Copy).then_inc(sem["ba_hi"], 1)
                    A(sel[:], ident[0:8, 0:8], ACT.Copy).then_inc(sem["sel_made"], 1)
                    A(nega[:], alog[:], ACT.Exp).then_inc(sem["a_exp"], 1)
                tile(NF // 2 - 1, 0)
                act.wait_ge(sem["ffn_act"], f * NF + NF - 2)
                split_act(a_hi, fact[:, 0:T], 0)
                tile(NF // 2 - 1, 1)
                act.wait_ge(sem["ffn_act"], (f + 1) * NF)
                s1 = s0 + 2 * NF

                def step(j, i=0):
                    k = j + 4 * i
                    if not isinstance(k, int) or k + AHEAD < NF:
                        split_hi(act, *slab(s1, j + AHEAD, i))
                    act.wait_ge(sem["slab_used"], s1 + k - 2)
                    A(a_hi[:, (j + 1) % RING, :], fact[:, bass.ds((k + 1) * T, T)], ACT.Copy).then_inc(sem["split_hi"], 1)
                step(0)
                with act.Fori(0, (NF - 2) // 4 - 1) as i:
                    for j in range(1, 5):
                        step(j, i)
                for k in range(NF - 5, NF - 1):
                    step(k)
                ahead[0] = s1 + NF

            act.dma_start(wpre[:], norms[0][0].partition_broadcast(P)).then_inc(sem["wpre_first"], 16)
            act.wait_ge(sem["const_made"], 2)
            A(warm[:], eps1[:], ACT.Sqrt)
            boundary(None, 0)
            ffn_stage(0, 0)
            boundary(0, 1)

            def finish_qkv(j):
                act.wait_ge(sem["conv_done"], j + 1)
                if j >= 10:
                    act.wait_ge(sem["vT_ready"], j - 9)
                dst = qkT[:, j, :] if j < 8 else vT[:, j % 2, :]
                A(dst, cacc[:, j % 2, :], ACT.Silu).then_inc(sem["qkv_done"], 1)

            ab = ps[:, 4, 0:NT * 8].rearrange("p (t c) -> p t c", c=8)
            for j in range(12):
                if j >= 2:
                    hi_next()
                if j:
                    finish_qkv(j - 1)
                act.wait_ge(sem["slab_used"], S_QKV + j + 1)
                if j >= 2:
                    act.wait_ge(sem["qkv_done"], j - 1)
                A(cacc[:, j % 2, :], ps[:, j % 4, :], ACT.Copy, scale=convw[:, 3, j:j + 1]).then_inc(sem["conv_start"], 1)
                if 1 <= j <= 8:
                    act.wait_ge(sem["sq_made"], j)
                    A(sq_hi[:, (j - 1) % 2, :], sq[:, (j - 1) % 2, :], ACT.Copy).then_inc(sem["sq_hi_made"], 1)
                if j == 0:
                    act.wait_ge(sem["ba_lo"], 1)
                    A(one_col_r[:], one_col[:], ACT.Copy).then_inc(sem["col_made"], 1)
                if j == 3:
                    act.wait_ge(sem["ba_summed"], 1)
                    A(baT[:], ps[0:2 * H, 6, :], ACT.Copy).then_inc(sem["ba_kept"], 1)
                if j == 6:
                    act.wait_ge(sem["ba_ready"], 1)
                    A(row_th(BETA0), ab[:, :, 0:H], ACT.Exp, scale=-1.0).then_inc(sem["exp_b"], 1)
                if j == 7:
                    act.wait_ge(sem["dt_min"], 1)
                    A(row(EXPT), row(DTM), ACT.Exp).then_inc(sem["exp_t"], 1)
                    act.wait_ge(sem["exp_t"], 1)
                    A(row(LNT), row(EXPT), ACT.Ln, bias=1.0).then_inc(sem["ln_t"], 1)
                if j == 10:
                    act.wait_ge(sem["qk_scale"], 1)
                    A(iv_hi[:], qk_iv[:], ACT.Copy).then_inc(sem["iv_split"], 1)
                if j == 9:
                    act.wait_ge(sem["sq_summed"], 8)
                    A(qk_rt[:], ps[0:8, 5, :], ACT.Sqrt, bias=eps1[0:8, :]).then_inc(sem["qk_root"], 1)
            finish_qkv(11)
            act.wait_ge(sem["beta_ready"], 1)
            act.wait_ge(sem["gc_ready"], 1)
            A(row(EGC), row(GC), ACT.Exp).then_inc(sem["decay_tok"], 1)
            act.wait_ge(sem["last_diff"], 1)
            A(row(DECT), row(LASTD), ACT.Exp).then_inc(sem["decay_tok"], 1)
            A(row(CD0, 2), ps[:, 4, 96:128], ACT.Exp).then_inc(sem["chunk_decay"], 1)

            def side_post(n):
                kind, j, _ = SIDE[n]
                act.wait_ge(sem["slab_used"], S_SIDE + n + 1)
                y = ps[:, n % 2, :]
                if kind == "qk":
                    A(mbqk[:, j, :], y, ACT.Copy, scale=(float(MD) ** -0.5 if j < 4 else 1.0)).then_inc(sem["mbqk_done"], 1)
                elif kind == "z":
                    A(zT[:, j, :], y, ACT.Silu).then_inc(sem["z_done"], 1)
                else:
                    if j:
                        act.wait_ge(sem["mbv_turned"], j)
                    A(mbvT[:], y, ACT.Copy).then_inc(sem["mbvT_done"], 1)

            def side(f):
                if f % 2 == 0:
                    hi_next()
                elif f > 2:
                    side_post(f // 2 - 1)

            side(0)
            side(1)
            for pair in range(2):
                f = 2 + 15 * pair
                pt = slice(2 * pair, 2 * pair + 2)
                side(f)
                act.wait_ge(sem["diff_made"], pair + 1)
                act.wait_ge(sem["x_kept"], 16)
                A(wq[:, pt, :, C:C + P], ps[:, 2:4, :].rearrange("p q (h d) -> p q h d", h=H), ACT.Exp).then_inc(sem["eg_made"], 1)
                act.wait_ge(sem["neg_made"], pair + 1)
                A(cmat[:], cmat[:], ACT.Exp).then_inc(sem["decay_row"], 1)
                act.wait_ge(sem["pos_made"], pair + 1)
                A(attnT[:, pt, :], attnT[:, pt, :], ACT.Exp).then_inc(sem["decay_col"], 1)
                side(f + 1)
                side(f + 2)
                for l in range(1, LEVELS):
                    n = 5 * pair + l
                    side(f + 1 + 2 * l)
                    act.wait_ge(sem["q_ready"], n)
                    if n > 1:
                        act.wait_ge(sem["dy_ready"], n - 1)
                        act.wait_ge(sem["dx_ready"], 4 * pair + min(l - 1, 4))
                    A(q_c[:], ps[:, 4, :].rearrange("p (e d) -> p e d", d=C), ACT.Copy).then_inc(sem["q_copied"], 1)
                    side(f + 2 + 2 * l)
                side(f + 13)
                side(f + 14)
                for q in range(2):
                    t = 2 * pair + q
                    act.wait_ge(sem["wt_ready"], t + 1)
                    dst = wq[:, t, :, :].rearrange("p h (c d) -> p h c d", d=C)[:, :, 0:4:3, :]
                    A(dst, ps[:, 2 + q, :].rearrange("p (h c d) -> p h c d", h=H, c=2), ACT.Copy).then_inc(sem["wt_done"], 1)
            side_post(15)

            def gate_post(g):
                act.wait_ge(sem["slab_used"], S_GATE + g + 1)
                A(gates[g][:], ps[:, g % 2, :], ACT.Copy).then_inc(sem["gate_kept"], 1)

            def units(g):
                for m in STEPS[g]:
                    if 2 <= m < N_UNITS + 2:
                        w = ((m - 2) % NT + 1) * P
                        act.wait_ge(sem["pT_ready"], m - 1)
                        A(probT[:, m % 2, 0:w], ps[:, 7, 0:w], ACT.Copy).then_inc(sem["pT_copied"], 1)
                    if m < N_UNITS:
                        w = (m % NT + 1) * P
                        act.wait_ge(sem["s_max"], m + 1)
                        A(logit[:, m % 3, 0:w], logit[:, m % 3, 0:w], ACT.Exp, bias=row(PM, 2)[:, m:m + 1],
                          accum_out=row(PS, 2)[:, m:m + 1]).then_inc(sem["p_done"], 1)

            for f in range(32):
                if f % 2 == 0:
                    hi_next()
                elif f > 2:
                    gate_post(f // 2 - 1)
                units(2 * f)
                if f < 16 and f % 2 == 1:
                    c = f // 2
                    r, ro = slice(c % 2 * C, (c % 2 + 1) * C), slice((1 - c % 2) * C, (2 - c % 2) * C)
                    act.wait_ge(sem["o_ready"], c + 1)
                    A(v[r, c // 2, :], ps[ro, 2 + c % 2, :], ACT.Copy).then_inc(sem["o_done"], 1)
                units(2 * f + 1)
                if f in SQUARES:
                    t = SQUARES[f]
                    if t >= 2:
                        act.wait_ge(sem["o_sum"], t - 1)
                    else:
                        act.wait_ge(sem["kv_ready"], 4)
                    act.wait_ge(sem["o_done"], 2 * t + 2)
                    A(prod[:, t % 2, :], v[:, t, :], ACT.Square).then_inc(sem["o_square"], 1)
                if f == 17:
                    act.wait_ge(sem["o_sum"], NT)
                    A(row(ORT), row(OSS), ACT.Sqrt, scale=1.0 / HD, bias=eps1[:]).then_inc(sem["o_root"], 1)
                if f in DN_CLOSE:
                    t = DN_CLOSE[f]
                    act.wait_ge(sem["o_gated"], t + 1)
                    A(odn_hi[:, :, t * P:(t + 1) * P], prod[:, t % 2, :].rearrange("p (k n) -> p k n", k=4),
                      ACT.Copy).then_inc(sem["oT_hi"], 1)
                for t in MB_CLOSE.get(f, ()):
                    act.wait_ge(sem["oT_ready"], NT + t + 1)
                    A(omb_hi[:, :, t * P:(t + 1) * P], ps[:, 2 + t, :].rearrange("p (k n) -> p k n", k=4),
                      ACT.Copy).then_inc(sem["oT_hi"], 1)
            gate_post(15)

            def split_merged(k):
                act.wait_ge(sem["merge_done"], max(k + 1, 4))
                split_act(m_hi, merged[:, k * T:(k + 1) * T], k, S_OUT + k - 3 if k >= RING else None)

            for n in range(NK):
                hi_next()
                for g, name in ((2 * n, "gate_dn"), (2 * n + 1, "gate_mb")):
                    act.wait_ge(sem["gate_kept"], g + 1)
                    A(gates[g][:], gates[g][:], ACT.Sigmoid).then_inc(sem[name], 1)
                if n >= 5:
                    split_merged(n - 5)
            for k in range(NK - 5, NK):
                if k > 3:
                    hi_next()
                split_merged(k)
                if k in (3, 4):
                    hi_next()
            boundary(1, 2)
            ffn_stage(1, S_FFN2)
            boundary(2, None)

        @block.vector
        def _(dve):
            ahead = [0]

            def lo_next():
                if ahead[0] < N_SLABS:
                    split_lo(dve, *slab(ahead[0], 0))
                    ahead[0] += 1

            def post(st, i):
                y = ps[:, ybank(i):ybank(i) + 2, :]
                dve.wait_ge(sem["y_root"], st * NT + i + 1)
                dve.reciprocal(y_iv[:, st, i:i + 1], y_rt[:, st, i:i + 1]).then_inc(sem["y_inverse"], 1)
                dve.wait_ge(sem["y_inverse"], st * NT + i + 1)
                dve.wait_ge(sem["wpost_in"], 16 * (st + 1))
                parts = 2 if st == 2 else 1
                if st or i:
                    dve.wait_ge(sem["x_done"], st * NT + parts * i)
                if i == 0 and st == 1:
                    dve.wait_ge(sem["x_back"], 16)
                w = D // parts
                for q in range(parts):
                    yq = y if parts == 1 else y[:, q:q + 1, :]
                    dve.scalar_tensor_tensor(scaled[:, q * w:(q + 1) * w].rearrange("p (a b) -> p a b", b=T), yq, y_iv[:, st, i:i + 1],
                                             wpost[:, q * w:(q + 1) * w].rearrange("p (a b) -> p a b", b=T), ALU.mult,
                                             ALU.mult).then_inc(sem["y_scaled"], 1)
                for q in range(parts):
                    dve.wait_ge(sem["y_scaled"], st * NT + parts * i + q + 1)
                    dve.tensor_tensor(x[:, i, q * w:(q + 1) * w], x[:, i, q * w:(q + 1) * w], scaled[:, q * w:(q + 1) * w],
                                      ALU.add).then_inc(sem["x_done"], 1)

            def pre(st, i):
                dve.wait_ge(sem["x_root"], st * NT + i + 1)
                dve.reciprocal(x_iv[:, st, i:i + 1], x_rt[:, st, i:i + 1]).then_inc(sem["x_inverse"], 1)
                dve.wait_ge(sem["x_inverse"], st * NT + i + 1)
                if i == 0:
                    if st:
                        dve.wait_ge(sem["wpre_in"], 16 * st)
                    else:
                        dve.wait_ge(sem["wpre_first"], 16)
                if i >= 2 or st:
                    dve.wait_ge(sem["h_turned"], 2 * (st * NT + i - 1))
                dve.scalar_tensor_tensor(hnat[:, i % 2, :], x[:, i, :], x_iv[:, st, i:i + 1], wpre[:],
                                         ALU.mult, ALU.mult).then_inc(sem["h_done"], 1)

            def turned(st, i, hf):
                dve.wait_ge(sem["hT_hi"], st * NT * 2 + TURNED.index((i, hf)) + 1)
                dst = (slice(None), slice(4 * hf, 4 * hf + 4), slice(i * P, (i + 1) * P))
                dve.tensor_tensor(hT_lo[dst], ps[:, ybank(i) + hf, :].rearrange("p (k n) -> p k n", k=4),
                                  hT_hi[dst].bitcast(F32), ALU.subtract).then_inc(sem["hT_lo"], 1)

            def boundary(post_st, pre_st):
                for i in range(NT):
                    if post_st is not None:
                        post(post_st, i)
                    if pre_st is None:
                        continue
                    if i >= 2:
                        lo_next()
                    if i == 2:
                        for i_hf in TURNED[:4]:
                            turned(pre_st, *i_hf)
                    pre(pre_st, i)
                    if i >= 2:
                        lo_next()
                if pre_st is not None:
                    for i_hf in TURNED[4:]:
                        turned(pre_st, *i_hf)

            def split_act(hi, lo, src, n, slot):
                dve.wait_ge(sem["split_hi"], n)
                dve.tensor_tensor(lo[:, slot, :], src, hi[:, slot, :].bitcast(F32), ALU.subtract).then_inc(sem["split_lo"], 1)

            def ffn_stage(f, s0):
                def tile(i, j):
                    if not (isinstance(i, int) and i == j == 0):
                        for q in range(2):
                            split_lo(dve, *slab(s0, AHEAD + 2 * j + q, i))
                    n = f * NF + 2 * i + j + 1
                    dve.wait_ge(sem["ffn_silu"], n)
                    dve.wait_ge(sem["slab_used"], s0 + 4 * i + 2 * j + 2)
                    dve.tensor_tensor(fact[:, bass.ds((2 * i + j) * T, T)], silu[:, j, :], ps[:, 2 * j + 1, :],
                                      ALU.mult).then_inc(sem["ffn_act"], 1)
                for j in range(2):
                    tile(0, j)
                with dve.Fori(1, NF // 2 - 1) as i:
                    for j in range(2):
                        tile(i, j)
                first = FINS[2 * f]
                if f == 0:
                    dve.wait_ge(sem["ba_hi"], 1)
                    dve.wait_ge(sem["convw_ready"], 1)
                    dve.tensor_copy(convw[:].rearrange("p k j -> p (k j)"), ps[:, 7, 0:48]).then_inc(sem["convw_done"], 1)
                    dve.tensor_tensor(wba_lo[:], wba_raw[:], wba_hi[:].bitcast(F32), ALU.subtract).then_inc(sem["ba_lo"], 1)
                tile(NF // 2 - 1, 0)
                split_act(a_hi, a_lo, fact[:, 0:T], first + 1, 0)
                tile(NF // 2 - 1, 1)
                s1 = s0 + 2 * NF

                def step(j, i=0):
                    k = j + 4 * i
                    if not isinstance(k, int) or k + AHEAD < NF:
                        split_lo(dve, *slab(s1, j + AHEAD, i))
                    split_act(a_hi, a_lo, fact[:, bass.ds((k + 1) * T, T)], first + k + 2, (j + 1) % RING)
                step(0)
                with dve.Fori(0, (NF - 2) // 4 - 1) as i:
                    for j in range(1, 5):
                        step(j, i)
                for k in range(NF - 5, NF - 1):
                    step(k)
                ahead[0] = s1 + NF

            boundary(None, 0)
            ffn_stage(0, 0)
            boundary(0, 1)

            def v_heads(h):
                dve.wait_ge(sem["vT_ready"], h + 1)
                dve.wait_ge(sem["beta_ready"], 1)
                dve.tensor_tensor(v[:, :, h * HD:(h + 1) * HD], ps[:, 6 + h % 2, :].rearrange("p (t d) -> p t d", d=HD),
                                  row_th(BETA)[:, :, h:h + 1].to_broadcast([P, NT, HD]), ALU.mult).then_inc(sem["v_done"], 1)

            ab = ps[:, 4, 0:NT * 8].rearrange("p (t c) -> p t c", c=8)

            def betas():
                dve.wait_ge(sem["exp_b"], 1)
                dve.tensor_tensor(row_th(DTA), ab[:, :, H:2 * H], dtb[:].unsqueeze(1).to_broadcast([P, NT, H]), ALU.add).then_inc(sem["dt_added"], 1)
                dve.tensor_scalar(row(BETA1), row(BETA0), 1.0, None, ALU.add).then_inc(sem["beta_sum"], 1)
                dve.wait_ge(sem["dt_added"], 1)
                dve.tensor_scalar(row(DTN), row(DTA), -1.0, None, ALU.mult).then_inc(sem["dt_neg"], 1)
                dve.wait_ge(sem["dt_neg"], 1)
                dve.tensor_tensor(row(DTM), row(DTA), row(DTN), ALU.min).then_inc(sem["dt_min"], 1)
                dve.wait_ge(sem["beta_sum"], 1)
                dve.reciprocal(row(BETA), row(BETA1)).then_inc(sem["beta_ready"], 1)
                dve.tensor_scalar(row(RELU), row(DTA), 0.0, None, ALU.max).then_inc(sem["relu_t"], 1)
                dve.wait_ge(sem["a_exp"], 1)
                dve.tensor_scalar(nega2[:], nega[:], -1.0, None, ALU.mult).then_inc(sem["a_neg"], 1)

            def decays():
                dve.wait_ge(sem["relu_t"], 1)
                dve.wait_ge(sem["ln_t"], 1)
                dve.tensor_tensor(row(GSUM), row(RELU), row(LNT), ALU.add).then_inc(sem["g_sum"], 1)
                dve.wait_ge(sem["g_sum"], 1)
                dve.wait_ge(sem["a_neg"], 1)
                dve.tensor_tensor(row_th(G), row_th(GSUM), nega2[:].unsqueeze(1).to_broadcast([P, NT, H]), ALU.mult).then_inc(sem["g_ready"], 1)

            for j in range(12):
                if j >= 2:
                    lo_next()
                if j == 10:
                    dve.wait_ge(sem["qk_root"], 1)
                    dve.reciprocal(qk_iv[:], qk_rt[:]).then_inc(sem["qk_inverse"], 1)
                    dve.wait_ge(sem["qk_inverse"], 1)
                    dve.tensor_scalar(qk_iv[:], qk_iv[:], qscale[:, 0:1], None, ALU.mult).then_inc(sem["qk_scale"], 1)
                dve.wait_ge(sem["conv_start"], j + 1)
                for k in range(1, 4):
                    acc = cacc[:, j % 2, k:T]
                    dve.scalar_tensor_tensor(acc, ps[:, j % 4, 0:T - k], convw[:, 3 - k, j:j + 1], acc, ALU.mult,
                                             ALU.add).then_inc(sem["conv_done" if k == 3 else "conv_tap"], 1)
                    if k < 3:
                        dve.wait_ge(sem["conv_tap"], 2 * j + k)
                if j == 6:
                    betas()
                if j == 7:
                    decays()
                if j == 10:
                    dve.wait_ge(sem["sums_ready"], 1)
                    dve.tensor_copy(row(GC), ps[:, 4, 64:80]).then_inc(sem["gc_ready"], 1)
                    dve.wait_ge(sem["gc_ready"], 1)
                    dve.tensor_tensor(row(LASTD), ps[:, 4, 80:96], row(GC), ALU.subtract).then_inc(sem["last_diff"], 1)
                if j == 11:
                    dve.wait_ge(sem["iv_split"], 1)
                    dve.tensor_tensor(iv_lo[:], qk_iv[:], iv_hi[:].bitcast(F32), ALU.subtract).then_inc(sem["iv_split"], 1)
                    v_heads(0)
                    v_heads(1)

            def side(f):
                if f % 2 == 0:
                    lo_next()
                if f in (29, 31):
                    keep_mbv(f // 2 - 14)

            def keep_mbv(j):
                dve.wait_ge(sem["mbv_turned"], j + 1)
                dve.tensor_copy(mbv[:, :, j * P:(j + 1) * P], ps[:, 7, :].rearrange("p (t d) -> p t d", d=P)).then_inc(sem["mbv_done"], 1)

            def qk_norm(j):
                dve.wait_ge(sem["qk_rows"], j + 1)
                dve.tensor_tensor(qkT[:, j, :], qkT[:, j, :], ps[:, ROW_BANKS[j % 4], :], ALU.mult).then_inc(sem["qk_done"], 1)

            side(0)
            for j in range(4):
                qk_norm(j)
            side(1)
            v_heads(2)
            v_heads(3)
            for j in range(4, 8):
                qk_norm(j)
            dve.wait_ge(sem["decay_tok"], 1)
            dve.tensor_tensor(row(BEG), row(EGC), row(BETA), ALU.mult).then_inc(sem["beta_exp"], 1)
            for pair in range(2):
                f = 2 + 15 * pair
                pt = slice(2 * pair, 2 * pair + 2)
                side(f)
                dve.wait_ge(sem["gb_ready"], pair + 1)
                if pair:
                    dve.wait_ge(sem["level_made"], LEVELS)
                dve.tensor_tensor(amat[:], banks(2), per_head(GC, 2 * pair, 2), ALU.subtract).then_inc(sem["diff_made"], 1)
                dve.wait_ge(sem["diff_made"], pair + 1)
                if pair:
                    dve.wait_ge(sem["wt_ready"], 2)
                dve.tensor_scalar(cmat[:], amat[:], -1.0, 0.0, ALU.mult, ALU.min).then_inc(sem["neg_made"], 1)
                dve.wait_ge(sem["x_kept"], 16)
                dve.tensor_scalar(attnT[:, pt, :].rearrange("p q (h d) -> p (q h) d", h=H), amat[:], 0.0, None,
                                  ALU.min).then_inc(sem["pos_made"], 1)
                dve.wait_ge(sem["eg_made"], pair + 1)
                dst = wq[:, pt, :, C:C + P]
                for q in range(2):
                    t = 2 * pair + q
                    dve.tensor_tensor(wq[:, t, :, C:C + P], wq[:, t, :, C:C + P], qkT[:, 0:H, t * P:(t + 1) * P],
                                      ALU.mult).then_inc(sem["qdec_done"], 1)
                dve.wait_ge(sem["kk_ready"], pair + 1)
                dve.wait_ge(sem["decay_row"], pair + 1)
                dve.wait_ge(sem["pos_made"], pair + 1)
                for e in range(2 * H):
                    ins = dve.scalar_tensor_tensor(amat[:, e, :], cmat[:, e, :], row(BETA)[:, 2 * pair * H + e:2 * pair * H + e + 1],
                                                   banks(4)[:, e, :], ALU.mult, ALU.mult)
                ins.then_inc(sem["amat_done"], 1)
                side(f + 1)
                dve.wait_ge(sem["decay_col"], pair + 1)
                at_p = attnT[:, pt, :].rearrange("p q (h d) -> p (q h) d", h=H)
                dve.tensor_tensor(at_p, at_p, over(upper[:], 2 * H), ALU.mult).then_inc(sem["dec_masked"], 1)
                dve.wait_ge(sem["level_made"], LEVELS * pair + 1)
                dve.tensor_tensor(x_bd[:], over(ident[:], 2 * H), cmat[:], ALU.subtract).then_inc(sem["x0_made"], 1)
                dve.wait_ge(sem["qk_ready"], pair + 1)
                dve.wait_ge(sem["dec_masked"], pair + 1)
                dve.tensor_tensor(at_p, at_p, banks(6), ALU.mult).then_inc(sem["attn_done"], 1)
                dve.wait_ge(sem["x0_made"], pair + 1)
                for hf in range(2):
                    r = slice(hf * C, (hf + 1) * C)
                    dve.tensor_copy(x_c[r, :, :], x_bd[r, :, r]).then_inc(sem["xc_made"], 1)
                side(f + 2)
                dve.wait_ge(sem["turned_0"], pair + 1)
                dve.tensor_tensor(y_c[:], over(ident_c[:], 2 * H), ps[:, 4, :].rearrange("p (e d) -> p e d", d=C),
                                  ALU.subtract).then_inc(sem["y_mat"], 1)
                for l in range(1, LEVELS):
                    n = 5 * pair + l
                    side(f + 1 + 2 * l)
                    side(f + 2 + 2 * l)
                    dve.wait_ge(sem["dy_ready"], n)
                    dve.wait_ge(sem["y_mat"], 6 * pair + l)
                    dve.tensor_tensor(y_c[:], y_c[:], ps[:, 5, :].rearrange("p (e d) -> p e d", d=C),
                                      ALU.subtract).then_inc(sem["y_mat"], 1)
                    if l < LEVELS - 1:
                        dve.wait_ge(sem["dx_ready"], 4 * pair + l)
                        if l > 1:
                            dve.wait_ge(sem["x_mat"], 4 * pair + l - 1)
                        else:
                            dve.wait_ge(sem["xc_made"], 2 * pair + 2)
                        dve.tensor_tensor(x_c[:], x_c[:], ps[:, 6, :].rearrange("p (e d) -> p e d", d=C),
                                          ALU.subtract).then_inc(sem["x_mat"], 1)
                side(f + 13)
                dve.wait_ge(sem["y_mat"], 6 * (pair + 1))
                for hf in range(2):
                    r = slice(hf * C, (hf + 1) * C)
                    dve.tensor_copy(x_bd[r, :, r], y_c[r, :, :]).then_inc(sem["x_blocks"], 1)
                dve.wait_ge(sem["kT_ready"], pair + 1)
                dve.wait_ge(sem["beta_exp"], 1)
                dve.wait_ge(sem["decay_tok"], 2)
                dve.tensor_tensor(cmat[:], banks(2), per_head(BEG, 2 * pair, 2), ALU.mult).then_inc(sem["kbe_done"], 1)
                dve.tensor_tensor(kdec[:, pt, :].rearrange("p q (h d) -> p (q h) d", h=H), banks(2), per_head(DECT, 2 * pair, 2),
                                  ALU.mult).then_inc(sem["kdec_done"], 1)
                side(f + 14)
                for q in range(2):
                    t = 2 * pair + q
                    dve.wait_ge(sem["u_ready"], t + 1)
                    dve.tensor_copy(v[:, t, :], ps[:, 4 + q, :]).then_inc(sem["u_done"], 1)
            keep_mbv(2)

            def mb_out(h):
                dve.wait_ge(sem["p_done"], h * NT + NT)
                dve.reciprocal(row(PI, 2)[:, h * NT:(h + 1) * NT], row(PS, 2)[:, h * NT:(h + 1) * NT]).then_inc(sem["p_inverse"], 1)
                dve.wait_ge(sem["p_inverse"], h + 1)
                dve.wait_ge(sem["pv_ready"], h + 1)
                dve.wait_ge(sem["o_ready"], 4)
                dve.tensor_tensor(omb[:, :, h * MD:(h + 1) * MD], ps[:, 6, 0:NT * MD].rearrange("p (t d) -> p t d", d=MD),
                                  row(PI, 2)[:, h * NT:(h + 1) * NT].unsqueeze(2).to_broadcast([P, NT, MD]),
                                  ALU.mult).then_inc(sem["mb_done"], 1)

            def units(g):
                for m in STEPS[g]:
                    if m < N_UNITS:
                        h, i = divmod(m, NT)
                        w = (i + 1) * P
                        dve.wait_ge(sem["s_ready"], m + 1)
                        if m >= 3:
                            dve.wait_ge(sem["pT_ready"], m - 2)
                        slope = 2.0 ** (-8.0 * (h + 1) / MH)
                        dve.scalar_tensor_tensor(logit[:, m % 3, 0:w], alibi[:, T - w:T], slope, ps[:, 5, 0:w],
                                                 ALU.mult, ALU.add).then_inc(sem["s_biased"], 1)
                        dve.wait_ge(sem["s_biased"], m + 1)
                        dve.tensor_reduce(row(PM, 2)[:, m:m + 1], logit[:, m % 3, 0:w], AX.X, ALU.max, negate=True).then_inc(sem["s_max"], 1)
                    if m >= NT + 2 and m % NT == 2:
                        mb_out(m // NT - 1)

            for f in range(32):
                if f % 2 == 0:
                    lo_next()
                units(2 * f)
                if f < 16:
                    c = f // 2
                    t, hf = divmod(c, 2)
                    r = slice(hf * C, (hf + 1) * C)
                if f < 16 and f % 2 == 0:
                    dve.wait_ge(sem["u_done"], t + 1)
                    if c >= 2:
                        dve.wait_ge(sem["o_ready"], c - 1)
                    if c == 0:
                        dve.tensor_copy(vnew[r, :], v[r, t, :]).then_inc(sem["vnew_done"], 1)
                        keep_mbv(3)
                    else:
                        dve.wait_ge(sem["ws_ready"], c)
                        dve.tensor_tensor(vnew[r, :], v[r, t, :], ps[r, 2 + hf, :], ALU.subtract).then_inc(sem["vnew_done"], 1)
                elif f < 15:
                    dve.wait_ge(sem["kv_ready"], c + 1)
                    if c == 0:
                        dve.tensor_copy(state[:], ps[:, 4, :]).then_inc(sem["s_done"], 1)
                    else:
                        dve.wait_ge(sem["s_done"], c)
                        for h in range(H):
                            hs = slice(h * HD, (h + 1) * HD)
                            cd = row(CD0 + hf)[:, t * H + h:t * H + h + 1]
                            ins = dve.scalar_tensor_tensor(state[:, hs], state[:, hs], cd, ps[:, 4, hs], ALU.mult, ALU.add)
                        ins.then_inc(sem["s_done"], 1)
                units(2 * f + 1)
                if f in SQUARES:
                    t = SQUARES[f]
                    dve.wait_ge(sem["o_square"], t + 1)
                    dve.tensor_reduce(small[:, OSS, t * H:(t + 1) * H], heads(prod[:, t % 2, :]), AX.X, ALU.add).then_inc(sem["o_sum"], 1)
                if f == 18:
                    dve.wait_ge(sem["o_root"], 1)
                    dve.reciprocal(row(OIV), row(ORT)).then_inc(sem["o_inverse"], 1)
                    dve.wait_ge(sem["o_inverse"], 1)
                if 18 <= f < 18 + NT:
                    t = f - 18
                    dve.tensor_tensor(heads(v[:, t, :]), heads(v[:, t, :]), per_head(OIV, t), ALU.mult).then_inc(sem["o_scaled"], 1)
                if f in DN_CLOSE:
                    t = DN_CLOSE[f]
                    dve.wait_ge(sem["oT_ready"], t + 1)
                    dve.wait_ge(sem["z_done"], 4)
                    if t >= 2:
                        dve.wait_ge(sem["oT_lo"], t - 1)
                    else:
                        dve.wait_ge(sem["o_sum"], NT)
                    dve.scalar_tensor_tensor(heads(prod[:, t % 2, :]), heads(ps[:, 2 + t % 2, :]), normw[:, 0:1],
                                             zT[:, :, t * P:(t + 1) * P], ALU.mult, ALU.mult).then_inc(sem["o_gated"], 1)
                    dve.wait_ge(sem["oT_hi"], t + 1)
                    dve.tensor_tensor(odn_lo[:, :, t * P:(t + 1) * P], heads(prod[:, t % 2, :]),
                                      odn_hi[:, :, t * P:(t + 1) * P].bitcast(F32), ALU.subtract).then_inc(sem["oT_lo"], 1)
                for t in MB_CLOSE.get(f, ()):
                    dve.wait_ge(sem["oT_hi"], NT + t + 1)
                    dve.tensor_tensor(omb_lo[:, :, t * P:(t + 1) * P], heads(ps[:, 2 + t, :]),
                                      omb_hi[:, :, t * P:(t + 1) * P].bitcast(F32), ALU.subtract).then_inc(sem["oT_lo"], 1)

            def split_merged(k):
                split_act(m_hi, m_lo, merged[:, k * T:(k + 1) * T], FINS[1] + k + 1, k % RING)

            for n in range(NK):
                lo_next()
                b = BRANCH_BANKS[n % 2]
                dve.wait_ge(sem["slab_used"], S_BRANCH + n + 1)
                dve.wait_ge(sem["gate_dn"], n + 1)
                if n:
                    dve.wait_ge(sem["merge_done"], n)
                dve.tensor_tensor(prod[:, 0, :], gates[2 * n][:], ps[:, b, :], ALU.mult).then_inc(sem["merge_dn"], 1)
                dve.wait_ge(sem["gate_mb"], n + 1)
                dve.tensor_tensor(prod[:, 1, :], gates[2 * n + 1][:], ps[:, b + 1, :], ALU.mult).then_inc(sem["merge_mb"], 1)
                dve.wait_ge(sem["merge_mb"], n + 1)
                dve.tensor_tensor(merged[:, n * T:(n + 1) * T], prod[:, 0, :], prod[:, 1, :], ALU.add).then_inc(sem["merge_done"], 1)
                if n >= 5:
                    split_merged(n - 5)
            for k in range(NK - 5, NK):
                if k > 3:
                    lo_next()
                split_merged(k)
                if k in (3, 4):
                    lo_next()
            boundary(1, 2)
            ffn_stage(1, S_FFN2)
            boundary(2, None)

        @block.tensor
        def _(pe):
            def products(out, pairs, first=True, last=True):
                n = len(pairs)
                for k, (s_hi, s_lo, m_hi, m_lo) in enumerate(pairs):
                    pe.matmul(out, s_hi, m_hi, start=first and k == 0, stop=False)
                    pe.matmul(out, s_hi, m_lo, start=False, stop=False)
                    mm = pe.matmul(out, s_lo, m_hi, start=False, stop=last and k == n - 1)
                return mm

            def kslice(slot, k):
                return w_hi[:, slot, k * P:(k + 1) * P], w_lo[:, slot, k * P:(k + 1) * P]

            def project(bank, slot):
                return products(ps[:, bank, :], [(*kslice(slot, k), hT_hi[:, k, :], hT_lo[:, k, :]) for k in range(NK)])

            def turn(st, i):
                if st == i == 0:
                    pe.wait_ge(sem["const_made"], 4)
                pe.wait_ge(sem["h_done"], st * NT + i + 1)
                for hf in range(2):
                    for k in range(4):
                        mm = pe.transpose(ps[:, ybank(i) + hf, k * P:(k + 1) * P],
                                          hnat[:, i % 2, (4 * hf + k) * P:(4 * hf + k + 1) * P], ident[:])
                    mm.then_inc(sem["h_turned"], 1)

            def opening(st, s0):
                for m in range(2):
                    cs = slice(m * 2 * P, (m + 1) * 2 * P)
                    for q in range(4):
                        s, slot, _ = slab(s0, q)
                        pe.wait_ge(sem["slab_lo"], s + 1)
                        for hf in range(2):
                            if q == 0:
                                pe.wait_ge(sem["hT_lo"], 2 * st * NT + (2 * (hf + 1) if m == 0 else 2 * NT))
                            mm = products(ps[:, q, cs], [(*kslice(slot, k), hT_hi[:, k, cs], hT_lo[:, k, cs])
                                                         for k in range(4 * hf, 4 * hf + 4)], hf == 0, hf == 1)
                        if m:
                            mm.then_inc(sem["slab_used"], 1)
                        elif q % 2 == 0:
                            turn(st, 2 + q // 2)

            def tile_product(a, a_slot, w_slot, i, first, last):
                ts = slice(i * P, (i + 1) * P)
                for hf in range(2):
                    cs = slice(hf * T, (hf + 1) * T)
                    mm = products(ps[:, ybank(i) + hf, :],
                                  [(a[0][:, a_slot, ts], a[1][:, a_slot, ts], w_hi[:, w_slot, cs], w_lo[:, w_slot, cs])],
                                  first, last)
                return mm

            def contract(a, s, w_slot, a_slot, n):
                pe.wait_ge(sem["split_lo"], n)
                pe.wait_ge(sem["slab_lo"], s + 1)
                for i in range(NT):
                    mm = tile_product(a, a_slot, w_slot, i, False, False)
                mm.then_inc(sem["slab_used"], 1)

            def contract_last(a, s0, k0, n, turn_st=None):
                for i in range(NT):
                    for q in range(RING):
                        s, slot, _ = slab(s0, k0 + q)
                        if i == 0:
                            pe.wait_ge(sem["split_lo"], n + q)
                            pe.wait_ge(sem["slab_lo"], s + 1)
                        if i == NT - 1 and q >= 2 and turn_st is not None:
                            turn(turn_st, q - 2)
                        mm = tile_product(a, (k0 + q) % RING, slot, i, False, q == RING - 1)
                        if i == NT - 1:
                            mm.then_inc(sem["slab_used"], 1)
                    if i < NT - 1:
                        mm.then_inc(sem["y_ready"], 1)

            def ffn_stage(f, s0):
                def tile(i, j):
                    for q, name in enumerate(("ffn_silu", "ffn_act")):
                        s, slot, _ = slab(s0, 2 * j + q, i)
                        pe.wait_ge(sem["slab_lo"], s + 1)
                        pe.wait_ge(sem[name], f * NF + 2 * i + j - 1)
                        project(2 * j + q, slot).then_inc(sem["slab_used"], 1)
                with pe.Fori(1, NF // 2) as i:
                    for j in range(2):
                        tile(i, j)
                s1, n, a = s0 + 2 * NF, FINS[2 * f] + 1, (a_hi, a_lo)
                s, slot, _ = slab(s1, 0)
                pe.wait_ge(sem["split_lo"], n)
                pe.wait_ge(sem["slab_lo"], s + 1)
                if f == 0:
                    pe.wait_ge(sem["convw_done"], 1)
                for i in (2, 3, 0, 1):
                    if i < 2:
                        pe.wait_ge(sem["ffn_act"], (f + 1) * NF - 1 + i)
                    mm = tile_product(a, 0, slot, i, True, False)
                mm.then_inc(sem["slab_used"], 1)
                with pe.Fori(0, (NF - 5) // 4) as i:
                    for j in range(1, 5):
                        contract(a, *slab(s1, j, i)[:2], j % RING, n + j + 4 * i)
                for k in range((NF - 5) // 4 * 4 + 1, NF - 4):
                    contract(a, *slab(s1, k)[:2], k % RING, n + k)
                contract_last(a, s1, NF - 4, n + NF - 4, 1 if f == 0 else None)

            turn(0, 0)
            turn(0, 1)
            opening(0, 0)
            pe.wait_ge(sem["const_in"], 16 * N_ROWS)
            pe.transpose(ps[:, 7, 0:48], convw_rows[:], ident[0:48, 0:48]).then_inc(sem["convw_ready"], 1)
            ffn_stage(0, 0)

            def sum_squares(j):
                if j == 0:
                    pe.wait_ge(sem["col_made"], 1)
                pe.wait_ge(sem["sq_lo_made"], j + 1)
                pe.matmul(ps[0:8, 5, :], one_col_r[:, j, :], sq_hi[:, j % 2, :], start=j == 0, stop=False)
                pe.matmul(ps[0:8, 5, :], one_col_r[:, j, :], sq_lo[:, j % 2, :], start=False, stop=j == 7).then_inc(sem["sq_summed"], 1)

            def turn_v(h):
                pe.wait_ge(sem["qkv_done"], 8 + h + 1)
                if h >= 2:
                    pe.wait_ge(sem["v_done"], h - 1)
                for t in range(NT):
                    mm = pe.transpose(ps[:, 6 + h % 2, t * P:(t + 1) * P], vT[:, h % 2, t * P:(t + 1) * P], ident[:])
                mm.then_inc(sem["vT_ready"], 1)

            def half_slab(first, f, quarter=None):
                s, slot, _ = slab(first, f // 2)
                ks = range(4 * (f % 2), 4 * (f % 2) + 4)
                if quarter is not None:
                    ks = ks[2 * quarter:2 * quarter + 2]
                if ks[0] == 0:
                    pe.wait_ge(sem["slab_lo"], s + 1)
                mm = products(ps[:, f // 2 % 2, :], [(*kslice(slot, k), hT_hi[:, k, :], hT_lo[:, k, :]) for k in ks],
                              ks[0] == 0, ks[-1] == NK - 1)
                if ks[-1] == NK - 1:
                    mm.then_inc(sem["slab_used"], 1)

            opening(1, S_QKV)
            pe.wait_ge(sem["ba_lo"], 1)
            products(ps[0:2 * H, 6, :], [(wba_hi[:, k, :], wba_lo[:, k, :], hT_hi[:, k, :], hT_lo[:, k, :])
                                         for k in range(NK)]).then_inc(sem["ba_summed"], 1)
            for j in range(4, 12):
                s, slot, _ = slab(S_QKV, j)
                pe.wait_ge(sem["slab_lo"], s + 1)
                pe.wait_ge(sem["conv_done"], j - 3)
                project(j % 4, slot).then_inc(sem["slab_used"], 1)
                if j < 10:
                    for n in {4: (0, 1), 5: (2,), 6: (3, 4)}.get(j, (j - 2,)):
                        sum_squares(n)
                if j == 5:
                    pe.wait_ge(sem["ba_kept"], 1)
                    for t in range(NT):
                        mm = pe.transpose(ps[:, 4, t * 8:(t + 1) * 8], baT[:, t * P:(t + 1) * P], ident[0:8, 0:8])
                    mm.then_inc(sem["ba_ready"], 1)
                if j == 9:
                    pe.wait_ge(sem["const_made"], N_CONST)
                    pe.wait_ge(sem["g_ready"], 1)
                    for n, m in enumerate((upper[:], same[:], half[:, 0, :], half[:, 1, :])):
                        mm = pe.matmul(ps[:, 4, 64 + n * 16:80 + n * 16], m, row(G), start=True, stop=True)
                    mm.then_inc(sem["sums_ready"], 1)
                if j >= 10:
                    turn_v(j - 10)

            POSTED = {"qk": "mbqk_done", "z": "z_done", "v": "mbvT_done"}

            def side(f):
                n = f // 2
                if f % 2 == 0:
                    if n < 2:
                        pe.wait_ge(sem["conv_done"], 9 + n)
                    else:
                        kind, j, _ = SIDE[n - 2]
                        pe.wait_ge(sem[POSTED[kind]], j + 1)
                half_slab(S_SIDE, f)
                if f in (28, 30):
                    turn_mbv(f // 2 - 14)

            def turn_mbv(j):
                pe.wait_ge(sem["mbvT_done"], j + 1)
                if j:
                    pe.wait_ge(sem["mbv_done"], j)
                else:
                    pe.wait_ge(sem["attn_done"], 2)
                for t in range(NT):
                    mm = pe.transpose(ps[:, 7, t * P:(t + 1) * P], mbvT[:, t * P:(t + 1) * P], ident[:])
                mm.then_inc(sem["mbv_turned"], 1)

            def four(out_bank, lhsT, rhs, transpose=False):
                for h in range(H):
                    hs = slice(h * HD, (h + 1) * HD)
                    if transpose:
                        mm = pe.transpose(ps[:, out_bank, hs], lhsT(h, hs), ident[:])
                    else:
                        mm = pe.matmul(ps[:, out_bank, hs], lhsT(h, hs), rhs(h, hs), start=True, stop=True)
                return mm

            def columns(bank, lhsT, rhs):
                for e in range(2 * H):
                    for r in (slice(0, C), slice(C, P)):
                        mm = pe.matmul(ps[r, bank, e * C:(e + 1) * C], lhsT(e, r), rhs(e, r), start=True, stop=True)
                return mm

            def qk_row(j):
                one = sel[:, j:j + 1].to_broadcast([8, P])
                bank = ROW_BANKS[j % 4]
                pe.matmul(ps[:, bank, :], one, iv_hi[:], start=True, stop=False)
                pe.matmul(ps[:, bank, :], one, iv_lo[:], start=False, stop=True).then_inc(sem["qk_rows"], 1)

            side(0)
            pe.wait_ge(sem["iv_split"], 2)
            pe.wait_ge(sem["sel_made"], 1)
            qk_row(0)
            pe.wait_ge(sem["conv_done"], 11)
            qk_row(1)
            side(1)
            pe.wait_ge(sem["chunk_decay"], 1)
            qk_row(2)
            pe.wait_ge(sem["conv_done"], 12)
            qk_row(3)
            turn_v(2)
            turn_v(3)
            for j in range(4, 8):
                pe.wait_ge(sem["qk_done"], j - 3)
                qk_row(j)
            for pair in range(2):
                f = 2 + 15 * pair
                tiles = [(2 * pair + q, q, slice((2 * pair + q) * P, (2 * pair + q + 1) * P)) for q in range(2)]
                side(f)
                pe.wait_ge(sem["qk_done"], 8)
                if pair:
                    pe.wait_ge(sem["wt_done"], 2)
                    pe.wait_ge(sem["u_done"], 2)
                for t, q, ts in tiles:
                    mm = four(2 + q, lambda h, hs: row(G)[:, t * H + h:t * H + h + 1].to_broadcast([P, P]), lambda h, hs: upper[:])
                mm.then_inc(sem["gb_ready"], 1)
                for t, q, ts in tiles:
                    mm = four(4 + q, lambda h, hs: qkT[:, H + h, ts], lambda h, hs: qkT[:, H + h, ts])
                mm.then_inc(sem["kk_ready"], 1)
                side(f + 1)
                pe.wait_ge(sem["v_done"], 4)
                for t, q, ts in tiles:
                    mm = four(6 + q, lambda h, hs: qkT[:, H + h, ts], lambda h, hs: qkT[:, h, ts])
                mm.then_inc(sem["qk_ready"], 1)
                side(f + 2)
                pe.wait_ge(sem["level_made"], LEVELS * pair + 1)
                columns(4, lambda e, r: cmat[r, e, r], lambda e, r: ident_c[r, :]).then_inc(sem["turned_0"], 1)
                for l in range(1, LEVELS):
                    side(f + 1 + 2 * l)
                    pe.wait_ge(sem["level_made"], LEVELS * pair + l + 1)
                    pe.wait_ge(sem["y_mat"], LEVELS * pair + l)
                    columns(4, lambda e, r: cmat[r, e, r], lambda e, r: y_c[r, e, :]).then_inc(sem["q_ready"], 1)
                    side(f + 2 + 2 * l)
                    pe.wait_ge(sem["q_copied"], 5 * pair + l)
                    if l > 1:
                        pe.wait_ge(sem["x_mat"], 4 * pair + l - 1)
                    else:
                        pe.wait_ge(sem["xc_made"], 2 * pair + 2)
                        pe.wait_ge(sem["attn_done"], pair + 1)
                    columns(5, lambda e, r: x_c[r, e, :], lambda e, r: q_c[r, e, :]).then_inc(sem["dy_ready"], 1)
                    if l < LEVELS - 1:
                        columns(6, lambda e, r: q_c[r, e, :], lambda e, r: x_c[r, e, :]).then_inc(sem["dx_ready"], 1)
                side(f + 13)
                for t, q, ts in tiles:
                    mm = four(2 + q, lambda h, hs: qkT[:, H + h, ts], None, True)
                mm.then_inc(sem["kT_ready"], 1)
                side(f + 14)
                pe.wait_ge(sem["x_blocks"], 2 * (pair + 1))
                pe.wait_ge(sem["kdec_done"], pair + 1)
                for t, q, ts in tiles:
                    four(2 + q, lambda h, hs: cmat[:, q * H + h, :], lambda h, hs: x_bd[:, q * H + h, :]).then_inc(sem["wt_ready"], 1)
                    four(4 + q, lambda h, hs: x_bd[:, q * H + h, :], lambda h, hs: v[:, t, hs]).then_inc(sem["u_ready"], 1)
            turn_mbv(2)

            def scores(m):
                h, i = divmod(m, NT)
                r = slice((h % 2) * MD, (h % 2 + 1) * MD)
                if m:
                    pe.wait_ge(sem["s_biased"], m)
                pe.matmul(ps[:, 5, 0:(i + 1) * P], mbqk[r, h // 2, i * P:(i + 1) * P],
                          mbqk[r, 4 + h // 2, 0:(i + 1) * P], start=True, stop=True).then_inc(sem["s_ready"], 1)

            def turn_p(m):
                i = m % NT
                pe.wait_ge(sem["p_done"], m + 1)
                if m:
                    pe.wait_ge(sem["pT_copied"], m)
                for j in range(i + 1):
                    mm = pe.transpose(ps[:, 7, j * P:(j + 1) * P], logit[:, m % 3, j * P:(j + 1) * P], ident[:])
                mm.then_inc(sem["pT_ready"], 1)

            def times_v(m):
                h, i = divmod(m, NT)
                pe.wait_ge(sem["pT_copied"], m + 1)
                if i == 0 and h:
                    pe.wait_ge(sem["mb_done"], h)
                for j in range(i + 1):
                    mm = pe.matmul(ps[:, 6, i * MD:(i + 1) * MD], probT[:, m % 2, j * P:(j + 1) * P],
                                   mbv[:, j, h * MD:(h + 1) * MD], start=j == 0, stop=j == i)
                if i == NT - 1:
                    mm.then_inc(sem["pv_ready"], 1)

            def units(g):
                for m in STEPS[g]:
                    if m == 0:
                        pe.wait_ge(sem["mbqk_done"], 8)
                        pe.wait_ge(sem["mbv_done"], 4)
                    if m < N_UNITS:
                        scores(m)
                    if m >= 3:
                        times_v(m - 3)
                    if 2 <= m < N_UNITS + 2:
                        turn_p(m - 2)

            for f in range(32):
                if f % 2 == 0:
                    if f < 4:
                        pe.wait_ge(sem["mbvT_done"], 3 + f // 2)
                    else:
                        pe.wait_ge(sem["gate_kept"], f // 2 - 1)
                half_slab(S_GATE, f, 0)
                if f == 0:
                    turn_mbv(3)
                units(2 * f)
                half_slab(S_GATE, f, 1)
                if f < 16:
                    c = f // 2
                    t, hf = divmod(c, 2)
                    r, ro = slice(hf * C, (hf + 1) * C), slice((1 - hf) * C, (2 - hf) * C)
                if f < 16 and f % 2 == 0:
                    pe.wait_ge(sem["wt_done"], NT)
                    pe.wait_ge(sem["u_done"], NT)
                    if c:
                        pe.wait_ge(sem["s_done"], c)
                        if c >= 2:
                            pe.wait_ge(sem["o_done"], c - 1)
                        for h in range(H):
                            hs = slice(h * HD, (h + 1) * HD)
                            mm = pe.matmul(ps[:, 2 + hf, hs], wq[:, t, h, hf * P:(hf + 1) * P], state[:, hs], start=h == 0,
                                           stop=False, skip_group_check=True)
                        mm.then_inc(sem["ws_ready"], 1)
                elif f < 16:
                    pe.wait_ge(sem["vnew_done"], c + 1)
                    if c < 2 * NT - 1:
                        for h in range(H):
                            hs = slice(h * HD, (h + 1) * HD)
                            mm = pe.matmul(ps[:, 4, hs], kdec[r, t, hs], vnew[r, hs], start=True, stop=True)
                        mm.then_inc(sem["kv_ready"], 1)
                    for h in range(H):
                        hs = slice(h * HD, (h + 1) * HD)
                        mm = pe.matmul(ps[ro, 2 + hf, hs], attnT[r, t, h * HD + hf * C:h * HD + (hf + 1) * C], vnew[r, hs],
                                       start=c == 0, stop=True, skip_group_check=True)
                    mm.then_inc(sem["o_ready"], 1)
                units(2 * f + 1)
                if f in DN_CLOSE:
                    t = DN_CLOSE[f]
                    pe.wait_ge(sem["o_scaled"], t + 1)
                    if t >= 2:
                        pe.wait_ge(sem["o_gated"], t - 1)
                    four(2 + t % 2, lambda h, hs: v[:, t, hs], None, True).then_inc(sem["oT_ready"], 1)
                for t in MB_CLOSE.get(f, ()):
                    pe.wait_ge(sem["mb_done"], MH)
                    pe.wait_ge(sem["o_gated"], NT)
                    four(2 + t, lambda h, hs: omb[:, t, hs], None, True).then_inc(sem["oT_ready"], 1)

            for n in range(NK):
                b = BRANCH_BANKS[n % 2]
                s, slot, _ = slab(S_BRANCH, n)
                pe.wait_ge(sem["slab_lo"], s + 1)
                if n == 0:
                    pe.wait_ge(sem["mb_done"], MH)
                if n == 1:
                    pe.wait_ge(sem["gate_kept"], 16)
                if n >= 2:
                    pe.wait_ge(sem["merge_mb"], n - 1)
                pe.wait_ge(sem["oT_lo"], NT)
                products(ps[:, b, :], [(*kslice(slot, k), odn_hi[:, k, :], odn_lo[:, k, :]) for k in range(4)])
                pe.wait_ge(sem["oT_lo"], 2 * NT)
                products(ps[:, b + 1, :], [(*kslice(slot, 4 + k), omb_hi[:, k, :], omb_lo[:, k, :]) for k in range(4)]).then_inc(sem["slab_used"], 1)
            for k in range(NK - RING):
                s, slot, _ = slab(S_OUT, k)
                if k:
                    contract((m_hi, m_lo), s, slot, k, FINS[1] + k + 1)
                    continue
                pe.wait_ge(sem["split_lo"], FINS[1] + 1)
                pe.wait_ge(sem["slab_lo"], s + 1)
                for i in (1, 2, 3, 0):
                    if i in (3, 0):
                        pe.wait_ge(sem["merge_mb"], NK - 1 if i else NK)
                    mm = tile_product((m_hi, m_lo), 0, slot, i, True, False)
                mm.then_inc(sem["slab_used"], 1)
            contract_last((m_hi, m_lo), S_OUT, NK - RING, FINS[1] + NK - RING + 1, 2)
            opening(2, S_FFN2)
            ffn_stage(1, S_FFN2)


N_ROWS = 5
N_CONST = 4 + 1 + 3 + 3 + 3 + 1 + 8 + 2 + 1 + 3 * LEVELS + 2


_INS = ["x", "ffn1_pre_w", "ffn1_w_gate", "ffn1_w_up", "ffn1_w_down", "ffn1_post_w", "mix_pre_w", "w_in",
        "dn_conv_w", "dn_a_log", "dn_dt_bias", "dn_norm_w", "w_branch_dn", "w_branch_mb", "w_out", "mix_post_w",
        "ffn2_pre_w", "ffn2_w_gate", "ffn2_w_up", "ffn2_w_down", "ffn2_post_w"]


def build(nc, a, out):
    hybrid_layer(nc, a["x"],
                 [(a["ffn1_w_gate"], a["ffn1_w_up"], a["ffn1_w_down"]), (a["ffn2_w_gate"], a["ffn2_w_up"], a["ffn2_w_down"])],
                 a["w_in"], a["dn_conv_w"], a["dn_a_log"], a["dn_dt_bias"], a["dn_norm_w"],
                 a["w_branch_dn"], a["w_branch_mb"], a["w_out"],
                 [(a["ffn1_pre_w"], a["ffn1_post_w"]), (a["mix_pre_w"], a["mix_post_w"]), (a["ffn2_pre_w"], a["ffn2_post_w"])],
                 out)


def kernel(**inputs):
    import numpy as _np
    import concourse.bacc as _bacc
    from concourse import mybir as _mybir
    from concourse.bass_utils import run_bass_kernel_spmd as _run

    nc = _bacc.Bacc("TRN2", target_bir_lowering=False, num_devices=1)
    arrays, args = {}, {}
    for name in _INS:
        arr = _np.ascontiguousarray(inputs[name])
        arrays[f"in_{name}_dram"] = arr
        args[name] = nc.dram_tensor(f"in_{name}_dram", arr.shape, _mybir.dt.from_np(arr.dtype), kind="ExternalInput").ap()[0]
    out = nc.dram_tensor("out_0_dram", (1, T, D), F32, kind="ExternalOutput").ap()[0]
    build(nc, args, out)
    r = _run(nc, [arrays], core_ids=[0])
    return r.results[0]["out_0_dram"]
```
